# Optimizing a Trainium2 kernel written in Bass

```python
import jax, jax.numpy as jnp
from jax import lax
import numpy as np
import math

D_MODEL = 2048
BATCH = 1
SEQ = 256
DEPTH = 1

N_MIXERS = 4
GROUP_WIDTH = D_MODEL // N_MIXERS
GDN_HEADS = 4
GDN_HEAD_DIM = GROUP_WIDTH // GDN_HEADS
MLSTM_HEADS = 4
MLSTM_HEAD_DIM = GROUP_WIDTH // MLSTM_HEADS
RGLRU_BLOCKS = 4
RGLRU_BLOCK_DIM = GROUP_WIDTH // RGLRU_BLOCKS
RGLRU_C = 8.0
RWKV_HEAD_DIM = 64
RWKV_HEADS = GROUP_WIDTH // RWKV_HEAD_DIM
RWKV_DECAY_LORA = 64
RWKV_A_LORA = 64
RWKV_GATE_LORA = 128
CONV_WIDTH = 4
CHUNK = 64
FFN_HIDDEN = -(-8 * D_MODEL // (3 * 256)) * 256
NORM_EPS = 1e-6
RWKV_LN_EPS = 64e-5

GDN_COLS = 4 * GROUP_WIDTH + 2 * GDN_HEADS
MLSTM_COLS = 4 * GROUP_WIDTH + 2 * MLSTM_HEADS
RGLRU_COLS = 2 * GROUP_WIDTH
RWKV_COLS = 3 * GROUP_WIDTH + RWKV_DECAY_LORA + RWKV_A_LORA + RWKV_GATE_LORA
IN_COLS = GDN_COLS + MLSTM_COLS + RGLRU_COLS + RWKV_COLS
MIXER_SPLITS = [GDN_COLS, GDN_COLS + MLSTM_COLS, GDN_COLS + MLSTM_COLS + RGLRU_COLS]


def rmsnorm(x, w, eps=NORM_EPS):
    xf = x.astype(jnp.float32)
    y = xf * lax.rsqrt(jnp.mean(xf * xf, axis=-1, keepdims=True) + eps)
    return (y * w.astype(jnp.float32)).astype(x.dtype)

def l2norm(x, eps=1e-6):
    xf = x.astype(jnp.float32)
    return xf * lax.rsqrt(jnp.sum(xf * xf, axis=-1, keepdims=True) + eps)

def head_layernorm(y, w, b, eps):
    mu = jnp.mean(y, axis=-1, keepdims=True)
    var = jnp.mean(jnp.square(y - mu), axis=-1, keepdims=True)
    return (y - mu) * lax.rsqrt(var + eps) * w + b

def causal_conv(x, w):
    return lax.conv_general_dilated(
        x, w[:, None, :].astype(x.dtype), window_strides=(1,), padding=[(w.shape[0] - 1, 0)],
        dimension_numbers=('NWC', 'WIO', 'NWC'), feature_group_count=x.shape[-1])

def heads(t, h):
    return t.reshape(t.shape[:-1] + (h, t.shape[-1] // h))

def to_chunks(t):
    b, T, h = t.shape[:3]
    t = t.reshape((b, T // CHUNK, CHUNK, h) + t.shape[3:])
    return jnp.transpose(t, (1, 0, 3, 2) + tuple(range(4, t.ndim)))

def from_chunks(t):
    nc, b, h, c, d = t.shape
    return jnp.transpose(t, (1, 0, 3, 2, 4)).reshape(b, nc * c, h, d)

def gated_delta_rule(q, k, v, g, beta):
    q, k, v = [to_chunks(t.astype(jnp.float32)) for t in (q, k, v)]
    g, beta = [to_chunks(t.astype(jnp.float32)) for t in (g, beta)]
    g = jnp.cumsum(g, axis=-1)
    causal = jnp.tril(jnp.ones((CHUNK, CHUNK), dtype=bool))
    decay = jnp.exp(jnp.where(causal, g[..., :, None] - g[..., None, :], -jnp.inf))
    kb = k * beta[..., None]
    lower = jnp.tril(jnp.einsum('nbhcd,nbhsd->nbhcs', kb, k) * decay, -1)
    eye = jnp.eye(CHUNK, dtype=jnp.float32)
    dv = v.shape[-1]
    rhs = jnp.concatenate([v * beta[..., None], kb * jnp.exp(g)[..., None]], axis=-1)
    sol = lax.linalg.triangular_solve(lower + eye, rhs, left_side=True, lower=True, unit_diagonal=True)
    u, w = sol[..., :dv], sol[..., dv:]
    attn = jnp.einsum('nbhcd,nbhsd->nbhcs', q, k) * decay
    q_dec = q * jnp.exp(g)[..., None]
    k_dec = k * jnp.exp(g[..., -1:] - g)[..., None]
    chunk_decay = jnp.exp(g[..., -1])

    def step(S, xs):
        u_c, w_c, attn_c, q_c, k_c, cd = xs
        v_new = u_c - jnp.einsum('bhcd,bhde->bhce', w_c, S)
        o = jnp.einsum('bhcd,bhde->bhce', q_c, S) + jnp.einsum('bhcs,bhse->bhce', attn_c, v_new)
        S = S * cd[..., None, None] + jnp.einsum('bhcd,bhce->bhde', k_c, v_new)
        return S, o

    S0 = jnp.zeros(q.shape[1:3] + (q.shape[-1], dv), jnp.float32)
    _, o = lax.scan(step, S0, (u, w, attn, q_dec, k_dec, chunk_decay))
    return from_chunks(o)

def gated_deltanet(u, conv_w, a_log, dt_bias, norm_w):
    W, H = GROUP_WIDTH, GDN_HEADS
    qkv, z, a_raw, b_raw = jnp.split(u, [3 * W, 4 * W, 4 * W + H], axis=-1)
    qkv = jax.nn.silu(causal_conv(qkv, conv_w))
    q, k, v = [heads(t, H) for t in jnp.split(qkv, 3, axis=-1)]
    q = l2norm(q) * GDN_HEAD_DIM ** -0.5
    k = l2norm(k)
    beta = jax.nn.sigmoid(b_raw.astype(jnp.float32))
    g = -jnp.exp(a_log.astype(jnp.float32)) * jax.nn.softplus(a_raw.astype(jnp.float32) + dt_bias)
    o = gated_delta_rule(q, k, v, g, beta)
    o = rmsnorm(o, norm_w) * jax.nn.silu(heads(z, H).astype(jnp.float32))
    return o.reshape(o.shape[:2] + (W,))

def mlstm_chunkwise(q, k, v, i_pre, log_f):
    q, k, v = [to_chunks(t.astype(jnp.float32)) for t in (q, k, v)]
    i_pre, log_f = [to_chunks(t) for t in (i_pre, log_f)]
    causal = jnp.tril(jnp.ones((CHUNK, CHUNK), dtype=bool))

    def step(carry, xs):
        C, n, m = carry
        q_c, k_c, v_c, i_c, f_c = xs
        b = jnp.cumsum(f_c, axis=-1)
        d = jnp.where(causal, b[..., :, None] - b[..., None, :] + i_c[..., None, :], -jnp.inf)
        inter = b + m[..., None]
        m_t = jnp.maximum(inter, jnp.max(d, axis=-1))
        s = jnp.einsum('bhtd,bhsd->bhts', q_c, k_c) * jnp.exp(d - m_t[..., None])
        a = jnp.exp(inter - m_t)
        num = a[..., None] * jnp.einsum('bhtd,bhde->bhte', q_c, C) + jnp.einsum('bhts,bhse->bhte', s, v_c)
        den = a * jnp.einsum('bhtd,bhd->bht', q_c, n) + jnp.sum(s, axis=-1)
        h = num / jnp.maximum(jnp.abs(den), jnp.exp(-m_t))[..., None]
        g = b[..., -1]
        w_log = g[..., None] - b + i_c
        m_new = jnp.maximum(g + m, jnp.max(w_log, axis=-1))
        scale_old = jnp.exp(g + m - m_new)
        w_in = jnp.exp(w_log - m_new[..., None])
        C = scale_old[..., None, None] * C + jnp.einsum('bhsd,bhse->bhde', k_c * w_in[..., None], v_c)
        n = scale_old[..., None] * n + jnp.einsum('bhsd,bhs->bhd', k_c, w_in)
        return (C, n, m_new), h

    bsz, hh, dk, dv = q.shape[1], q.shape[2], q.shape[-1], v.shape[-1]
    carry0 = (jnp.zeros((bsz, hh, dk, dv), jnp.float32), jnp.zeros((bsz, hh, dk), jnp.float32),
              jnp.zeros((bsz, hh), jnp.float32))
    _, h = lax.scan(step, carry0, (q, k, v, i_pre, log_f))
    return from_chunks(h)

def mlstm(u, conv_w, b_i, b_f, norm_w):
    W, H = GROUP_WIDTH, MLSTM_HEADS
    qk, v, o_raw, i_raw, f_raw = jnp.split(u, [2 * W, 3 * W, 4 * W, 4 * W + H], axis=-1)
    qk = jax.nn.silu(causal_conv(qk, conv_w))
    q, k = [heads(t, H) for t in jnp.split(qk, 2, axis=-1)]
    k = k * MLSTM_HEAD_DIM ** -0.5
    i_pre = i_raw.astype(jnp.float32) + b_i
    log_f = jax.nn.log_sigmoid(f_raw.astype(jnp.float32) + b_f)
    h_tilde = mlstm_chunkwise(q, k, heads(v, H), i_pre, log_f)
    h = jax.nn.sigmoid(heads(o_raw, H).astype(jnp.float32)) * h_tilde
    h = rmsnorm(h, norm_w)
    return h.reshape(h.shape[:2] + (W,))

def linear_scan_combine(left, right):
    a_l, b_l = left
    a_r, b_r = right
    return a_l * a_r, a_r * b_l + b_r

def rglru_block(u, conv_w, conv_b, w_a, b_a, w_x, b_x, lam):
    xb, gate = jnp.split(u, 2, axis=-1)
    xb = causal_conv(xb, conv_w) + conv_b
    xh = heads(xb, RGLRU_BLOCKS)
    r = jax.nn.sigmoid((jnp.einsum('btni,nij->btnj', xh, w_a).reshape(xb.shape) + b_a).astype(jnp.float32))
    i = jax.nn.sigmoid((jnp.einsum('btni,nij->btnj', xh, w_x).reshape(xb.shape) + b_x).astype(jnp.float32))
    log_a = -RGLRU_C * r * jax.nn.softplus(-lam.astype(jnp.float32))
    a = jnp.exp(log_a)
    inp = jnp.sqrt(-jnp.expm1(2.0 * log_a)) * (i * xb.astype(jnp.float32))
    _, h = lax.associative_scan(linear_scan_combine, (a, inp), axis=1)
    return h * jax.nn.gelu(gate.astype(jnp.float32))

def rwkv7_scan(r, w, k, v, kk, a):
    xs = [jnp.swapaxes(t.astype(jnp.float32), 0, 1) for t in (r, w, k, v, -kk, kk * a)]

    def step(S, inp):
        r_t, w_t, k_t, v_t, a_t, b_t = inp
        sa = jnp.einsum('bhij,bhj->bhi', S, a_t)
        S = S * w_t[:, :, None, :] + sa[..., None] * b_t[:, :, None, :] + v_t[..., None] * k_t[:, :, None, :]
        return S, jnp.einsum('bhij,bhj->bhi', S, r_t)

    S0 = jnp.zeros(r.shape[:1] + r.shape[2:] + r.shape[-1:], jnp.float32)
    _, y = lax.scan(step, S0, xs)
    return jnp.swapaxes(y, 0, 1)

def rwkv7_time_mix(u, mu, w0, w2, a0, a2, g2, k_k, k_a, r_k, ln_w, ln_b):
    W, H = GROUP_WIDTH, RWKV_HEADS
    u_prev = jnp.pad(u, ((0, 0), (1, 0), (0, 0)))[:, :-1]
    u = u + (u_prev - u) * mu
    r, k, v, w_lo, a_lo, g_lo = jnp.split(
        u, [W, 2 * W, 3 * W, 3 * W + RWKV_DECAY_LORA, 3 * W + RWKV_DECAY_LORA + RWKV_A_LORA], axis=-1)
    w_raw = -jax.nn.softplus(-(w0 + jnp.tanh(w_lo) @ w2).astype(jnp.float32)) - 0.5
    decay = jnp.exp(-jnp.exp(w_raw))
    a = jax.nn.sigmoid((a0 + a_lo @ a2).astype(jnp.float32))
    g = (jax.nn.sigmoid(g_lo) @ g2).astype(jnp.float32)
    kk = l2norm(heads(k * k_k, H))
    k = k.astype(jnp.float32) * (1.0 + (a - 1.0) * k_a)
    r, k, v, decay, a = [heads(t.astype(jnp.float32), H) for t in (r, k, v, decay, a)]
    y = rwkv7_scan(r, decay, k, v, kk, a)
    y = head_layernorm(y, ln_w, ln_b, RWKV_LN_EPS)
    y = y + jnp.sum(r * k * r_k, axis=-1, keepdims=True) * v
    return y.reshape(y.shape[:2] + (W,)) * g

def first_inputs(seed: int = 0) -> dict:
    key = jax.random.key(seed)
    ks = iter(jax.random.split(key, 48))
    L, D, W = DEPTH, D_MODEL, GROUP_WIDTH
    f32 = jnp.float32

    def normal(shape, scale):
        return jax.random.normal(next(ks), shape, f32) * scale

    def uniform(shape, lo, hi):
        return jax.random.uniform(next(ks), shape, f32, lo, hi)

    def gain(shape):
        return 1.0 + normal(shape, 0.02)

    dt = jnp.exp(uniform((L, GDN_HEADS), float(np.log(1e-3)), float(np.log(0.1))))
    a_pow = uniform((L, W), 0.9, 0.999) ** (1.0 / RGLRU_C)
    return {
        'x': normal((BATCH, SEQ, D), 1.0),
        'attn_norm': gain((L, D)),
        'w_in': normal((L, D, IN_COLS), D ** -0.5),
        'gdn_conv': normal((L, CONV_WIDTH, 3 * W), CONV_WIDTH ** -0.5),
        'gdn_a_log': jnp.log(uniform((L, GDN_HEADS), 1.0, 16.0)),
        'gdn_dt_bias': dt + jnp.log(-jnp.expm1(-dt)),
        'gdn_norm': gain((L, GDN_HEAD_DIM)),
        'mlstm_conv': normal((L, CONV_WIDTH, 2 * W), CONV_WIDTH ** -0.5),
        'mlstm_b_i': normal((L, MLSTM_HEADS), 0.1),
        'mlstm_b_f': uniform((L, MLSTM_HEADS), 3.0, 6.0),
        'mlstm_norm': gain((L, MLSTM_HEADS, MLSTM_HEAD_DIM)),
        'rglru_conv': normal((L, CONV_WIDTH, W), CONV_WIDTH ** -0.5),
        'rglru_conv_b': normal((L, W), 0.01),
        'rglru_w_a': normal((L, RGLRU_BLOCKS, RGLRU_BLOCK_DIM, RGLRU_BLOCK_DIM), RGLRU_BLOCK_DIM ** -0.5),
        'rglru_b_a': normal((L, W), 0.01),
        'rglru_w_x': normal((L, RGLRU_BLOCKS, RGLRU_BLOCK_DIM, RGLRU_BLOCK_DIM), RGLRU_BLOCK_DIM ** -0.5),
        'rglru_b_x': normal((L, W), 0.01),
        'rglru_lambda': jnp.log(a_pow) - jnp.log1p(-a_pow),
        'rwkv_mu': uniform((L, RWKV_COLS), 0.0, 1.0),
        'rwkv_w0': uniform((L, W), -6.0, 1.0),
        'rwkv_w2': normal((L, RWKV_DECAY_LORA, W), 0.1),
        'rwkv_a0': normal((L, W), 0.1),
        'rwkv_a2': normal((L, RWKV_A_LORA, W), 0.5 * RWKV_A_LORA ** -0.5),
        'rwkv_g2': normal((L, RWKV_GATE_LORA, W), RWKV_GATE_LORA ** -0.5),
        'rwkv_k_k': 0.85 + normal((L, W), 0.05),
        'rwkv_k_a': 1.0 + normal((L, W), 0.05),
        'rwkv_r_k': normal((L, RWKV_HEADS, RWKV_HEAD_DIM), 0.1),
        'rwkv_ln_w': gain((L, RWKV_HEADS, RWKV_HEAD_DIM)),
        'rwkv_ln_b': normal((L, RWKV_HEADS, RWKV_HEAD_DIM), 0.01),
        'w_out': normal((L, N_MIXERS * W, D), (N_MIXERS * W) ** -0.5),
        'ffn_norm': gain((L, D)),
        'ffn_w_gate': normal((L, D, FFN_HIDDEN), D ** -0.5),
        'ffn_w_up': normal((L, D, FFN_HIDDEN), D ** -0.5),
        'ffn_w_down': normal((L, FFN_HIDDEN, D), FFN_HIDDEN ** -0.5),
        'final_norm': gain((D,)),
    }

def first_block(x, attn_norm, w_in, gdn_conv, gdn_a_log, gdn_dt_bias, gdn_norm,
              mlstm_conv, mlstm_b_i, mlstm_b_f, mlstm_norm,
              rglru_conv, rglru_conv_b, rglru_w_a, rglru_b_a, rglru_w_x, rglru_b_x, rglru_lambda,
              rwkv_mu, rwkv_w0, rwkv_w2, rwkv_a0, rwkv_a2, rwkv_g2, rwkv_k_k, rwkv_k_a, rwkv_r_k,
              rwkv_ln_w, rwkv_ln_b, w_out, ffn_norm, ffn_w_gate, ffn_w_up, ffn_w_down, final_norm):
    for l in range(DEPTH):
        n = rmsnorm(x, attn_norm[l])
        u = n @ w_in[l]
        u_gdn, u_mlstm, u_rglru, u_rwkv = jnp.split(u, MIXER_SPLITS, axis=-1)
        y_gdn = gated_deltanet(u_gdn, gdn_conv[l], gdn_a_log[l], gdn_dt_bias[l], gdn_norm[l])
        y_mlstm = mlstm(u_mlstm, mlstm_conv[l], mlstm_b_i[l], mlstm_b_f[l], mlstm_norm[l])
        y_rglru = rglru_block(u_rglru, rglru_conv[l], rglru_conv_b[l], rglru_w_a[l], rglru_b_a[l],
                              rglru_w_x[l], rglru_b_x[l], rglru_lambda[l])
        y_rwkv = rwkv7_time_mix(u_rwkv, rwkv_mu[l], rwkv_w0[l], rwkv_w2[l], rwkv_a0[l], rwkv_a2[l],
                                rwkv_g2[l], rwkv_k_k[l], rwkv_k_a[l], rwkv_r_k[l], rwkv_ln_w[l], rwkv_ln_b[l])
        mix = jnp.concatenate([y.astype(x.dtype) for y in (y_gdn, y_mlstm, y_rglru, y_rwkv)], axis=-1)
        x = x + mix @ w_out[l]
        n = rmsnorm(x, ffn_norm[l])
        x = x + (jax.nn.silu(n @ ffn_w_gate[l]) * (n @ ffn_w_up[l])) @ ffn_w_down[l]
    return rmsnorm(x, final_norm)


_first_inputs = first_inputs


def first_inputs(seed=0):
    import zlib

    import numpy as np

    out = dict(_first_inputs(seed))
    spreads = {}
    factors = {'gdn_norm': 123.823,
     'mlstm_b_i': 64.0,
     'mlstm_norm': 75.612,
     'rglru_conv_b': 121.32,
     'rglru_b_a': 200.0,
     'rglru_b_x': 200.0,
     'rwkv_w2': 5.875,
     'rwkv_a0': 5.145,
     'rwkv_k_k': 110.765,
     'rwkv_k_a': 4.256,
     'rwkv_ln_w': 154.313,
     'rwkv_ln_b': 200.0,
     'ffn_norm': 13.182,
     'final_norm': 23.435,
     'rglru_w_a': 32.384,
     'rglru_lambda': 28.256,
     'rglru_conv': 8.0,
     'rglru_w_x': 8.0,
     'rwkv_r_k': 5.387}
    for name, (base, spread) in spreads.items():
        noise = np.random.default_rng([zlib.crc32(name.encode()), seed]).standard_normal(out[name].shape)
        drawn = base * np.exp(spread * noise) if base else spread * noise
        out[name] = __import__('jax').numpy.asarray(drawn.astype(out[name].dtype))
    for name, factor in factors.items():
        out[name] = (out[name] * factor).astype(out[name].dtype)
    return out


_narrow_inputs = first_inputs


def first_inputs(seed=0):

    out = dict(_narrow_inputs(seed))
    wider = {'gdn_norm': 4.15,
     'mlstm_norm': 4.15,
     'rwkv_k_k': 3.94,
     'rwkv_r_k': 4.15,
     'rwkv_ln_w': 4.15,
     'rwkv_ln_b': 5.95,
     'final_norm': 3.21}
    for name, times in wider.items():
        mean = out[name].mean()
        out[name] = (mean + times * (out[name] - mean)).astype(out[name].dtype)
    return out


HEAD_DIM = 64
HEADS_PER_MIXER = 8
MIX_WIDTH = N_MIXERS * HEADS_PER_MIXER * HEAD_DIM
D_FF = 4 * D_MODEL
QBLK = 128
EPS = 1e-6
NEG = -1e30
BIG = 1e30

N_BUCKETS = 32
MAX_EXACT = 16
MAX_DISTANCE = 4096
N_BIAS_HEADS = 3 * HEADS_PER_MIXER

NSA_KV_GROUPS = 2
NSA_Q_PER_GROUP = HEADS_PER_MIXER // NSA_KV_GROUPS
NSA_KV_WIDTH = NSA_KV_GROUPS * HEAD_DIM
NSA_CMP_LEN = 32
NSA_CMP_STRIDE = 16
NSA_CMP_HIDDEN = 256
NSA_SEL_LEN = 64
NSA_TOP_N = 16
NSA_WINDOW = 512

MOBA_BLOCK = 256
MOBA_TOPK = 3

LONGNET_PATTERNS = ((128, 1), (512, 4), (2048, 16))

GW = HEADS_PER_MIXER * HEAD_DIM
PROJ_SIZES = (
    GW, NSA_KV_WIDTH, NSA_KV_WIDTH, NSA_KV_WIDTH, NSA_KV_WIDTH, NSA_KV_WIDTH, NSA_KV_WIDTH, 3 * HEADS_PER_MIXER,
    GW, GW, GW,
    GW, GW, GW, HEADS_PER_MIXER,
    GW, GW, GW,
)
PROJ_WIDTH = 5920


def rmsnorm_2(x, g):
    xf = x.astype(jnp.float32)
    y = xf * lax.rsqrt(jnp.mean(xf * xf, axis=-1, keepdims=True) + EPS)
    return (y * g.astype(jnp.float32)).astype(x.dtype)

def t5_bucket(dist):
    dist = jnp.maximum(dist, 0)
    rel = jnp.log(jnp.maximum(dist, 1).astype(jnp.float32) / MAX_EXACT) / math.log(MAX_DISTANCE / MAX_EXACT)
    large = jnp.minimum(MAX_EXACT + (rel * (N_BUCKETS - MAX_EXACT)).astype(jnp.int32), N_BUCKETS - 1)
    return jnp.where(dist < MAX_EXACT, dist, large)

def masked_softmax(s, mask):
    s = jnp.where(mask, s, NEG)
    p = jax.nn.softmax(s, axis=-1)
    return jnp.where(mask, p, 0.0)

def merge_blocks(o):
    o = jnp.moveaxis(o, 0, -3)
    return o.reshape(o.shape[:-3] + (o.shape[-3] * o.shape[-2], o.shape[-1]))

def banded_attention(q, k, v, max_dist, dist_step, bias_tab):
    B, G, R, L, hd = q.shape
    nb = -(-L // QBLK)
    Lp = nb * QBLK
    nw = -(-max_dist // QBLK)
    q = jnp.pad(q, ((0, 0), (0, 0), (0, 0), (0, Lp - L), (0, 0)))
    kv_pad = ((0, 0), (0, 0), (nw * QBLK, Lp - L), (0, 0))
    kb = jnp.pad(k, kv_pad).reshape(B, G, nb + nw, QBLK, hd)
    vb = jnp.pad(v, kv_pad).reshape(B, G, nb + nw, QBLK, hd)
    blk_idx = jnp.arange(nb)[:, None] + jnp.arange(nw + 1)[None, :]
    kw = kb[:, :, blk_idx].reshape(B, G, nb, (nw + 1) * QBLK, hd)
    vw = vb[:, :, blk_idx].reshape(B, G, nb, (nw + 1) * QBLK, hd)
    qb = q.reshape(B, G, R, nb, QBLK, hd)
    s = jnp.einsum('bgrnqd,bgnkd->bgrnqk', qb, kw).astype(jnp.float32) * (hd ** -0.5)
    qpos = jnp.arange(Lp).reshape(nb, QBLK)
    kpos = (blk_idx[:, :, None] * QBLK + jnp.arange(QBLK)).reshape(nb, -1) - nw * QBLK
    dist = qpos[:, :, None] - kpos[:, None, :]
    mask = (dist >= 0) & (dist <= max_dist) & (kpos[:, None, :] >= 0)
    bias = jnp.moveaxis(bias_tab[t5_bucket(dist * dist_step)], -1, 0).reshape(G, R, nb, QBLK, -1)
    s = jnp.where(mask, s + bias, NEG)
    lse = jax.nn.logsumexp(s, axis=-1)
    p = jnp.exp(s - lse[..., None])
    o = jnp.einsum('bgrnqk,bgnkd->bgrnqd', p.astype(v.dtype), vw)
    o = o.reshape(B, G, R, Lp, hd)[:, :, :, :L]
    lse = lse.reshape(B, G, R, Lp)[..., :L]
    return o, lse

def nsa_compress(kx, pe, w1, w2):
    B, G, T, hd = kx.shape
    nc = (T - NSA_CMP_LEN) // NSA_CMP_STRIDE + 1
    idx = jnp.arange(nc)[:, None] * NSA_CMP_STRIDE + jnp.arange(NSA_CMP_LEN)[None, :]
    blk = kx[:, :, idx] + pe
    hmid = jax.nn.gelu(blk.reshape(B, G, nc, NSA_CMP_LEN * hd) @ w1)
    return hmid @ w2

def nsa_attention(q, k_cmp, v_cmp, k_slc, v_slc, k_win, v_win, gate_logits,
                  cmp_pe, phik_w1, phik_w2, phiv_w1, phiv_w2, bias_tab):
    B, G, R, T, hd = q.shape
    scale = hd ** -0.5
    kc = nsa_compress(k_cmp, cmp_pe, phik_w1, phik_w2)
    vc = nsa_compress(v_cmp, cmp_pe, phiv_w1, phiv_w2)
    nc = kc.shape[2]
    ns = T // NSA_SEL_LEN
    n_sel = min(NSA_TOP_N, ns)
    c_end = jnp.arange(nc) * NSA_CMP_STRIDE + NSA_CMP_LEN - 1
    s_start = jnp.arange(ns) * NSA_SEL_LEN
    overlap = ((c_end[:, None] - NSA_CMP_LEN + 1 < s_start[None, :] + NSA_SEL_LEN)
               & (c_end[:, None] >= s_start[None, :])).astype(jnp.float32)
    kbl = k_slc.reshape(B, G, ns, NSA_SEL_LEN, hd)
    vbl = v_slc.reshape(B, G, ns, NSA_SEL_LEN, hd)
    tab_gr = bias_tab.T.reshape(G, R, N_BUCKETS)
    b_i = jnp.arange(B)[:, None, None, None]
    g_i = jnp.arange(G)[None, :, None, None]
    g6 = jnp.arange(G)[None, :, None, None, None, None]
    r6 = jnp.arange(R)[None, None, :, None, None, None]
    blk_id = jnp.arange(ns)

    def block(i):
        t = i * QBLK + jnp.arange(QBLK)
        qb = lax.dynamic_slice_in_dim(q, i * QBLK, QBLK, axis=3)
        sc = jnp.einsum('bgrqd,bgcd->bgrqc', qb, kc).astype(jnp.float32) * scale
        dc = t[:, None] - c_end[None, :]
        sc = sc + jnp.moveaxis(bias_tab[t5_bucket(dc)], -1, 0).reshape(G, R, QBLK, nc)
        pc = masked_softmax(sc, dc >= 0)
        o_c = jnp.einsum('bgrqc,bgcd->bgrqd', pc.astype(vc.dtype), vc)
        imp = jnp.einsum('bgrqc,cn->bgqn', pc, overlap)
        cur = t // NSA_SEL_LEN
        forced = (blk_id[None, :] == 0) | (blk_id[None, :] == cur[:, None]) | (blk_id[None, :] == cur[:, None] - 1)
        valid = s_start[None, :] <= t[:, None]
        imp = jnp.where(forced, BIG, jnp.where(valid, imp, NEG))
        _, sel = lax.top_k(imp, n_sel)
        ks = kbl[b_i, g_i, sel]
        vs = vbl[b_i, g_i, sel]
        ss = jnp.einsum('bgrqd,bgqnkd->bgrqnk', qb, ks).astype(jnp.float32) * scale
        spos = sel[..., None] * NSA_SEL_LEN + jnp.arange(NSA_SEL_LEN)
        ds = t[None, None, :, None, None] - spos
        ss = ss + tab_gr[g6, r6, t5_bucket(ds)[:, :, None]]
        ss = ss.reshape(B, G, R, QBLK, n_sel * NSA_SEL_LEN)
        ps = masked_softmax(ss, (ds >= 0).reshape(B, G, 1, QBLK, n_sel * NSA_SEL_LEN))
        o_s = jnp.einsum('bgrqk,bgqkd->bgrqd', ps.astype(vs.dtype),
                         vs.reshape(B, G, QBLK, n_sel * NSA_SEL_LEN, hd))
        return o_c, o_s

    o_c, o_s = lax.map(block, jnp.arange(T // QBLK))
    o_c = merge_blocks(o_c)
    o_s = merge_blocks(o_s)
    o_w, _ = banded_attention(q, k_win, v_win, NSA_WINDOW - 1, 1, bias_tab)
    gates = jax.nn.sigmoid(gate_logits.astype(jnp.float32)).reshape(B, T, 3, G, R).transpose(2, 0, 3, 4, 1)[..., None]
    o = gates[0] * o_c + gates[1] * o_s + gates[2] * o_w
    return o.reshape(B, G * R, T, hd)

def moba_attention(q, k, v, bias_tab):
    B, H, T, hd = q.shape
    scale = hd ** -0.5
    nkb = -(-T // MOBA_BLOCK)
    pad = ((0, 0), (0, 0), (0, nkb * MOBA_BLOCK - T), (0, 0))
    kb = jnp.pad(k, pad).reshape(B, H, nkb, MOBA_BLOCK, hd)
    vb = jnp.pad(v, pad).reshape(B, H, nkb, MOBA_BLOCK, hd)
    kmean = jnp.mean(kb.astype(jnp.float32), axis=3).astype(k.dtype)
    n_top = min(MOBA_TOPK, nkb)
    tab_t = bias_tab.T
    b_i = jnp.arange(B)[:, None, None, None]
    h_i = jnp.arange(H)[None, :, None, None]
    h5 = jnp.arange(H)[None, :, None, None, None]

    def block(i):
        t = i * QBLK + jnp.arange(QBLK)
        cur = (i * QBLK) // MOBA_BLOCK
        qb = lax.dynamic_slice_in_dim(q, i * QBLK, QBLK, axis=2)
        gate = jnp.einsum('bhqd,bhnd->bhqn', qb, kmean).astype(jnp.float32)
        gate = jnp.where(jnp.arange(nkb) < cur, gate, NEG)
        _, sel = lax.top_k(gate, n_top)
        ks = kb[b_i, h_i, sel]
        vs = vb[b_i, h_i, sel]
        s_sel = jnp.einsum('bhqd,bhqnkd->bhqnk', qb, ks).astype(jnp.float32) * scale
        pos_sel = sel[..., None] * MOBA_BLOCK + jnp.arange(MOBA_BLOCK)
        s_sel = s_sel + tab_t[h5, t5_bucket(t[None, None, :, None, None] - pos_sel)]
        mask_sel = jnp.broadcast_to((sel < cur)[..., None], pos_sel.shape)
        k_own = lax.dynamic_index_in_dim(kb, cur, axis=2, keepdims=False)
        v_own = lax.dynamic_index_in_dim(vb, cur, axis=2, keepdims=False)
        d_own = t[:, None] - (cur * MOBA_BLOCK + jnp.arange(MOBA_BLOCK))[None, :]
        s_own = jnp.einsum('bhqd,bhkd->bhqk', qb, k_own).astype(jnp.float32) * scale + tab_t[:, t5_bucket(d_own)]
        n_sel_keys = n_top * MOBA_BLOCK
        s = jnp.concatenate([s_sel.reshape(B, H, QBLK, n_sel_keys), s_own], axis=-1)
        mask = jnp.concatenate([mask_sel.reshape(B, H, QBLK, n_sel_keys),
                                jnp.broadcast_to(d_own >= 0, (B, H, QBLK, MOBA_BLOCK))], axis=-1)
        p = masked_softmax(s, mask).astype(v.dtype)
        return (jnp.einsum('bhqk,bhqkd->bhqd', p[..., :n_sel_keys], vs.reshape(B, H, QBLK, n_sel_keys, hd))
                + jnp.einsum('bhqk,bhkd->bhqd', p[..., n_sel_keys:], v_own))

    return merge_blocks(lax.map(block, jnp.arange(T // QBLK)))

def fox_attention(q, k, v, log_f):
    B, H, T, hd = q.shape
    scale = hd ** -0.5
    c = jnp.cumsum(log_f, axis=-1)
    kpos = jnp.arange(T)

    def block(i):
        t = i * QBLK + jnp.arange(QBLK)
        qb = lax.dynamic_slice_in_dim(q, i * QBLK, QBLK, axis=2)
        cq = lax.dynamic_slice_in_dim(c, i * QBLK, QBLK, axis=2)
        s = jnp.einsum('bhqd,bhkd->bhqk', qb, k).astype(jnp.float32) * scale + (cq[..., None] - c[:, :, None, :])
        p = masked_softmax(s, kpos[None, :] <= t[:, None])
        return jnp.einsum('bhqk,bhkd->bhqd', p.astype(v.dtype), v)

    return merge_blocks(lax.map(block, jnp.arange(T // QBLK)))

def dilated_attention(q, k, v, bias_tab):
    B, H, T, hd = q.shape
    outs, lses = [], []
    for window, dil in LONGNET_PATTERNS:
        L = T // dil

        def fold(z):
            return z.reshape(B, H, L, dil, hd).transpose(0, 3, 1, 2, 4).reshape(B * dil, H, L, hd)

        o, lse = banded_attention(fold(q)[:, :, None], fold(k), fold(v), window // dil, dil, bias_tab)
        outs.append(o[:, :, 0].reshape(B, dil, H, L, hd).transpose(0, 2, 3, 1, 4).reshape(B, H, T, hd))
        lses.append(lse[:, :, 0].reshape(B, dil, H, L).transpose(0, 2, 3, 1).reshape(B, H, T))
    w = jax.nn.softmax(jnp.stack(lses, axis=0), axis=0)
    out = w[0][..., None] * outs[0] + w[1][..., None] * outs[1] + w[2][..., None] * outs[2]
    return out.astype(q.dtype)

def hybrid_mixer(h, w_in, w_out, cmp_pe, phik_w1, phik_w2, phiv_w1, phiv_w2, fox_bias, rel_bias):
    B, T, _ = h.shape
    proj = h @ w_in
    splits = [int(s) for s in np.cumsum(PROJ_SIZES)[:-1]]
    (qa, kca, vca, ksa, vsa, kwa, vwa, ga,
     qb, kb, vb,
     qc, kc, vc, fc,
     qd, kd, vd) = jnp.split(proj, splits, axis=-1)

    def heads(z):
        n = z.shape[-1] // HEAD_DIM
        return z.reshape(B, T, n, HEAD_DIM).transpose(0, 2, 1, 3)

    hm = HEADS_PER_MIXER
    qa_g = heads(qa).reshape(B, NSA_KV_GROUPS, NSA_Q_PER_GROUP, T, HEAD_DIM)
    o_a = nsa_attention(qa_g, heads(kca), heads(vca), heads(ksa), heads(vsa), heads(kwa), heads(vwa), ga,
                        cmp_pe, phik_w1, phik_w2, phiv_w1, phiv_w2, rel_bias[:, 0:hm])
    o_b = moba_attention(heads(qb), heads(kb), heads(vb), rel_bias[:, hm:2 * hm])
    log_f = jax.nn.log_sigmoid((fc + fox_bias).astype(jnp.float32)).transpose(0, 2, 1)
    o_c = fox_attention(heads(qc), heads(kc), heads(vc), log_f)
    o_d = dilated_attention(heads(qd), heads(kd), heads(vd), rel_bias[:, 2 * hm:3 * hm])
    o = jnp.concatenate([o_a.astype(h.dtype), o_b.astype(h.dtype), o_c.astype(h.dtype), o_d.astype(h.dtype)], axis=1)
    o = o.transpose(0, 2, 1, 3).reshape(B, T, MIX_WIDTH)
    return o @ w_out

def second_inputs(seed: int = 0) -> dict:
    key = jax.random.key(seed)
    ks = jax.random.split(key, 17)

    def nrm(k, shape, fan):
        return jax.random.normal(k, shape, jnp.float32) * fan ** -0.5

    def gain(k):
        return 1.0 + 0.05 * jax.random.normal(k, (DEPTH, D_MODEL), jnp.float32)

    cmp_in = NSA_CMP_LEN * HEAD_DIM
    return {
        "x": jax.random.normal(ks[0], (BATCH, SEQ, D_MODEL), jnp.float32),
        "w_in": nrm(ks[1], (DEPTH, D_MODEL, PROJ_WIDTH), D_MODEL),
        "w_out": nrm(ks[2], (DEPTH, MIX_WIDTH, D_MODEL), MIX_WIDTH),
        "g_mix_pre": gain(ks[3]),
        "g_mix_post": gain(ks[4]),
        "g_mlp_pre": gain(ks[5]),
        "g_mlp_post": gain(ks[6]),
        "w_up": nrm(ks[7], (DEPTH, D_MODEL, D_FF), D_MODEL),
        "w_down": nrm(ks[8], (DEPTH, D_FF, D_MODEL), D_FF),
        "cmp_pe": 0.1 * jax.random.normal(ks[9], (DEPTH, NSA_CMP_LEN, HEAD_DIM), jnp.float32),
        "phik_w1": nrm(ks[10], (DEPTH, cmp_in, NSA_CMP_HIDDEN), cmp_in),
        "phik_w2": nrm(ks[11], (DEPTH, NSA_CMP_HIDDEN, HEAD_DIM), NSA_CMP_HIDDEN),
        "phiv_w1": nrm(ks[12], (DEPTH, cmp_in, NSA_CMP_HIDDEN), cmp_in),
        "phiv_w2": nrm(ks[13], (DEPTH, NSA_CMP_HIDDEN, HEAD_DIM), NSA_CMP_HIDDEN),
        "fox_bias": 4.0 + 0.5 * jax.random.normal(ks[14], (DEPTH, HEADS_PER_MIXER), jnp.float32),
        "rel_bias": 0.5 * jax.random.normal(ks[15], (N_BUCKETS, N_BIAS_HEADS), jnp.float32),
    }

def second_block(x, w_in, w_out, g_mix_pre, g_mix_post, g_mlp_pre, g_mlp_post, w_up, w_down,
              cmp_pe, phik_w1, phik_w2, phiv_w1, phiv_w2, fox_bias, rel_bias):
    for l in range(DEPTH):
        h = rmsnorm_2(x, g_mix_pre[l])
        mix = hybrid_mixer(h, w_in[l], w_out[l], cmp_pe[l], phik_w1[l], phik_w2[l],
                           phiv_w1[l], phiv_w2[l], fox_bias[l], rel_bias)
        x = x + rmsnorm_2(mix, g_mix_post[l])
        h2 = rmsnorm_2(x, g_mlp_pre[l])
        y = jnp.square(jax.nn.relu(h2 @ w_up[l])) @ w_down[l]
        x = x + rmsnorm_2(y, g_mlp_post[l])
    return x


def setup_inputs(seed=0):
    out = dict(first_inputs(seed))
    for name, value in second_inputs(seed + 1).items():
        if name != "x":
            out[name + "_2"] = value
    return out


def reference(
    x, attn_norm, w_in, gdn_conv, gdn_a_log, gdn_dt_bias, gdn_norm, mlstm_conv, mlstm_b_i,
    mlstm_b_f, mlstm_norm, rglru_conv, rglru_conv_b, rglru_w_a, rglru_b_a, rglru_w_x, rglru_b_x,
    rglru_lambda, rwkv_mu, rwkv_w0, rwkv_w2, rwkv_a0, rwkv_a2, rwkv_g2, rwkv_k_k, rwkv_k_a,
    rwkv_r_k, rwkv_ln_w, rwkv_ln_b, w_out, ffn_norm, ffn_w_gate, ffn_w_up, ffn_w_down,
    final_norm, w_in_2, w_out_2, g_mix_pre_2, g_mix_post_2, g_mlp_pre_2, g_mlp_post_2, w_up_2,
    w_down_2, cmp_pe_2, phik_w1_2, phik_w2_2, phiv_w1_2, phiv_w2_2, fox_bias_2, rel_bias_2,
):
    x = first_block(
        x, attn_norm, w_in, gdn_conv, gdn_a_log, gdn_dt_bias, gdn_norm, mlstm_conv, mlstm_b_i,
        mlstm_b_f, mlstm_norm, rglru_conv, rglru_conv_b, rglru_w_a, rglru_b_a, rglru_w_x,
        rglru_b_x, rglru_lambda, rwkv_mu, rwkv_w0, rwkv_w2, rwkv_a0, rwkv_a2, rwkv_g2, rwkv_k_k,
        rwkv_k_a, rwkv_r_k, rwkv_ln_w, rwkv_ln_b, w_out, ffn_norm, ffn_w_gate, ffn_w_up,
        ffn_w_down, final_norm,
    )
    return second_block(
        x, w_in_2, w_out_2, g_mix_pre_2, g_mix_post_2, g_mlp_pre_2, g_mlp_post_2, w_up_2,
        w_down_2, cmp_pe_2, phik_w1_2, phik_w2_2, phiv_w1_2, phiv_w2_2, fox_bias_2, rel_bias_2,
    )


_drawn_inputs = setup_inputs


def setup_inputs(seed=0):
    import zlib

    import numpy as np

    out = dict(_drawn_inputs(seed))
    spreads = {}
    factors = {'g_mix_pre_2': 8.0,
     'g_mix_post_2': 27.426,
     'g_mlp_pre_2': 26.024,
     'g_mlp_post_2': 29.358,
     'cmp_pe_2': 8.0,
     'phik_w1_2': 8.0,
     'phik_w2_2': 8.0,
     'phiv_w1_2': 4.636,
     'phiv_w2_2': 3.284,
     'fox_bias_2': 64.0,
     'rel_bias_2': 6.333}
    for name, (base, spread) in spreads.items():
        noise = np.random.default_rng([zlib.crc32(name.encode()), seed]).standard_normal(out[name].shape)
        drawn = base * np.exp(spread * noise) if base else spread * noise
        out[name] = __import__('jax').numpy.asarray(drawn.astype(out[name].dtype))
    for name, factor in factors.items():
        out[name] = (out[name] * factor).astype(out[name].dtype)
    return out
```

```python
from contextlib import ExitStack

import numpy as np

import concourse.bass as bass
from concourse import mybir

F32 = mybir.dt.float32
ALU = mybir.AluOpType
ACT = mybir.ActivationFunctionType
AX = mybir.AxisListType

P = 128
T = 256
TT = T // P
D = 2048
KD = D // P
W = 512
F1 = 5632
F2 = 8192
EPS = 1e-6
SLOTS = 4
NEG = -1e30
HUGE8 = -8e30

GROUPS1 = ((0, 8), (2056, 8), (4112, 4), (5136, 7))
GATES1 = (2048, 4104)
GQ, GK, GV, GZ = 0, 4, 8, 12
MQ, MK, MV, MO = 16, 20, 24, 28
RX, RG = 32, 36
WR, WK, WV, WWA, WG = 40, 44, 48, 52, 53
GROUPS2 = ((0, 5), (1304, 6), (2840, 6), (4384, 6))
NSA_GATES, FOX_GATES = 1280, 4376
AQ, AKC, AVC, AKS, AVS, AKW, AVW = 0, 4, 5, 6, 7, 8, 9
BQ, BK, BV = 10, 14, 18
CQ, CK, CV_ = 22, 26, 30
DQ, DK, DV = 34, 38, 42

TABLE0 = (("attn_norm", 16), ("ffn_norm", 16), ("g_mix_pre_2", 16), ("g_mlp_pre_2", 16), ("cmp_pe_2", 16))
TABLE1 = (("gdn_conv", 48), ("mlstm_conv", 32), ("rglru_conv", 16))
TABLE2 = (("rglru_conv_b", 4), ("rglru_b_a", 4), ("rglru_b_x", 4), ("rglru_lambda", 4), ("rwkv_mu", 14),
          ("rwkv_w0", 4), ("rwkv_a0", 4), ("rwkv_k_k", 4), ("rwkv_k_a", 4), ("rwkv_r_k", 4),
          ("rwkv_ln_w", 4), ("rwkv_ln_b", 4), ("gdn_norm", 1), ("mlstm_norm", 4))
TABLES = (TABLE0, TABLE1, TABLE2)


def column_of():
    at, out = 0, {}
    for table in TABLES:
        for name, n in table:
            out[name] = at
            at += n
    return out, at


COL, NCOL = column_of()


def bucket(d):
    edges = (16, 23, 32, 46, 64, 91, 128, 182)
    return d if d < 16 else 15 + sum(d >= e for e in edges)


def constants():
    i = np.arange(P)
    row, col = i[:, None], i[None, :]
    out = {
        "ident": np.eye(P),
        "ones": np.ones((P, T)),
        "ones64": (row // 64 == col // 64) * 1.0,
        "causal_T": np.where(row <= col, 0.0, NEG),
        "strict_T": (row < col) * 1.0,
        "strict64_T": (row < col) * (row // 64 == col // 64) * 1.0,
        "incl64_T": (row <= col) * (row // 64 == col // 64) * 1.0,
        "causal8": np.where(col <= row, 0.0, HUGE8),
    }
    for b in (1, 2, 4, 8, 16, 32, 64):
        out[f"level{b}"] = ((col // b) % 2 == 1) * (row // b == col // b - 1) * 1.0
    out["from31"] = (row >= 31) * 1.0
    out["sel"] = np.zeros((P, 8, P))
    for h in range(8):
        out["sel"][h, h] = 1.0
    t = np.arange(T)
    out["reset64"] = np.broadcast_to((t % 64 != 0) * 1.0, (P, T))
    out["reset128"] = np.broadcast_to((t % 128 != 0) * 1.0, (P, T))
    dist = 255 - np.arange(384)
    hot = np.zeros((P, 384))
    extra = np.zeros((P, 384))
    for n, d in enumerate(dist):
        hot[bucket(max(d, 0)), n] = 8.0
        count = int(d <= 128) + int(d % 4 == 0) + int(d % 16 == 0)
        extra[:16, n] = 0.0 if d >= 0 else HUGE8
        extra[16:24, n] = 8 * np.log(count) if d >= 0 and count else HUGE8
    out["hot8"] = hot
    out["extra8"] = extra
    flat = {k: v.reshape(P, -1).astype(np.float32) for k, v in out.items()}
    where, at = {}, 0
    for k, v in flat.items():
        where[k] = (at, v.shape[1])
        at += v.shape[1]
    return np.ascontiguousarray(np.concatenate(list(flat.values()), axis=1)), where


CONST, CONST_AT = constants()
NCONST = CONST.shape[1]


class Marks:

    def __init__(self, sem, order):
        self.sem, self.order, self.n = sem, list(order), 0
        assert len(set(self.order)) == len(self.order)

    def did(self, name, ins):
        assert self.order[self.n] == name, (self.order[self.n], name)
        self.n += 1
        ins.then_inc(self.sem, 1)

    def wait(self, eng, name):
        eng.wait_ge(self.sem, self.order.index(name) + 1)


def build(nc, A, out, stop=99):
    ctx = ExitStack()

    def sb(name, shape):
        return ctx.enter_context(nc.sbuf_tensor(name, shape, F32))

    def sem(name):
        return ctx.enter_context(nc.semaphore(name))

    X = sb("X", [P, TT, D])
    NT = sb("NT", [P, KD, T])
    RING = sb("RING", [P, SLOTS, 4096])
    BIG = sb("BIG", [P, 64, T])
    TMP = sb("TMP", [P, TT, D])
    CST = sb("CST", [P, NCONST])
    PAR = sb("PAR", [P, NCOL])
    ST = sb("ST", [P, 16])
    GT = sb("GT", [32, 4, T])
    HC = sb("HC", [8, 8])
    PS = ctx.enter_context(nc.psum_tensor("PS", [P, 8, 512], F32))

    bias_rows = nc.dram_tensor("bias_rows", (24, 384), F32).ap()
    bias_skew = nc.dram_tensor("bias_skew", (24, P, 384), F32).ap()

    def cst(name, parts=P):
        at, n = CONST_AT[name]
        return CST[0:parts, at:at + n]

    IDENT, UNIT, ONES64 = cst("ident"), cst("ones"), cst("ones64")
    ONES = UNIT[:, 0:P]
    SEL = cst("sel", 8).rearrange("p (h m) -> p h m", h=8)

    def par(name, i=0, n=1):
        return PAR[:, COL[name] + i:COL[name] + i + n]

    def spread(columns, n):
        return columns.rearrange("p (k o) -> p k o", o=1).broadcast_to([P, columns.shape[1], n])

    def repeated(block, k):
        return block.rearrange("p (o n) -> p o n", o=1).broadcast_to([P, k, block.shape[1]])

    slot_full = [sem(f"slot_full{i}") for i in range(SLOTS)]
    item_used = sem("item_used")
    pair_out = sem("pair_out")
    sq_done = sem("sq_done")
    mean_done = sem("mean_done")
    sd_done = sem("sd_done")
    rs_done = sem("rs_done")
    xn_done = sem("xn_done")
    turned = sem("turned")
    norm_out = sem("norm_out")

    def ring_cols(slot):
        return RING[:, slot, :].rearrange("p (k n) -> p k n", k=KD)

    def ring_rows(slot):
        return RING[:, slot, :].rearrange("p (k n) -> p k n", k=2)

    def stream_loop(eng, n0, count, body):
        rounds = count // SLOTS
        if rounds > 1:
            with eng.Fori(0, rounds) as r:
                for j in range(SLOTS):
                    body((n0 + j) % SLOTS, n0 + j, r, j, True)
        else:
            rounds = 0
        for j in range(rounds * SLOTS, count):
            body((n0 + j) % SLOTS, n0 + j, 0, j, False)

    def load_item(sp, src_of, slot, first, r, j, dst, fresh):
        if first >= SLOTS:
            sp.wait_ge(item_used, first + SLOTS * r - SLOTS + 1)
        elif not fresh:
            raise AssertionError("a loop over the first items")
        sp.dma_start(dst, src_of(j + SLOTS * r)).then_inc(slot_full[slot], 16)

    def load_cols(sp, n0, groups):
        for w, c0, count in groups:
            wv = w.rearrange("(k p) n -> p k n", p=P)
            src = lambda i: wv[:, :, bass.ds(c0 + i * 256, 256)]
            if n0 < SLOTS:
                for j in range(SLOTS):
                    load_item(sp, src, (n0 + j) % SLOTS, n0 + j, 0, j, ring_cols((n0 + j) % SLOTS), True)
                src0 = src
                src = lambda i: src0(i + SLOTS)
                n0, count = n0 + SLOTS, count - SLOTS
            stream_loop(sp, n0, count, lambda slot, first, r, j, loop:
                        load_item(sp, src, slot, first, r, j, ring_cols(slot), False))
            n0 += count
        return n0

    def load_interleaved(sp, n0, wa, wb, pairs):
        views = [w.rearrange("(k p) n -> p k n", p=P) for w in (wa, wb)]
        rounds = 2 * pairs // SLOTS
        with sp.Fori(0, rounds) as r:
            for j in range(SLOTS):
                slot = (n0 + j) % SLOTS
                sp.wait_ge(item_used, n0 + j + SLOTS * r - SLOTS + 1)
                sp.dma_start(ring_cols(slot), views[j % 2][:, :, bass.ds((r * 2 + j // 2) * 256, 256)])\
                    .then_inc(slot_full[slot], 16)
        assert rounds * SLOTS == 2 * pairs
        return n0 + 2 * pairs

    def load_rows(sp, n0, w):
        wv = w.rearrange("(g k p) n -> g p k n", p=P, k=2)
        count = w.shape[0] // 256
        stream_loop(sp, n0, count, lambda slot, first, r, j, loop:
                    load_item(sp, lambda i: wv[bass.ds(i, 1)].rearrange("o p k n -> (o p) k n"),
                              slot, first, r, j, ring_rows(slot), False))
        return n0 + count

    def pe_cols(pe, n0, q0, count):
        def body(slot, first, r, j, loop):
            item, pair = first + SLOTS * r, q0 + j + SLOTS * r
            pe.wait_ge(slot_full[slot], 16 * (first // SLOTS + 1) + 16 * r)
            if q0 + j >= 4:
                pe.wait_ge(pair_out, pair - 3)
            bank = (q0 + j) % 4
            for c in range(2):
                for k in range(KD):
                    mm = nc.tensor.matmul(PS[:, bank, c * T:(c + 1) * T],
                                          ring_cols(slot)[:, k, c * P:(c + 1) * P], NT[:, k, :],
                                          start=(k == 0), stop=(k == KD - 1))
            mm.then_inc(item_used, 1)
        if q0 < 4:
            for j in range(4):
                body((n0 + j) % SLOTS, n0 + j, 0, j, False)
            n0, q0, count = n0 + 4, q0 + 4, count - 4
        stream_loop(pe, n0, count, body)

    def evacuate(act, n0, q0, count, tile0):
        def body(slot, first, r, j, loop):
            act.wait_ge(item_used, first + SLOTS * r + 1)
            act.activation(BIG[:, bass.ds(tile0 + 2 * j + 2 * SLOTS * r, 2), :],
                           PS[:, (q0 + j) % 4, :].rearrange("p (c t) -> p c t", c=2), ACT.Copy)\
                .then_inc(pair_out, 1)
        stream_loop(act, n0, count, body)

    def pe_rows(pe, n0, count, lhs):
        def one(slot, first, r, k0, start, stop):
            pe.wait_ge(slot_full[slot], 16 * (first // SLOTS + 1) + 16 * r)
            for kk in range(2):
                for t in range(TT):
                    for c in range(4):
                        mm = nc.tensor.matmul(PS[:, 4 * t + c, :], lhs[:, k0 + kk, t * P:(t + 1) * P],
                                              ring_rows(slot)[:, kk, c * 512:(c + 1) * 512],
                                              start=(start and kk == 0), stop=(stop and kk == 1))
            mm.then_inc(item_used, 1)
        for j in range(count):
            one((n0 + j) % SLOTS, n0 + j, 0, 2 * j, j == 0, j == count - 1)

    def norm_act(act, q, ready):
        for t in range(TT):
            ready(act, t)
            act.activation(TMP[:, t, :], X[:, t, :], ACT.Square, accum_out=ST[:, t:t + 1]).then_inc(sq_done, 1)
        act.wait_ge(mean_done, q + 1)
        act.activation(ST[:, 4:6], ST[:, 2:4], ACT.Sqrt).then_inc(sd_done, 1)

    def norm_dve(dve, q, gain):
        dve.wait_ge(sq_done, 2 * q + 2)
        dve.tensor_scalar(ST[:, 2:4], ST[:, 0:2], 1.0 / D, EPS, ALU.mult, ALU.add).then_inc(mean_done, 1)
        dve.wait_ge(sd_done, q + 1)
        dve.reciprocal(ST[:, 6:8], ST[:, 4:6]).then_inc(rs_done, 1)
        dve.wait_ge(rs_done, q + 1)
        if gain is None:
            return
        for t in range(TT):
            dve.tensor_scalar(TMP[:, t, :], X[:, t, :], ST[:, 6 + t:7 + t], None, ALU.mult).then_inc(xn_done, 1)
        n = q_turn[q]
        for i in range(8):
            t, b = i // 4, i % 4
            dve.wait_ge(turned, 8 * n + i + 1)
            dve.tensor_tensor(NT[:, 4 * b:4 * b + 4, t * P:(t + 1) * P],
                              PS[:, i, :].rearrange("p (k t) -> p k t", k=4),
                              spread(par(gain, 4 * b, 4), P), ALU.mult).then_inc(norm_out, 1)

    def norm_pe(pe, q):
        n = q_turn[q]
        for i in range(8):
            t, b = i // 4, i % 4
            if b == 0:
                pe.wait_ge(xn_done, 2 * n + t + 1)
            for k in range(4):
                mm = nc.tensor.transpose(PS[:, i, k * P:(k + 1) * P],
                                         TMP[:, t, (4 * b + k) * P:(4 * b + k + 1) * P], IDENT)
            mm.then_inc(turned, 1)

    q_turn = {0: 0, 1: 1, 3: 2, 5: 3}

    in_loaded = sem("in_loaded")
    par_loaded = sem("par_loaded")
    par_turned = sem("par_turned")
    par_out = sem("par_out")
    bias_made = sem("bias_made")
    bias_out = sem("bias_out")
    bias_moved = sem("bias_moved")
    gate_loaded = sem("gate_loaded")
    gates_made = sem("gates_made")
    gates_out = sem("gates_out")

    w_in = A["w_in"][0]
    PROWS = [TMP[:, 0, 0:P], TMP[:, 0, P:2 * P], TMP[:, 0, 2 * P:3 * P]]
    BIASR = TMP[0:24, 0, 1024:1024 + 384]
    RB = TMP[0:32, 0, 512:512 + 24]
    WGATE = BIG[:, 56:58, :].rearrange("p a t -> p (a t)")[:, 0:256].rearrange("p (k n) -> p k n", k=KD)

    with nc.Block() as block:
        @block.sync
        def _(sp):
            sp.dma_start(CST[:, :], A["const"]).then_inc(in_loaded, 16)
            sp.dma_start(X[:, :, :], A["x"][0].rearrange("(t p) d -> p t d", p=P)).then_inc(in_loaded, 16)
            for n, c in enumerate(GATES1):
                sp.dma_start(WGATE[:, :, 8 * n:8 * n + 8],
                             w_in[:, c:c + 8].rearrange("(k p) n -> p k n", p=P)).then_inc(gate_loaded, 16)
            load_cols(sp, 0, [(w_in, c, n) for c, n in GROUPS1])

        @block.scalar
        def _(act):
            for b, table in enumerate(TABLES):
                at = 0
                for name, n in table:
                    src = A[name]
                    flat = src.rearrange(" ".join("abcd"[:len(src.shape)]) + " -> ("
                                         + " ".join("abcd"[:len(src.shape)]) + ")")
                    act.dma_start(PROWS[b][at:at + n, :], flat.rearrange("(r c) -> r c", c=P))\
                        .then_inc(par_loaded, 16)
                    at += n
            act.dma_start(RB, A["rel_bias_2"]).then_inc(par_loaded, 16)
            for n, name in enumerate(("gdn_a_log", "gdn_dt_bias", "mlstm_b_i", "mlstm_b_f")):
                act.dma_start(HC[0:4, n:n + 1], A[name][0].rearrange("(h o) -> h o", o=1)).then_inc(par_loaded, 16)
            act.dma_start(HC[0:8, 4:5], A["fox_bias_2"][0].rearrange("(h o) -> h o", o=1)).then_inc(par_loaded, 16)
            act.wait_ge(bias_out, 1)
            act.dma_start(bias_rows, BIASR).then_inc(bias_moved, 16)
            act.wait_ge(bias_moved, 16)
            act.dma_start(bias_skew, bias_rows.rearrange("h (o i) -> h o i", o=1).broadcast_to([24, P, 384]))\
                .then_inc(bias_moved, 16)
            act.wait_ge(par_out, 3)
            norm_act(act, 0, lambda e, t: e.wait_ge(in_loaded, 32))
            at, n = 0, 0
            for _, pairs in GROUPS1:
                evacuate(act, n, n, pairs, at)
                n, at = n + pairs, at + 2 * pairs
            act.wait_ge(gates_made, 1)
            act.activation(GT[0:4, :, :], PS[0:4, 6:8, :].rearrange("p b (c t) -> p (b c) t", c=2), ACT.Copy)\
                .then_inc(gates_out, 1)
            act.wait_ge(bias_moved, 32)

        @block.vector
        def _(dve):
            at = 0
            for b, table in enumerate(TABLES):
                n = sum(k for _, k in table)
                dve.wait_ge(par_turned, b + 1)
                dve.tensor_copy(PAR[:, at:at + n], PS[:, 4 + b, 0:n]).then_inc(par_out, 1)
                at += n
            dve.wait_ge(bias_made, 1)
            dve.tensor_tensor(BIASR, PS[0:24, 7, 0:384], cst("extra8", 24), ALU.add).then_inc(bias_out, 1)
            dve.wait_ge(bias_moved, 16)
            dve.wait_ge(par_out, 3)
            norm_dve(dve, 0, "attn_norm")

        @block.tensor
        def _(pe):
            pe.wait_ge(in_loaded, 32)
            pe.wait_ge(par_loaded, 16 * (sum(len(t) for t in TABLES) + 6))
            for b, table in enumerate(TABLES):
                n = sum(k for _, k in table)
                nc.tensor.transpose(PS[:, 4 + b, 0:n], PROWS[b][0:n, :], IDENT[0:n, 0:n]).then_inc(par_turned, 1)
            nc.tensor.matmul(PS[0:24, 7, 0:384], RB, cst("hot8", 32), start=True, stop=True).then_inc(bias_made, 1)
            pe.wait_ge(par_out, 3)
            pe.wait_ge(bias_out, 1)
            norm_pe(pe, 0)
            pe.wait_ge(norm_out, 8)
            n = 0
            for _, pairs in GROUPS1:
                pe_cols(pe, n, n, pairs)
                n += pairs
            pe.wait_ge(gate_loaded, 32)
            for g in range(4):
                for k in range(KD):
                    mm = nc.tensor.matmul(PS[0:4, 6 + g // 2, (g % 2) * T:(g % 2 + 1) * T],
                                          WGATE[:, k, 4 * g:4 * g + 4], NT[:, k, :],
                                          start=(k == 0), stop=(k == KD - 1))
            mm.then_inc(gates_made, 1)
    if stop == 0:
        return ctx

    R_ = RING[:, :, :].rearrange("p s n -> p (s n)")
    T_ = TMP[:, :, :].rearrange("p t n -> p (t n)")

    def area(base, at, k, n=P):
        return base[:, at:at + k * n].rearrange("p (k n) -> p k n", k=k)

    CV = area(R_, 0, 24, T)
    CONVS = ([("gdn_conv", 12, j, GQ + j) for j in range(12)] + [("mlstm_conv", 8, j, MQ + j) for j in range(8)]
             + [("rglru_conv", 4, j, RX + j) for j in range(4)])
    SPARE = BIG[:, 54:64, :]
    ROW = lambda n: SPARE[0:4, n, :]
    O8 = BIG[:, 16:24, :]

    conv_lead = sem("conv_lead")
    conv_tap = sem("conv_tap")
    conv_silu = sem("conv_silu")
    NCV = len(CONVS)
    with nc.Block() as block:
        @block.scalar
        def _(act):
            for i, (name, n, j, u) in enumerate(CONVS):
                w = par(name, 3 * n + j)
                if name == "rglru_conv":
                    act.activation(CV[:, i, :], BIG[:, u, :], ACT.Identity, bias=par("rglru_conv_b", j), scale=w)\
                        .then_inc(conv_lead, 1)
                else:
                    act.activation(CV[:, i, :], BIG[:, u, :], ACT.Copy, scale=w).then_inc(conv_lead, 1)
            for g in range(5):
                act.wait_ge(conv_tap, 2 * NCV + 4 * g + 4)
                act.activation(CV[:, 4 * g:4 * g + 4, :], CV[:, 4 * g:4 * g + 4, :], ACT.Silu).then_inc(conv_silu, 1)

        @block.vector
        def _(dve):
            for step, tap in enumerate((2, 1, 0)):
                for i, (name, n, j, u) in enumerate(CONVS):
                    s = 3 - tap
                    if step == 0:
                        dve.wait_ge(conv_lead, i + 1)
                    else:
                        dve.wait_ge(conv_tap, (step - 1) * NCV + i + 1)
                    dve.scalar_tensor_tensor(out=CV[:, i, s:T], in0=BIG[:, u, 0:T - s], scalar=par(name, tap * n + j),
                                             in1=CV[:, i, s:T], op0=ALU.mult, op1=ALU.add).then_inc(conv_tap, 1)

    def marks(name, order):
        return Marks(sem(name), order)

    def m3(at, k=8):
        return area(R_, 6144 + at * 1024, k)
    EGB, DT_, AT_, LT_, QD, KDT, XI, XT, CT, CX = [m3(i) for i in range(10)]
    EGB, QD, KDT = [v.rearrange("p m t -> p (m t)").rearrange("p (h t) -> p h t", h=4) for v in (EGB, QD, KDT)]
    fl = lambda v: v.rearrange("p a b -> p (a b)")
    VB, KN, VNEW = [fl(BIG[:, 4 * i:4 * i + 4, :]).rearrange("p (m t) -> p m t", m=8) for i in range(3)]
    SQ8, T18 = [area(T_, 2048 * i, 8, T) for i in range(2)]
    RR, SS = [area(T_, 512 * i, 4) for i in range(2)]
    COLS = SPARE[:, 9, 0:16]
    SM = SPARE[:, 9, 16:32]
    NB = SPARE[:, 9, 32:40]
    LEVELS = (1, 2, 4, 8, 16, 32, 64)

    def ps_m(bank, nb=2):
        return PS[:, bank:bank + nb, :].rearrange("p b (m t) -> p (b m) t", t=P)

    def ps_t(bank, nb=2):
        return PS[:, bank:bank + nb, :].rearrange("p b (m t) -> p (b m) t", t=T)

    gp = marks("gdn_products", ["ssq", "cols", "rows", "kkqk", "v_nat", "k_nat", "cx0"]
               + [f"{s}{l}" for l in range(1, 7) for s in ("cx", "y")] + ["vn0", "o0", "ks", "vn1", "o1"])
    ga = marks("gdn_scalar", ["beta", "ealog", "ex1", "ln", "sd", "egb", "dt", "kd"] + [f"cxs{l}" for l in range(1, 7)]
               + ["vn0s", "s", "o0s", "vn1s", "o1s"])
    gv = marks("gdn_vector", ["sq", "xg", "ax", "e1", "sp", "g", "scan", "t1", "rn", "qk_norm", "cols_out", "nb", "dt",
                              "gl", "dl", "at", "lt1", "lt2", "lt", "ct0", "vb", "qd", "kdt", "kn"]
               + ["x0", "ct1"] + [s for l in range(1, 6) for s in (f"x{l}", f"ct{l + 1}")] + ["x6", "r1"])
    with nc.Block() as block:
        @block.scalar
        def _(act):
            ga.did("beta", act.activation(ROW(0), GT[0:4, 1, :], ACT.Sigmoid))
            ga.did("ealog", act.activation(HC[0:4, 5:6], HC[0:4, 0:1], ACT.Exp))
            gv.wait(act, "ax")
            ga.did("ex1", act.activation(ROW(2), ROW(2), ACT.Exp, scale=-1.0))
            gv.wait(act, "e1")
            ga.did("ln", act.activation(ROW(2), ROW(2), ACT.Ln))
            gv.wait(act, "t1")
            ga.did("sd", act.activation(T18, T18, ACT.Sqrt))
            gv.wait(act, "gl")
            ga.did("egb", act.activation(EGB, ps_t(4), ACT.Exp))
            gv.wait(act, "dt")
            ga.did("dt", act.activation(DT_, DT_, ACT.Exp))
            gv.wait(act, "dl")
            ga.did("kd", act.activation(SM, SM, ACT.Exp))
            for l in range(1, 7):
                gp.wait(act, f"cx{l}")
                ga.did(f"cxs{l}", act.activation(CX, ps_m(0), ACT.Copy))
            gp.wait(act, "vn0")
            ga.did("vn0s", act.activation(VNEW[:, 0:4, :], ps_m(6, 1), ACT.Copy))
            gp.wait(act, "o0")
            ga.did("s", act.activation(SS, ps_m(0, 1), ACT.Copy))
            ga.did("o0s", act.activation(O8[:, 0:4, 0:P], ps_m(7, 1), ACT.Copy))
            gp.wait(act, "vn1")
            ga.did("vn1s", act.activation(VNEW[:, 4:8, :], ps_m(6, 1), ACT.Copy))
            gp.wait(act, "o1")
            ga.did("o1s", act.activation(O8[:, 0:4, P:T], ps_m(2, 1), ACT.Copy))

        @block.vector
        def _(dve):
            dve.wait_ge(conv_silu, 5)
            gv.did("sq", dve.tensor_tensor(SQ8, CV[:, 0:8, :], CV[:, 0:8, :], ALU.mult))
            gv.did("xg", dve.tensor_scalar(ROW(1), GT[0:4, 0, :], HC[0:4, 1:2], None, ALU.add))
            gv.wait(dve, "xg")
            gv.did("ax", dve.scalar_tensor_tensor(out=ROW(2), in0=ROW(1), scalar=-1.0, in1=ROW(1), op0=ALU.mult, op1=ALU.max))
            ga.wait(dve, "ex1")
            gv.did("e1", dve.tensor_scalar(ROW(2), ROW(2), 1.0, None, ALU.add))
            ga.wait(dve, "ln")
            gv.did("sp", dve.scalar_tensor_tensor(out=ROW(3), in0=ROW(1), scalar=0.0, in1=ROW(2),
                                                  op0=ALU.max, op1=ALU.add))
            gv.wait(dve, "sp")
            gv.did("g", dve.tensor_scalar(ROW(4), ROW(3), HC[0:4, 5:6], -1.0, ALU.mult, ALU.mult))
            gv.wait(dve, "g")
            gv.did("scan", dve.tensor_tensor_scan(ROW(5), cst("reset128", 4), ROW(4), 0.0, ALU.mult, ALU.add))
            gp.wait(dve, "ssq")
            gv.did("t1", dve.tensor_scalar(T18, ps_t(0, 4), EPS, None, ALU.add))
            ga.wait(dve, "sd")
            gv.did("rn", dve.reciprocal(T18, T18))
            gv.wait(dve, "rn")
            dve.scalar_tensor_tensor(out=fl(CV[:, 0:4, :]), in0=fl(CV[:, 0:4, :]), scalar=float(P) ** -0.5,
                                     in1=fl(T18[:, 0:4, :]), op0=ALU.mult, op1=ALU.mult)
            gv.did("qk_norm", dve.tensor_tensor(CV[:, 4:8, :], CV[:, 4:8, :], T18[:, 4:8, :], ALU.mult))
            gp.wait(dve, "cols")
            gv.did("cols_out", dve.tensor_copy(COLS, PS[:, 6, 0:16]))
            gv.wait(dve, "cols_out")
            gv.did("nb", dve.tensor_scalar(NB, COLS[:, 8:16], -1.0, None, ALU.mult))
            gp.wait(dve, "rows")
            for m in range(8):
                c, h = m // 4, m % 4
                last = dve.scalar_tensor_tensor(out=DT_[:, m, :], in0=ps_t(4)[:, h, c * P:(c + 1) * P],
                                                scalar=COLS[:, m:m + 1], in1=cst("causal_T"),
                                                op0=ALU.subtract, op1=ALU.add)
            gv.did("dt", last)
            ends = ps_t(4).rearrange("p h (c t) -> p c h t", c=2)[:, :, :, P - 1]
            gv.did("gl", dve.tensor_copy(SM[:, 8:16].rearrange("p (c h) -> p c h", c=2), ends))
            gv.wait(dve, "gl")
            gv.did("dl", dve.tensor_tensor(SM[:, 0:8], SM[:, 8:16], COLS[:, 0:8], ALU.subtract))
            gp.wait(dve, "kkqk")
            ga.wait(dve, "dt")
            gv.did("at", dve.tensor_tensor(AT_, ps_m(2), DT_, ALU.mult))
            gv.did("lt1", dve.tensor_tensor(LT_, ps_m(0), DT_, ALU.mult))
            gv.wait(dve, "lt1")
            gv.did("lt2", dve.tensor_tensor(LT_, LT_, repeated(cst("strict_T"), 8), ALU.mult))
            gv.wait(dve, "lt2")
            for c in range(2):
                last = dve.tensor_tensor(LT_[:, 4 * c:4 * c + 4, :], LT_[:, 4 * c:4 * c + 4, :],
                                         ps_t(6)[:, :, c * P:(c + 1) * P], ALU.mult)
            gv.did("lt", last)
            gv.wait(dve, "lt")
            gv.did("ct0", dve.tensor_tensor(CT, LT_, repeated(cst("level1"), 8), ALU.mult))
            gp.wait(dve, "v_nat")
            gv.did("vb", dve.tensor_tensor(VB, ps_m(6), spread(COLS[:, 8:16], P), ALU.mult))
            ga.wait(dve, "egb")
            gv.did("qd", dve.tensor_tensor(QD, CV[:, 0:4, :], EGB, ALU.mult))
            gv.did("kdt", dve.tensor_tensor(KDT, CV[:, 4:8, :], EGB, ALU.mult))
            gp.wait(dve, "k_nat")
            ga.wait(dve, "kd")
            gv.did("kn", dve.tensor_tensor(KN, ps_m(4), spread(SM[:, 0:8], P), ALU.mult))
            gp.wait(dve, "cx0")
            dve.tensor_tensor(XI, repeated(IDENT, 8), ps_m(0), ALU.subtract)
            gv.did("x0", dve.tensor_tensor(XT, repeated(IDENT, 8), CT, ALU.subtract))
            gv.wait(dve, "x0")
            gv.did("ct1", dve.tensor_tensor(CT, LT_, repeated(cst("level2"), 8), ALU.mult))
            for l in range(1, 7):
                gp.wait(dve, f"y{l}")
                if l < 6:
                    dve.tensor_tensor(XI, XI, ps_m(2), ALU.subtract)
                gv.did(f"x{l}", dve.tensor_tensor(XT, XT, ps_m(4), ALU.subtract))
                if l < 6:
                    gv.did(f"ct{l + 1}", dve.tensor_tensor(CT, LT_, repeated(cst(f"level{LEVELS[l + 1]}"), 8), ALU.mult))
            gp.wait(dve, "ks")
            for h in range(4):
                last = dve.scalar_tensor_tensor(out=RR[:, h, :], in0=ps_m(1, 1)[:, h, :], scalar=NB[:, 4 + h:5 + h],
                                                in1=VB[:, 4 + h, :], op0=ALU.mult, op1=ALU.add)
            gv.did("r1", last)

        @block.tensor
        def _(pe):
            mmul = nc.tensor.matmul

            def each(dst, lhs, rhs, ms):
                for n, m in enumerate(ms):
                    last = mmul(dst[:, n, :], lhs(m), rhs(m), start=True, stop=True)
                return last

            def turn(dst, src, ms):
                for n, m in enumerate(ms):
                    last = nc.tensor.transpose(dst[:, n, :], src(m), IDENT)
                return last

            chunk = lambda base, m: CV[:, base + m % 4, (m // 4) * P:(m // 4 + 1) * P]
            gv.wait(pe, "sq")
            for b in range(4):
                last = mmul(PS[:, b, :], ONES, fl(SQ8[:, 2 * b:2 * b + 2, :]), start=True, stop=True)
            gp.did("ssq", last)
            gv.wait(pe, "scan")
            ga.wait(pe, "beta")
            for n, row in enumerate((ROW(5), ROW(0))):
                for c in range(2):
                    last = nc.tensor.transpose(PS[:, 6, 8 * n + 4 * c:8 * n + 4 * c + 4], row[:, c * P:(c + 1) * P],
                                               IDENT[0:4, 0:4])
            gp.did("cols", last)
            gv.wait(pe, "cols_out")
            for n, row in enumerate((ROW(5), ROW(0))):
                for h in range(4):
                    last = mmul(ps_t(4 + 2 * n)[:, h, :], SEL[0:4, h, :], row, start=True, stop=True)
            gp.did("rows", last)
            gv.wait(pe, "qk_norm")
            each(ps_m(0), lambda m: chunk(4, m), lambda m: chunk(4, m), range(8))
            gp.did("kkqk", each(ps_m(2), lambda m: chunk(4, m), lambda m: chunk(0, m), range(8)))
            gv.wait(pe, "lt")
            gp.did("v_nat", turn(ps_m(6), lambda m: chunk(8, m), range(8)))
            ga.wait(pe, "egb")
            gp.did("k_nat", turn(ps_m(4), lambda m: chunk(4, m), range(8)))
            gv.wait(pe, "ct0")
            gp.did("cx0", turn(ps_m(0), lambda m: CT[:, m, :], range(8)))
            for l in range(1, 7):
                gv.wait(pe, f"ct{l}")
                gp.did(f"cx{l}", each(ps_m(0), lambda m: CT[:, m, :], lambda m: XI[:, m, :], range(8)))
                ga.wait(pe, f"cxs{l}")
                if l < 6:
                    each(ps_m(2), lambda m: XT[:, m, :], lambda m: CX[:, m, :], range(8))
                gv.wait(pe, "kn")
                gp.did(f"y{l}", each(ps_m(4), lambda m: CX[:, m, :], lambda m: XT[:, m, :], range(8)))
            gv.wait(pe, "x6")
            gp.did("vn0", each(ps_m(6, 1), lambda m: XT[:, m, :], lambda m: VB[:, m, :], range(4)))
            ga.wait(pe, "vn0s")
            each(ps_m(7, 1), lambda m: VNEW[:, m, :], lambda m: AT_[:, m, :], range(4))
            gp.did("o0", each(ps_m(0, 1), lambda m: KN[:, m, :], lambda m: VNEW[:, m, :], range(4)))
            ga.wait(pe, "s")
            gp.did("ks", each(ps_m(1, 1), lambda m: KDT[:, m, P:T], lambda m: SS[:, m, :], range(4)))
            gv.wait(pe, "r1")
            gp.did("vn1", each(ps_m(6, 1), lambda m: XT[:, 4 + m, :], lambda m: RR[:, m, :], range(4)))
            ga.wait(pe, "vn1s")
            for h in range(4):
                mmul(ps_m(2, 1)[:, h, :], SS[:, h, :], QD[:, h, P:T], start=True, stop=False)
                last = mmul(ps_m(2, 1)[:, h, :], VNEW[:, 4 + h, :], AT_[:, 4 + h, :], start=False, stop=True)
            gp.did("o1", last)
    if stop == 1:
        return ctx

    lp = marks("mlstm_products", ["cols", "rows", "kq", "v_nat", "den_num"])
    la = marks("mlstm_scalar", ["sig", "ex1", "ln", "em", "exp", "ad"])
    lv = marks("mlstm_vector", ["i", "xf", "ax", "e1", "lf", "scan", "c", "m", "nm", "bm", "cols_out", "e", "p", "vn",
                                "md", "rd", "h", "o"])
    EE = area(R_, 6144, 4, 384)
    PP = area(R_, 6144 + 1536, 4, 384)
    DD = area(R_, 6144 + 3072, 4, T)
    SIG = area(R_, 6144 + 4096, 4, T)
    VNM = area(R_, 6144 + 5120, 8)
    with nc.Block() as block:
        @block.scalar
        def _(act):
            la.did("sig", act.activation(SIG, BIG[:, MO:MO + 4, :], ACT.Sigmoid))
            lv.wait(act, "ax")
            la.did("ex1", act.activation(ROW(2), ROW(2), ACT.Exp, scale=-1.0))
            lv.wait(act, "e1")
            la.did("ln", act.activation(ROW(2), ROW(2), ACT.Ln))
            lv.wait(act, "bm")
            la.did("em", act.activation(ROW(7), ROW(7), ACT.Exp, scale=-1.0))
            lv.wait(act, "e")
            la.did("exp", act.activation(EE, EE, ACT.Exp))
            lp.wait(act, "den_num")
            la.did("ad", act.activation(DD, ps_t(0), ACT.Abs))

        @block.vector
        def _(dve):
            lv.did("i", dve.tensor_scalar(ROW(0), GT[0:4, 2, :], HC[0:4, 2:3], None, ALU.add))
            lv.did("xf", dve.tensor_scalar(ROW(1), GT[0:4, 3, :], HC[0:4, 3:4], None, ALU.add))
            lv.wait(dve, "xf")
            lv.did("ax", dve.scalar_tensor_tensor(out=ROW(2), in0=ROW(1), scalar=-1.0, in1=ROW(1), op0=ALU.mult, op1=ALU.max))
            la.wait(dve, "ex1")
            lv.did("e1", dve.tensor_scalar(ROW(2), ROW(2), 1.0, None, ALU.add))
            la.wait(dve, "ln")
            lv.did("lf", dve.scalar_tensor_tensor(out=ROW(3), in0=ROW(1), scalar=0.0, in1=ROW(2),
                                                  op0=ALU.min, op1=ALU.subtract))
            lv.wait(dve, "lf")
            lv.did("scan", dve.tensor_tensor_scan(ROW(4), UNIT[0:4, :], ROW(3), 0.0, ALU.mult, ALU.add))
            lv.wait(dve, "scan")
            lv.did("c", dve.tensor_tensor(ROW(5), ROW(0), ROW(4), ALU.subtract))
            lv.wait(dve, "c")
            lv.did("m", dve.tensor_tensor_scan(ROW(6), ROW(5), ROW(5), 0.0, ALU.max, ALU.max))
            lv.wait(dve, "m")
            lv.did("nm", dve.tensor_scalar(ROW(8), ROW(6), -1.0, None, ALU.mult))
            lv.did("bm", dve.tensor_tensor(ROW(7), ROW(4), ROW(6), ALU.add))
            lp.wait(dve, "cols")
            lv.did("cols_out", dve.tensor_copy(COLS[:, 0:8], PS[:, 0, 0:8]))
            lv.wait(dve, "cols_out")
            lp.wait(dve, "rows")
            for h in range(4):
                nm = ps_t(4)[:, h, :]
                dve.scalar_tensor_tensor(out=EE[:, h, 0:P], in0=nm[:, 0:P], scalar=COLS[:, h:h + 1],
                                         in1=cst("causal_T"), op0=ALU.add, op1=ALU.add)
                dve.tensor_scalar(EE[:, h, P:T], nm[:, P:T], COLS[:, h:h + 1], None, ALU.add)
                last = dve.scalar_tensor_tensor(out=EE[:, h, T:384], in0=nm[:, P:T], scalar=COLS[:, 4 + h:5 + h],
                                                in1=cst("causal_T"), op0=ALU.add, op1=ALU.add)
            lv.did("e", last)
            lp.wait(dve, "kq")
            la.wait(dve, "exp")
            lv.did("p", dve.scalar_tensor_tensor(out=PP, in0=PS[:, 0:4, 0:384], scalar=float(P) ** -0.5, in1=EE,
                                                 op0=ALU.mult, op1=ALU.mult))
            lp.wait(dve, "v_nat")
            lv.did("vn", dve.tensor_copy(VNM, ps_m(4)))
            lp.wait(dve, "den_num")
            la.wait(dve, "ad")
            lv.did("md", dve.tensor_tensor(DD, DD, ps_t(6), ALU.max))
            lv.wait(dve, "md")
            lv.did("rd", dve.reciprocal(DD, DD))
            lv.wait(dve, "rd")
            lv.did("h", dve.tensor_tensor(DD, DD, ps_t(2), ALU.mult))
            lv.wait(dve, "h")
            la.wait(dve, "sig")
            lv.did("o", dve.tensor_tensor(O8[:, 4:8, :], DD, SIG, ALU.mult))

        @block.tensor
        def _(pe):
            mmul = nc.tensor.matmul
            lv.wait(pe, "c")
            for c in range(2):
                last = nc.tensor.transpose(PS[:, 0, 4 * c:4 * c + 4], ROW(5)[:, c * P:(c + 1) * P], IDENT[0:4, 0:4])
            lp.did("cols", last)
            lv.wait(pe, "nm")
            la.wait(pe, "em")
            for n, row in enumerate((ROW(8), ROW(7))):
                for h in range(4):
                    last = mmul(ps_t(4 + 2 * n)[:, h, :], SEL[0:4, h, :], row, start=True, stop=True)
            lp.did("rows", last)
            lv.wait(pe, "cols_out")
            for h in range(4):
                q, k = CV[:, 12 + h, :], CV[:, 16 + h, :]
                mmul(PS[:, h, 0:T], k[:, 0:P], q, start=True, stop=True)
                last = mmul(PS[:, h, T:384], k[:, P:T], q[:, P:T], start=True, stop=True)
            lp.did("kq", last)
            lv.wait(pe, "e")
            for c in range(2):
                for h in range(4):
                    last = nc.tensor.transpose(ps_m(4)[:, 4 * c + h, :], BIG[:, MV + h, c * P:(c + 1) * P], IDENT)
            lp.did("v_nat", last)
            lv.wait(pe, "vn")
            for h in range(4):
                for bank, lhs in ((0, [ONES, ONES]), (2, [VNM[:, h, :], VNM[:, 4 + h, :]])):
                    dst = ps_t(bank)[:, h, :]
                    mmul(dst, lhs[0], PP[:, h, 0:T], start=True, stop=False)
                    last = mmul(dst[:, P:T], lhs[1], PP[:, h, T:384], start=False, stop=True)
            lp.did("den_num", last)
    if stop == 2:
        return ctx

    hp = marks("headnorm_products", ["ssq"])
    ha = marks("headnorm_scalar", ["silu", "sd"])
    hv = marks("headnorm_vector", ["sq", "ms", "rs", "scaled", "gated"])
    GATE = area(R_, 6144, 4, T)
    with nc.Block() as block:
        @block.scalar
        def _(act):
            ha.did("silu", act.activation(GATE, BIG[:, GZ:GZ + 4, :], ACT.Silu))
            hv.wait(act, "ms")
            ha.did("sd", act.activation(T18, T18, ACT.Sqrt))

        @block.vector
        def _(dve):
            hv.did("sq", dve.tensor_tensor(SQ8, O8, O8, ALU.mult))
            hp.wait(dve, "ssq")
            hv.did("ms", dve.tensor_scalar(T18, ps_t(0, 4), 1.0 / P, EPS, ALU.mult, ALU.add))
            ha.wait(dve, "sd")
            hv.did("rs", dve.reciprocal(T18, T18))
            hv.wait(dve, "rs")
            for i in range(8):
                gain = par("gdn_norm") if i < 4 else par("mlstm_norm", i - 4)
                last = dve.scalar_tensor_tensor(out=NT[:, i, :], in0=O8[:, i, :], scalar=gain, in1=T18[:, i, :],
                                                op0=ALU.mult, op1=ALU.mult)
            hv.did("scaled", last)
            hv.wait(dve, "scaled")
            ha.wait(dve, "silu")
            hv.did("gated", dve.tensor_tensor(NT[:, 0:4, :], NT[:, 0:4, :], GATE, ALU.mult))

        @block.tensor
        def _(pe):
            hv.wait(pe, "sq")
            for b in range(4):
                last = nc.tensor.matmul(PS[:, b, :], ONES, fl(SQ8[:, 2 * b:2 * b + 2, :]), start=True, stop=True)
            hp.did("ssq", last)

    rg_loaded = sem("rglru_loaded")
    rp = marks("rglru_products", ["r", "i"])
    ra = marks("rglru_scalar", ["le", "ll", "r", "i", "tanh", "a", "sqrt", "gelu"])
    rv = marks("rglru_vector", ["labs", "l1", "lneg", "lsp", "lsp8", "d1", "rec", "sq", "ix", "inp", "scan", "out"])
    WA_, WX_ = area(R_, 6144, 4), area(R_, 6656, 4)
    RR4, II4, TH, AA, GE, DE, HH = [area(R_, 7168 + 1024 * i, 4, T) for i in range(7)]
    LAM = SPARE[:, 9, 64:68]
    LT1, LT2, LSP, LNEG8 = [SPARE[:, 9, 68 + 4 * i:72 + 4 * i] for i in range(4)]
    XB = CV[:, 20:24, :]
    with nc.Block() as block:
        @block.sync
        def _(sp):
            sp.dma_start(WA_, A["rglru_w_a"][0].rearrange("n i j -> i n j")).then_inc(rg_loaded, 16)
            sp.dma_start(WX_, A["rglru_w_x"][0].rearrange("n i j -> i n j")).then_inc(rg_loaded, 16)

        @block.scalar
        def _(act):
            rv.wait(act, "labs")
            ra.did("le", act.activation(LT1, LT1, ACT.Exp, scale=-1.0))
            rv.wait(act, "l1")
            ra.did("ll", act.activation(LT1, LT1, ACT.Ln))
            rp.wait(act, "r")
            for n in range(4):
                last = act.activation(RR4[:, n, :], ps_t(0)[:, n, :], ACT.Sigmoid, bias=par("rglru_b_a", n))
            ra.did("r", last)
            rp.wait(act, "i")
            for n in range(4):
                last = act.activation(II4[:, n, :], ps_t(2)[:, n, :], ACT.Sigmoid, bias=par("rglru_b_x", n))
            ra.did("i", last)
            rv.wait(act, "lsp8")
            ra.wait(act, "r")
            for n in range(4):
                last = act.activation(TH[:, n, :], RR4[:, n, :], ACT.Tanh, scale=LSP[:, n:n + 1])
            ra.did("tanh", last)
            for n in range(4):
                last = act.activation(AA[:, n, :], RR4[:, n, :], ACT.Exp, scale=LNEG8[:, n:n + 1])
            ra.did("a", last)
            rv.wait(act, "sq")
            ra.did("sqrt", act.activation(TH, TH, ACT.Sqrt))
            ra.did("gelu", act.activation(GE, BIG[:, RG:RG + 4, :], ACT.Gelu_apprx_tanh))

        @block.vector
        def _(dve):
            lam = par("rglru_lambda", 0, 4)
            rv.did("labs", dve.scalar_tensor_tensor(out=LT1, in0=lam, scalar=-1.0, in1=lam, op0=ALU.mult, op1=ALU.max))
            ra.wait(dve, "le")
            rv.did("l1", dve.tensor_scalar(LT1, LT1, 1.0, None, ALU.add))
            rv.did("lneg", dve.tensor_scalar(LT2, lam, -1.0, 0.0, ALU.mult, ALU.max))
            rv.wait(dve, "lneg")
            ra.wait(dve, "ll")
            rv.did("lsp", dve.tensor_tensor(LSP, LT2, LT1, ALU.add))
            rv.wait(dve, "lsp")
            dve.tensor_scalar(LNEG8, LSP, -8.0, None, ALU.mult)
            rv.did("lsp8", dve.tensor_scalar(LSP, LSP, 8.0, None, ALU.mult))
            ra.wait(dve, "tanh")
            rv.did("d1", dve.tensor_scalar(DE, TH, 1.0, None, ALU.add))
            rv.wait(dve, "d1")
            rv.did("rec", dve.reciprocal(DE, DE))
            rv.wait(dve, "rec")
            rv.did("sq", dve.scalar_tensor_tensor(out=fl(TH), in0=fl(TH), scalar=2.0, in1=fl(DE),
                                                  op0=ALU.mult, op1=ALU.mult))
            ra.wait(dve, "i")
            rv.did("ix", dve.tensor_tensor(II4, II4, XB, ALU.mult))
            rv.wait(dve, "ix")
            ra.wait(dve, "sqrt")
            rv.did("inp", dve.tensor_tensor(II4, II4, TH, ALU.mult))
            rv.wait(dve, "inp")
            for n in range(4):
                last = dve.tensor_tensor_scan(HH[:, n, :], AA[:, n, :], II4[:, n, :], 0.0, ALU.mult, ALU.add)
            rv.did("scan", last)
            rv.wait(dve, "scan")
            ra.wait(dve, "gelu")
            rv.did("out", dve.tensor_tensor(NT[:, 8:12, :], HH, GE, ALU.mult))

        @block.tensor
        def _(pe):
            pe.wait_ge(rg_loaded, 32)
            for name, w, bank in (("r", WA_, 0), ("i", WX_, 2)):
                for n in range(4):
                    last = nc.tensor.matmul(ps_t(bank)[:, n, :], w[:, n, :], XB[:, n, :], start=True, stop=True)
                rp.did(name, last)
    if stop == 3:
        return ctx

    wload = sem("rwkv_loaded")
    wp = marks("rwkv_products", ["w2", "a2", "g2", "kkss", "v_nat", "b_nat", "k_nat", "lt", "pt", "qbt", "qkt", "cx0"]
               + [s for l in range(1, 6) for s in ((f"cx{l}", f"y{l}", f"yt{l}") if l < 5 else (f"cx{l}", f"yt{l}"))]
               + [s for c in range(4) for s in ((f"r{c}", f"u{c}", f"y_{c}") + ((f"s{c}",) if c < 3 else ()))]
               + ["mean", "rk", "var"])
    wa = marks("rwkv_scalar", ["tanh", "sg", "sig", "a", "g", "w", "wi", "wp", "kksd", "vn", "bn", "kn"]
               + [f"cxs{l}" for l in range(1, 6)]
               + [s for c in range(4) for s in (f"r{c}", f"u{c}", f"y_{c}")] + ["sd"])
    wv = marks("rwkv_vector", ["diff0", "diff", "dmu", "mix", "ld", "cum", "cmp", "kkr", "kksq", "kkt", "kkrec", "kk",
                               "am1", "kp", "rt", "kt", "b", "bt", "at0", "at", "zero", "lt", "pt", "ct0",
                               "qbt", "qkt", "x0", "ct1"]
               + [s for l in range(1, 5) for s in (f"x{l}", f"xt{l}", f"ct{l + 1}")] + ["xt5"]
               + [s for c in range(3) for s in (f"sa{c}", f"s{c}")]
               + ["rk0", "rk1", "cen", "var", "ms", "rs", "n0", "n1", "n2", "rkv", "n3", "out"])
    W2, A2, G2 = R_[0:64, 0:512], R_[64:128, 0:512], R_[:, 512:1024]
    DIFF = area(R_, 1024, 14, T)
    MIXED = BIG[:, 40:54, :]
    r4, k4, v4 = [BIG[:, 40 + 4 * i:44 + 4 * i, :] for i in range(3)]
    e4 = [BIG[:, 4 * i:4 * i + 4, :] for i in range(10)]
    LD, CUM, WC, WI, WP_, AS, GG, KKN, KP_, RTL = e4
    KTL, BTL, ATL, T4 = [area(T_, 1024 * i, 4, T) for i in range(4)]
    M16 = [area(R_, 2048 * i, 16) for i in range(8)]
    MLT, MPT, MQB, MQK, MXI, MXT, MCT, MCX = M16

    def mat(h, t):
        return 8 * (h % 2) + 2 * (h // 2) + t

    VNW, BNW, KNW = [fl(e).rearrange("p (t c) -> p t c", t=2) for e in (AS, CUM, WI)]
    SW = fl(BIG[:, 54:56, :]).rearrange("p (h i) -> p h i", h=4)
    RS_, US = [fl(BIG[:, 56 + 2 * i:58 + 2 * i, :]) for i in range(2)]
    YW = fl(BIG[:, 60:64, :]).rearrange("p (h t) -> p h t", h=4)
    with nc.Block() as block:
        @block.sync
        def _(sp):
            sp.dma_start(W2, A["rwkv_w2"][0]).then_inc(wload, 16)
            sp.dma_start(A2, A["rwkv_a2"][0]).then_inc(wload, 16)
            sp.dma_start(G2, A["rwkv_g2"][0]).then_inc(wload, 16)

        @block.scalar
        def _(act):
            wv.wait(act, "mix")
            wa.did("tanh", act.activation(BIG[0:64, WWA, :], BIG[0:64, WWA, :], ACT.Tanh))
            wa.did("sg", act.activation(BIG[:, WG, :], BIG[:, WG, :], ACT.Sigmoid))
            wp.wait(act, "w2")
            for i in range(4):
                last = act.activation(LD[:, i, :], ps_t(0)[:, i, :], ACT.Sigmoid, bias=par("rwkv_w0", i))
            wa.did("sig", last)
            wp.wait(act, "a2")
            for i in range(4):
                last = act.activation(AS[:, i, :], ps_t(2)[:, i, :], ACT.Sigmoid, bias=par("rwkv_a0", i))
            wa.did("a", last)
            wp.wait(act, "g2")
            wa.did("g", act.activation(GG, ps_t(4), ACT.Copy))
            wv.wait(act, "cmp")
            wa.did("w", act.activation(WC, CUM, ACT.Exp))
            wa.did("wi", act.activation(WI, CUM, ACT.Exp, scale=-1.0))
            wa.did("wp", act.activation(WP_, LD, ACT.Exp))
            wv.wait(act, "kkt")
            wa.did("kksd", act.activation(T4, T4, ACT.Sqrt))
            wv.wait(act, "at")
            wp.wait(act, "v_nat")
            wa.did("vn", act.activation(VNW, PS[:, 0:2, :], ACT.Copy))
            wp.wait(act, "b_nat")
            wa.did("bn", act.activation(BNW, PS[:, 2:4, :], ACT.Copy))
            wp.wait(act, "k_nat")
            wa.did("kn", act.activation(KNW, PS[:, 4:6, :], ACT.Copy))
            for l in range(1, 6):
                wp.wait(act, f"cx{l}")
                wa.did(f"cxs{l}", act.activation(MCX, ps_m(0, 4), ACT.Copy))
            for c in range(4):
                rows = slice(64 * (c % 2), 64 * (c % 2) + 64)
                wp.wait(act, f"r{c}")
                wa.did(f"r{c}", act.activation(RS_[rows, :], PS[rows, 0, :], ACT.Copy))
                wp.wait(act, f"u{c}")
                wa.did(f"u{c}", act.activation(US[rows, :], PS[rows, 1, :], ACT.Copy))
                wp.wait(act, f"y_{c}")
                wa.did(f"y_{c}", act.activation(YW[:, :, 64 * c:64 * c + 64],
                                                PS[:, 2, 0:256].rearrange("p (h t) -> p h t", h=4), ACT.Copy))
            wv.wait(act, "ms")
            wa.did("sd", act.activation(T4, T4, ACT.Sqrt))

        @block.vector
        def _(dve):
            def stt(out, a, s, b, op0, op1):
                return dve.scalar_tensor_tensor(out=out, in0=a, scalar=s, in1=b, op0=op0, op1=op1)

            wv.did("diff0", dve.tensor_scalar(DIFF[:, :, 0:1], MIXED[:, :, 0:1], -1.0, None, ALU.mult))
            wv.did("diff", dve.tensor_tensor(DIFF[:, :, 1:T], MIXED[:, :, 0:T - 1], MIXED[:, :, 1:T], ALU.subtract))
            wv.wait(dve, "diff")
            wv.did("dmu", dve.tensor_tensor(DIFF, DIFF, spread(par("rwkv_mu", 0, 14), T), ALU.mult))
            wv.wait(dve, "dmu")
            wv.did("mix", dve.tensor_tensor(MIXED, MIXED, DIFF, ALU.add))
            wa.wait(dve, "sig")
            wv.did("ld", dve.tensor_scalar(LD, LD, -float(np.exp(-0.5)), None, ALU.mult))
            wv.wait(dve, "ld")
            for i in range(4):
                last = dve.tensor_tensor_scan(CUM[:, i, :], cst("reset64"), LD[:, i, :], 0.0, ALU.mult, ALU.add)
            wv.did("cum", last)
            wv.wait(dve, "cum")
            wv.did("cmp", dve.tensor_tensor(LD, CUM, LD, ALU.subtract))
            wv.did("kkr", dve.tensor_tensor(KKN, k4, spread(par("rwkv_k_k", 0, 4), T), ALU.mult))
            wv.wait(dve, "kkr")
            wv.did("kksq", dve.tensor_tensor(T4, KKN, KKN, ALU.mult))
            wp.wait(dve, "kkss")
            wv.did("kkt", dve.tensor_scalar(T4, ps_t(6), EPS, None, ALU.add))
            wa.wait(dve, "kksd")
            wv.did("kkrec", dve.reciprocal(T4, T4))
            wv.wait(dve, "kkrec")
            wv.did("kk", dve.tensor_tensor(KKN, KKN, T4, ALU.mult))
            wv.wait(dve, "kk")
            wa.wait(dve, "a")
            for i in range(4):
                last = dve.tensor_scalar(T4[:, i, :], AS[:, i, :], -1.0, par("rwkv_k_a", i), ALU.add, ALU.mult)
            wv.did("am1", last)
            wv.wait(dve, "am1")
            wv.did("kp", stt(fl(KP_), fl(T4), 1.0, fl(k4), ALU.add, ALU.mult))
            wv.wait(dve, "kp")
            wa.wait(dve, "wp")
            wv.did("rt", dve.tensor_tensor(RTL, r4, WC, ALU.mult))
            wv.did("kt", dve.tensor_tensor(KTL, KP_, WI, ALU.mult))
            wv.did("b", dve.tensor_tensor(BTL, KKN, AS, ALU.mult))
            wv.wait(dve, "b")
            wv.did("bt", dve.tensor_tensor(BTL, BTL, WI, ALU.mult))
            wv.did("at0", dve.tensor_tensor(ATL, KKN, WP_, ALU.mult))
            wv.wait(dve, "at0")
            wv.did("at", dve.tensor_scalar(ATL, ATL, -1.0, None, ALU.mult))
            wv.did("zero", dve.memset(SW, 0.0))
            strict, incl = repeated(cst("strict64_T"), 16), repeated(cst("incl64_T"), 16)
            wp.wait(dve, "lt")
            wv.did("lt", stt(MLT, ps_m(0, 4), -1.0, strict, ALU.mult, ALU.mult))
            wp.wait(dve, "pt")
            wv.did("pt", dve.tensor_tensor(MPT, ps_m(4, 4), strict, ALU.mult))
            wv.wait(dve, "lt")
            wv.did("ct0", dve.tensor_tensor(MCT, MLT, repeated(cst("level1"), 16), ALU.mult))
            wp.wait(dve, "qbt")
            wv.did("qbt", dve.tensor_tensor(MQB, ps_m(0, 4), incl, ALU.mult))
            wp.wait(dve, "qkt")
            wv.did("qkt", dve.tensor_tensor(MQK, ps_m(4, 4), incl, ALU.mult))
            wp.wait(dve, "cx0")
            dve.tensor_tensor(MXI, repeated(IDENT, 16), ps_m(0, 4), ALU.subtract)
            wv.did("x0", dve.tensor_tensor(MXT, repeated(IDENT, 16), MCT, ALU.subtract))
            wv.wait(dve, "x0")
            wv.did("ct1", dve.tensor_tensor(MCT, MLT, repeated(cst("level2"), 16), ALU.mult))
            for l in range(1, 5):
                wp.wait(dve, f"y{l}")
                wp.wait(dve, f"yt{l}")
                wv.did(f"x{l}", dve.tensor_tensor(MXI, MXI, ps_m(4, 4), ALU.subtract))
                wv.did(f"xt{l}", dve.tensor_tensor(MXT, MXT, ps_m(0, 4), ALU.subtract))
                wv.did(f"ct{l + 1}", dve.tensor_tensor(MCT, MLT, repeated(cst(f"level{LEVELS[l + 1]}"), 16), ALU.mult))
            wp.wait(dve, "yt5")
            wv.did("xt5", dve.tensor_tensor(MXT, MXT, ps_m(0, 4), ALU.subtract))
            for c in range(3):
                wp.wait(dve, f"s{c}")
                if c == 0:
                    wv.wait(dve, "zero")
                for e in range(2):
                    q = slice(64 * e, 64 * e + 64)
                    last = dve.tensor_tensor(SW[q, :, q], SW[q, :, q], ps_m(3, 1)[q, :, q], ALU.add)
                wv.did(f"sa{c}", last)
                wv.wait(dve, f"sa{c}")
                for e in range(2):
                    q = slice(64 * e, 64 * e + 64)
                    decay = WC[q, :, 64 * c + 63:64 * c + 64].broadcast_to([64, 4, 64])
                    last = dve.tensor_tensor(SW[q, :, q], SW[q, :, q], decay, ALU.mult)
                wv.did(f"s{c}", last)
            wv.did("rk0", dve.tensor_tensor(LD, r4, KP_, ALU.mult))
            wv.wait(dve, "rk0")
            wv.did("rk1", dve.tensor_tensor(LD, LD, spread(par("rwkv_r_k", 0, 4), T), ALU.mult))
            wp.wait(dve, "mean")
            wv.did("cen", stt(YW, ps_t(4), -1.0 / 64, YW, ALU.mult, ALU.add))
            wv.wait(dve, "cen")
            wv.did("var", dve.tensor_tensor(KKN, YW, YW, ALU.mult))
            wp.wait(dve, "var")
            wv.did("ms", dve.tensor_scalar(T4, ps_t(6), 1.0 / 64, 64e-5, ALU.mult, ALU.add))
            wa.wait(dve, "sd")
            wv.did("rs", dve.reciprocal(T4, T4))
            wv.wait(dve, "rs")
            wv.did("n0", dve.tensor_tensor(YW, YW, T4, ALU.mult))
            wv.wait(dve, "n0")
            wv.did("n1", dve.tensor_tensor(YW, YW, spread(par("rwkv_ln_w", 0, 4), T), ALU.mult))
            wv.wait(dve, "n1")
            wv.did("n2", dve.tensor_tensor(YW, YW, spread(par("rwkv_ln_b", 0, 4), T), ALU.add))
            wv.did("rkv", dve.tensor_tensor(KKN, v4, ps_t(0), ALU.mult))
            wv.wait(dve, "rkv")
            wv.did("n3", dve.tensor_tensor(YW, YW, KKN, ALU.add))
            wv.wait(dve, "n3")
            wv.did("out", dve.tensor_tensor(NT[:, 12:16, :], YW, GG, ALU.mult))

        @block.tensor
        def _(pe):
            mmul = nc.tensor.matmul
            pe.wait_ge(wload, 48)
            wa.wait(pe, "sg")
            for name, w, x, bank in (("w2", W2, BIG[0:64, WWA, :], 0), ("a2", A2, BIG[64:128, WWA, :], 2),
                                     ("g2", G2, BIG[:, WG, :], 4)):
                for i in range(4):
                    last = mmul(ps_t(bank)[:, i, :], w[:, i * P:(i + 1) * P], x, start=True, stop=True)
                wp.did(name, last)
            wv.wait(pe, "kksq")
            for b in range(2):
                last = mmul(PS[:, 6 + b, :], ONES64, fl(T4[:, 2 * b:2 * b + 2, :]), start=True, stop=True)
            wp.did("kkss", last)
            wv.wait(pe, "at")
            wa.wait(pe, "g")
            for name, src, bank in (("v_nat", v4, 0), ("b_nat", BTL, 2), ("k_nat", KTL, 4)):
                for t in range(TT):
                    for i in range(4):
                        last = nc.tensor.transpose(PS[:, bank + t, i * P:(i + 1) * P],
                                                   src[:, i, t * P:(t + 1) * P], IDENT)
                wp.did(name, last)
            wa.wait(pe, "kn")
            for name, lhs, rhs, bank in (("lt", BTL, ATL, 0), ("pt", KTL, ATL, 4), ("qbt", BTL, RTL, 0),
                                         ("qkt", KTL, RTL, 4)):
                if name == "qbt":
                    wv.wait(pe, "lt")
                if name == "qkt":
                    wv.wait(pe, "pt")
                for m in range(16):
                    h, t = 2 * (m % 8 // 2) + m // 8, m % 2
                    q = slice(64 * (h % 2), 64 * (h % 2) + 64)
                    last = mmul(ps_m(bank, 4)[:, m, :], lhs[q, h // 2, t * P:(t + 1) * P],
                                rhs[q, h // 2, t * P:(t + 1) * P], start=True, stop=True)
                wp.did(name, last)
            wv.wait(pe, "qbt")
            for m in range(16):
                last = nc.tensor.transpose(ps_m(0, 4)[:, m, :], MCT[:, m, :], IDENT)
            wp.did("cx0", last)
            for l in range(1, 6):
                wv.wait(pe, f"ct{l}")
                for m in range(16):
                    last = mmul(ps_m(0, 4)[:, m, :], MCT[:, m, :], MXI[:, m, :], start=True, stop=True)
                wp.did(f"cx{l}", last)
                wa.wait(pe, f"cxs{l}")
                if l < 5:
                    for m in range(16):
                        last = mmul(ps_m(4, 4)[:, m, :], MXT[:, m, :], MCX[:, m, :], start=True, stop=True)
                    wp.did(f"y{l}", last)
                for m in range(16):
                    last = mmul(ps_m(0, 4)[:, m, :], MCX[:, m, :], MXT[:, m, :], start=True, stop=True)
                wp.did(f"yt{l}", last)
            wv.wait(pe, "xt5")
            for c in range(4):
                t, q = c // 2, slice(64 * (c % 2), 64 * (c % 2) + 64)
                cols = slice(64 * c, 64 * c + 64)
                if c:
                    wv.wait(pe, f"s{c - 1}")
                for hp2 in range(4):
                    if c:
                        mmul(PS[q, 0, hp2 * P:(hp2 + 1) * P], ATL[:, hp2, cols], SW[:, hp2, :], start=True, stop=False)
                    for e in range(2):
                        h = 2 * hp2 + e
                        last = mmul(PS[q, 0, 64 * h:64 * h + 64], MPT[q, mat(h, t), q], VNW[q, t, 64 * h:64 * h + 64],
                                    start=(c == 0), stop=(c == 0 or e == 1))
                wp.did(f"r{c}", last)
                wa.wait(pe, f"r{c}")
                for h in range(8):
                    last = mmul(PS[q, 1, 64 * h:64 * h + 64], MXT[q, mat(h, t), q], RS_[q, 64 * h:64 * h + 64],
                                start=True, stop=True)
                wp.did(f"u{c}", last)
                wa.wait(pe, f"u{c}")
                for hp2 in range(4):
                    dst = PS[:, 2, 64 * hp2:64 * hp2 + 64]
                    if c:
                        mmul(dst, SW[:, hp2, :], RTL[:, hp2, cols], start=True, stop=False)
                    for e in range(2):
                        h = 2 * hp2 + e
                        hc, o = slice(64 * h, 64 * h + 64), slice(64 * e, 64 * e + 64)
                        mmul(dst[o, :], US[q, hc], MQB[q, mat(h, t), q], start=(c == 0), stop=False)
                        last = mmul(dst[o, :], VNW[q, t, hc], MQK[q, mat(h, t), q], start=False, stop=True)
                wp.did(f"y_{c}", last)
                if c < 3:
                    for h in range(8):
                        hc, o = slice(64 * h, 64 * h + 64), slice(64 * (h % 2), 64 * (h % 2) + 64)
                        mmul(PS[o, 3, hc], BNW[q, t, hc], US[q, hc], start=True, stop=False)
                        last = mmul(PS[o, 3, hc], KNW[q, t, hc], VNW[q, t, hc], start=False, stop=True)
                    wp.did(f"s{c}", last)
            wa.wait(pe, "y_3")
            for b in range(2):
                last = mmul(PS[:, 4 + b, :], ONES64, fl(YW[:, 2 * b:2 * b + 2, :]), start=True, stop=True)
            wp.did("mean", last)
            wv.wait(pe, "rk1")
            for b in range(2):
                last = mmul(PS[:, b, :], ONES64, fl(LD[:, 2 * b:2 * b + 2, :]), start=True, stop=True)
            wp.did("rk", last)
            wv.wait(pe, "var")
            for b in range(2):
                last = mmul(PS[:, 6 + b, :], ONES64, fl(KKN[:, 2 * b:2 * b + 2, :]), start=True, stop=True)
            wp.did("var", last)
    if stop == 4:
        return ctx

    N_IN = sum(n for _, n in GROUPS1)
    N_OUT, N_GU = D // 256, F1 // 256
    B0 = N_IN
    B1 = B0 + N_OUT
    B2 = B1 + 2 * N_GU
    B3 = B2 + N_GU
    N_IN2 = sum(n for _, n in GROUPS2)
    B4 = B3 + N_IN2
    acted = sem("hidden_acted")
    hidden = sem("hidden_made")
    res_done = sem("residual_done")
    gain_loaded = sem("gain_loaded")
    gate2_loaded = sem("gate2_loaded")
    gates2_made = sem("gates2_made")
    ACTED = area(T_, 0, 2, 512)
    GAIN1 = fl(BIG[:, 44:52, :])
    WGATE2 = fl(BIG[:, 56:58, :]).rearrange("p (k n) -> p k n", k=KD)

    def row_gain(a):
        return a.rearrange("(o d) -> o d", o=1).broadcast_to([P, D])

    def pe_hidden_pairs(pe, n0, h0, units):
        rounds = units // 2
        def unit(j, r):
            for c in range(2):
                item = n0 + 2 * j + c
                slot = item % SLOTS
                pe.wait_ge(slot_full[slot], 16 * (item // SLOTS + 1) + 16 * r)
                if c == 0:
                    pe.wait_ge(hidden, h0 + 2 * r + j - 1)
                for half in range(2):
                    for k in range(KD):
                        mm = nc.tensor.matmul(PS[:, 2 * (j % 2) + c, half * T:(half + 1) * T],
                                              ring_cols(slot)[:, k, half * P:(half + 1) * P], NT[:, k, :],
                                              start=(k == 0), stop=(k == KD - 1))
                mm.then_inc(item_used, 1)
        assert units % 2 == 0
        with pe.Fori(0, rounds) as r:
            for j in range(2):
                unit(j, r)

    def act_hidden_pairs(act, n0, a0, units):
        with act.Fori(0, units // 2) as r:
            for j in range(2):
                act.wait_ge(item_used, n0 + 4 * r + 2 * j + 1)
                act.wait_ge(hidden, a0 + 2 * r + j - 1)
                act.activation(ACTED[:, j, :], PS[:, 2 * j, :], ACT.Silu).then_inc(acted, 1)

    def dve_hidden_pairs(dve, n0, a0, units):
        with dve.Fori(0, units // 2) as r:
            for j in range(2):
                dve.wait_ge(item_used, n0 + 4 * r + 2 * j + 2)
                dve.wait_ge(acted, a0 + 2 * r + j + 1)
                dve.tensor_tensor(BIG[:, bass.ds(4 * r + 2 * j, 2), :],
                                  ACTED[:, j, :].rearrange("p (c t) -> p c t", c=2),
                                  PS[:, 2 * j + 1, :].rearrange("p (c t) -> p c t", c=2), ALU.mult)\
                    .then_inc(hidden, 1)

    H0 = 2
    with nc.Block() as block:
        @block.sync
        def _(sp):
            n = load_rows(sp, B0, A["w_out"][0])
            n = load_interleaved(sp, n, A["ffn_w_gate"][0], A["ffn_w_up"][0], N_GU)
            sp.dma_start(GAIN1, row_gain(A["final_norm"])).then_inc(gain_loaded, 16)
            for c, k, at in ((NSA_GATES, 24, 0), (FOX_GATES, 8, 24)):
                sp.dma_start(WGATE2[:, :, at:at + k], A["w_in_2"][0][:, c:c + k].rearrange("(k p) n -> p k n", p=P))\
                    .then_inc(gate2_loaded, 16)
            n = load_rows(sp, n, A["ffn_w_down"][0])
            load_cols(sp, n, [(A["w_in_2"][0], c, k) for c, k in GROUPS2])

        @block.scalar
        def _(act):
            norm_act(act, 1, lambda e, t: e.wait_ge(res_done, t + 1))
            act.wait_ge(norm_out, 16)
            act_hidden_pairs(act, B1, H0, N_GU)
            norm_act(act, 2, lambda e, t: e.wait_ge(res_done, 2 + t + 1))
            norm_act(act, 3, lambda e, t: e.wait_ge(res_done, 4 + t + 1))
            at, n, q = 0, B3, N_IN
            for _, pairs in GROUPS2:
                evacuate(act, n, q, pairs, at)
                n, q, at = n + pairs, q + pairs, at + 2 * pairs
            act.wait_ge(gates2_made, 1)
            act.activation(GT[0:24, 0, :], PS[0:24, 6, 0:T], ACT.Copy)
            act.activation(GT[0:8, 1, :], PS[0:8, 6, T:2 * T], ACT.Copy)

        def add_residual(dve, used):
            dve.wait_ge(item_used, used)
            for t in range(TT):
                dve.tensor_tensor(X[:, t, :], X[:, t, :], PS[:, 4 * t:4 * t + 4, :].rearrange("p b n -> p (b n)"),
                                  ALU.add).then_inc(res_done, 1)

        @block.vector
        def _(dve):
            for _ in range(H0):
                dve.engine_nop().then_inc(hidden, 1)
            add_residual(dve, B1)
            dve.wait_ge(res_done, 2)
            norm_dve(dve, 1, "ffn_norm")
            dve_hidden_pairs(dve, B1, 0, N_GU)
            add_residual(dve, B3)
            dve.wait_ge(res_done, 4)
            norm_dve(dve, 2, None)
            dve.wait_ge(gain_loaded, 16)
            for t in range(TT):
                dve.scalar_tensor_tensor(out=X[:, t, :], in0=X[:, t, :], scalar=ST[:, 6 + t:7 + t], in1=GAIN1,
                                         op0=ALU.mult, op1=ALU.mult).then_inc(res_done, 1)
            dve.wait_ge(res_done, 6)
            norm_dve(dve, 3, "g_mix_pre_2")

        @block.tensor
        def _(pe):
            pe_rows(pe, B0, N_OUT, NT)
            norm_pe(pe, 1)
            pe.wait_ge(norm_out, 16)
            pe_hidden_pairs(pe, B1, H0, N_GU)
            pe.wait_ge(hidden, H0 + N_GU)
            pe_rows(pe, B2, N_GU, BIG)
            norm_pe(pe, 3)
            pe.wait_ge(norm_out, 24)
            n, q = B3, N_IN
            for _, pairs in GROUPS2:
                pe_cols(pe, n, q, pairs)
                n, q = n + pairs, q + pairs
            pe.wait_ge(gate2_loaded, 32)
            for at, k, c in ((0, 24, 0), (24, 8, T)):
                for kt in range(KD):
                    mm = nc.tensor.matmul(PS[0:k, 6, c:c + T], WGATE2[:, kt, at:at + k], NT[:, kt, :],
                                          start=(kt == 0), stop=(kt == KD - 1))
            mm.then_inc(gates2_made, 1)
    if stop == 5:
        return ctx

    G8 = area(R_, 0, 24, T)
    VNAT = R_[:, 6144:6144 + 3584].rearrange("p (t c) -> p t c", t=TT)
    KDUP = R_[:, 9728:9728 + 1024].rearrange("p (s g t) -> p s g t", s=2, g=2)
    ZSH = R_[:, 10752:10752 + 1024].rearrange("p (v g t) -> p v g t", v=2, g=2)
    CB = area(R_, 11776, 8, 384)
    VTILES = [AVS, AVW] + [BV + i for i in range(4)] + [CV_ + i for i in range(4)] + [DV + i for i in range(4)]
    W1 = [area(T_, 0, 16, T), BIG[:, 46:62, :]]
    SMALL = R_[:, 14848:16384]
    BT = SMALL[:, 0:960].rearrange("p (v l g n) -> p v l g n", v=2, l=16, g=2)
    W2K = SMALL[:, 960:1216].rearrange("p (h d) -> p h d", h=2)
    W2V = SMALL[:, 1216:1344].rearrange("p (h d) -> p h d", h=2)
    HID = SMALL[:, 1344:1464].rearrange("p (v h n) -> p v h n", v=2, h=2)
    KC = SMALL[:, 1464:1494]
    VC = fl(BIG[:, 62:63, :])[0:15, 0:128]
    GATEC = fl(BIG[:, 62:63, :])[:, 128:176].rearrange("p (t n) -> p t n", t=TT)
    FCOL = fl(BIG[:, 62:63, :])[:, 176:192].rearrange("p (t n) -> p t n", t=TT)
    FR = [GT[0:8, i, :] for i in range(4)] + [fl(BIG[:, 63:64, :])[0:8, :]]
    windows_moved = sem("windows_moved")
    keys_moved = sem("keys_moved")
    cload = sem("cmp_weights_loaded")
    biasin = sem("bias_loaded")
    cp = marks("prep_products", ["hid", "kvc"] + ["vn0", "vn1", "cols", "fox"])
    ca = marks("prep_scalar", ["gates", "fex", "fln", "gelu", "vn0", "vn1"])
    cv = marks("prep_vector", ["bt", "fx", "fax", "fe1", "flf", "fscan", "fn8", "kvc", "cols", "cb"])
    with nc.Block() as block:
        @block.sync
        def _(sp):
            for v, tile in enumerate((AKC, AVC)):
                for g in range(2):
                    src = BIG[64 * g:64 * g + 64, tile, :]
                    sp.dma_start(ZSH[0:64, v, g, :], src).then_inc(windows_moved, 16)
                    sp.dma_start(ZSH[64:128, v, g, 0:T - 1], src[:, 1:T]).then_inc(windows_moved, 16)
            for w, src in zip(W1, ("phik_w1_2", "phiv_w1_2")):
                sp.dma_start(w, A[src][0].rearrange("(l p) h -> p l h", p=P)).then_inc(cload, 16)
            w2 = A["phik_w2_2"][0].rearrange("(h p) d -> p h d", p=P)
            sp.dma_start(W2K[:, :, 0:64], w2).then_inc(cload, 16)
            sp.dma_start(W2K[:, :, 64:128], w2).then_inc(cload, 16)
            sp.dma_start(W2V, A["phiv_w2_2"][0].rearrange("(h p) d -> p h d", p=P)).then_inc(cload, 16)
            for s, tile in enumerate((AKS, AKW)):
                for g in range(2):
                    for e in range(2):
                        sp.dma_start(KDUP[64 * e:64 * e + 64, s, g, :], BIG[64 * g:64 * g + 64, tile, :])\
                            .then_inc(keys_moved, 16)
            skew = bass.AP(bias_skew.tensor, 127, [[383, P], [P * 384, 24], [1, T]])
            sp.dma_start(G8, skew).then_inc(biasin, 16)
            sp.wait_ge(biasin, 16)
            sp.wait_ge(keys_moved, 128)

        @block.scalar
        def _(act):
            ca.did("gates", act.activation(GT[0:24, 0, :], GT[0:24, 0, :], ACT.Sigmoid))
            cv.wait(act, "fax")
            ca.did("fex", act.activation(FR[2], FR[2], ACT.Exp, scale=-1.0))
            cv.wait(act, "fe1")
            ca.did("fln", act.activation(FR[2], FR[2], ACT.Ln))
            cp.wait(act, "hid")
            ca.did("gelu", act.activation(HID, PS[:, 0, 0:120].rearrange("p (v h n) -> p v h n", v=2, h=2),
                                          ACT.Gelu_apprx_tanh))
            for t in range(TT):
                cp.wait(act, f"vn{t}")
                ca.did(f"vn{t}", act.activation(VNAT[:, t, :], fl(PS[:, 2:6, :])[:, 0:1792], ACT.Copy))

        @block.vector
        def _(dve):
            dve.wait_ge(windows_moved, 128)
            for v in range(2):
                for g in range(2):
                    for half in range(2):
                        src = ZSH[:, v, g, 16 * half:16 * half + 240].rearrange("p (n l two) -> p l n two", l=8, two=2)
                        last = dve.tensor_tensor(BT[:, v, 8 * half:8 * half + 8, g, :], src[:, :, :, 0],
                                                 spread(par("cmp_pe_2", 8 * half, 8), 15), ALU.add)
            cv.did("bt", last)
            cv.did("fx", dve.tensor_scalar(FR[1], FR[1], HC[0:8, 4:5], None, ALU.add))
            cv.wait(dve, "fx")
            cv.did("fax", dve.scalar_tensor_tensor(out=FR[2], in0=FR[1], scalar=-1.0, in1=FR[1],
                                                   op0=ALU.mult, op1=ALU.max))
            ca.wait(dve, "fex")
            cv.did("fe1", dve.tensor_scalar(FR[2], FR[2], 1.0, None, ALU.add))
            ca.wait(dve, "fln")
            cv.did("flf", dve.scalar_tensor_tensor(out=FR[3], in0=FR[1], scalar=0.0, in1=FR[2],
                                                   op0=ALU.min, op1=ALU.subtract))
            cv.wait(dve, "flf")
            cv.did("fscan", dve.tensor_tensor_scan(FR[4], UNIT[0:8, :], FR[3], 0.0, ALU.mult, ALU.add))
            cv.wait(dve, "fscan")
            cv.did("fn8", dve.tensor_scalar(FR[4], FR[4], -8.0, None, ALU.mult))
            cp.wait(dve, "kvc")
            dve.tensor_copy(KC, PS[:, 1, 0:30])
            cv.did("kvc", dve.tensor_copy(VC, PS[0:15, 1, 32:160]))
            cp.wait(dve, "cols")
            dve.tensor_copy(GATEC, PS[:, 6, 0:48].rearrange("p (t n) -> p t n", t=TT))
            cv.did("cols", dve.tensor_copy(FCOL, PS[:, 6, 48:64].rearrange("p (t n) -> p t n", t=TT)))
            cv.wait(dve, "cols")
            cp.wait(dve, "fox")
            for h in range(8):
                row = ps_t(2, 4)[:, h, :]
                dve.scalar_tensor_tensor(out=CB[:, h, 0:P], in0=row[:, 0:P], scalar=FCOL[:, 0, h:h + 1],
                                         in1=cst("causal8"), op0=ALU.subtract, op1=ALU.add)
                dve.tensor_scalar(CB[:, h, P:T], row[:, 0:P], FCOL[:, 1, h:h + 1], None, ALU.subtract)
                last = dve.scalar_tensor_tensor(out=CB[:, h, T:384], in0=row[:, P:T], scalar=FCOL[:, 1, h:h + 1],
                                                in1=cst("causal8"), op0=ALU.subtract, op1=ALU.add)
            cv.did("cb", last)

        @block.tensor
        def _(pe):
            mmul = nc.tensor.matmul
            pe.wait_ge(cload, 80)
            cv.wait(pe, "bt")
            for v in range(2):
                for ht in range(2):
                    at = (2 * v + ht) * 30
                    for l in range(16):
                        last = mmul(PS[:, 0, at:at + 30], W1[v][:, l, ht * P:(ht + 1) * P],
                                    BT[:, v, l, :, :].rearrange("p g n -> p (g n)"), start=(l == 0), stop=(l == 15))
            cp.did("hid", last)
            ca.wait(pe, "gelu")
            for ht in range(2):
                mmul(PS[:, 1, 0:30], W2K[:, ht, :], HID[:, 0, ht, :], start=(ht == 0), stop=(ht == 1))
            for g in range(2):
                for ht in range(2):
                    last = mmul(PS[0:15, 1, 32 + 64 * g:96 + 64 * g], HID[:, 1, ht, 15 * g:15 * g + 15], W2V[:, ht, :],
                                start=(ht == 0), stop=(ht == 1))
            cp.did("kvc", last)
            for t in range(TT):
                if t:
                    ca.wait(pe, "vn0")
                for i, tile in enumerate(VTILES):
                    last = nc.tensor.transpose(fl(PS[:, 2:6, :])[:, i * P:(i + 1) * P],
                                               BIG[:, tile, t * P:(t + 1) * P], IDENT)
                cp.did(f"vn{t}", last)
            cv.wait(pe, "fn8")
            ca.wait(pe, "gates")
            for t in range(TT):
                nc.tensor.transpose(PS[:, 6, 24 * t:24 * t + 24], GT[0:24, 0, t * P:(t + 1) * P], IDENT[0:24, 0:24])
                last = nc.tensor.transpose(PS[:, 6, 48 + 8 * t:56 + 8 * t], FR[4][:, t * P:(t + 1) * P], IDENT[0:8, 0:8])
            cp.did("cols", last)
            ca.wait(pe, "vn1")
            for h in range(8):
                last = mmul(ps_t(2, 4)[:, h, :], SEL[:, h, :], FR[4], start=True, stop=True)
            cp.did("fox", last)
    if stop == 6:
        return ctx

    PARTS = [(kind, h) for h in range(8) for kind in ("sel", "win", "cmp")]
    PARTS += [(kind, h) for kind in ("moba", "fox", "long") for h in range(8)]
    NPART = len(PARTS)
    FIRST = {"sel": True, "win": False, "cmp": False}
    LAST = {"sel": False, "win": False, "cmp": True}
    NE, NS, NPT = 4, 3, 3
    E2 = [T_[:, 384 * i:384 * i + 384] for i in range(NE)]
    PT2 = [T_[:, 1536 + 384 * i:1920 + 384 * i] for i in range(NPT)]
    STAT = T_[:, 2688:2688 + 3 * 2 * NPART].rearrange("p (s n q) -> p s n q", s=3, q=2)
    MINS, SUMS, RECS = [STAT[:, i] for i in range(3)]
    scored = sem("scored")
    lowest = sem("lowest")
    exped = sem("exped")
    recip = sem("reciprocals")
    gated = sem("reciprocals_gated")
    probs = sem("probs")
    probs_T = sem("probs_T")
    probs_out = sem("probs_out")
    valued = sem("valued")
    head_out = sem("head_pair_out")

    def query(kind, h):
        tile = {"moba": BQ, "fox": CQ, "long": DQ}.get(kind, AQ) + h // 2
        return BIG[64 * (h % 2):64 * (h % 2) + 64, tile, :]

    def key(kind, h):
        e = slice(64 * (h % 2), 64 * (h % 2) + 64)
        if kind in ("sel", "win"):
            return KDUP[e, ("sel", "win").index(kind), h // 4, :]
        if kind == "cmp":
            return KC[e, 15 * (h // 4):15 * (h // 4) + 15]
        return BIG[e, {"moba": BK, "fox": CK, "long": DK}[kind] + h // 2, :]

    def value(kind, h, t):
        if kind in ("sel", "win"):
            at = P * ("sel", "win").index(kind) + 64 * (h // 4)
        else:
            at = P * {"moba": 2, "fox": 6, "long": 10}[kind] + 64 * h
        return VNAT[:, t, at:at + 64]

    def spans(kind):
        return ((0, 7), (P, 15)) if kind == "cmp" else ((0, P), (P, T))

    def bias_of(kind, h, t):
        if kind == "fox":
            return CB[:, h, 0:P] if t == 0 else CB[:, h, P:384]
        row = G8[:, {"moba": 8, "long": 16}.get(kind, 0) + h, :]
        if kind == "cmp":
            first = 159 if t == 0 else 31
            n = spans(kind)[t][1]
            return row[:, first:first + 16 * (n - 1) + 1:16]
        return row[:, P:T] if t == 0 else row

    def o_index(kind, h):
        return {"moba": 4, "fox": 8, "long": 12}.get(kind, 0) + h // 2

    with nc.Block() as block:
        @block.tensor
        def _(pe):
            mmul = nc.tensor.matmul

            def scores(i):
                kind, h = PARTS[i]
                if i >= NS:
                    pe.wait_ge(lowest, i - NS + 1)
                q, k = query(kind, h), key(kind, h)
                for t, (at, n) in enumerate(spans(kind)):
                    last = mmul(PS[:, i % NS, at:at + n], q[:, t * P:(t + 1) * P], k[:, 0:n], start=True, stop=True)
                last.then_inc(scored, 1)

            def turn_probs(i):
                kind, h = PARTS[i]
                pe.wait_ge(probs, i + 1)
                if i >= NPT:
                    pe.wait_ge(probs_out, i - NPT + 1)
                bank, e = PS[:, 3 + i % NPT, :], E2[i % NE]
                if kind == "cmp":
                    for t, (at, n) in enumerate(spans(kind)):
                        last = nc.tensor.transpose(bank[0:n, at:at + P], e[:, at:at + n], IDENT)
                else:
                    for b in range(3):
                        last = nc.tensor.transpose(bank[:, b * P:(b + 1) * P], e[:, b * P:(b + 1) * P], IDENT)
                last.then_inc(probs_T, 1)

            def values(i):
                kind, h = PARTS[i]
                pe.wait_ge(probs_out, i + 1)
                o, e = o_index(kind, h), 64 * (h % 2)
                first, final = FIRST.get(kind, True), LAST.get(kind, True)
                if first and h % 2 == 0 and o >= 2:
                    pe.wait_ge(head_out, o - 1)
                dst, pt = PS[e:e + 64, 6 + o % 2, 0:T], PT2[i % NPT]
                if kind == "cmp":
                    v = VC[:, 64 * (h // 4):64 * (h // 4) + 64]
                    mmul(dst[:, 0:P], v[0:7, :], pt[0:7, 0:P], start=False, stop=False)
                    last = mmul(dst[:, P:T], v, pt[0:15, P:T], start=False, stop=True)
                else:
                    mmul(dst, value(kind, h, 0), pt[:, 0:T], start=first, stop=False)
                    last = mmul(dst[:, P:T], value(kind, h, 1), pt[:, T:384], start=False, stop=final)
                last.then_inc(valued, 1)

            for i in range(NPART + 3):
                if i < NPART:
                    scores(i)
                if 0 <= i - 2 < NPART:
                    turn_probs(i - 2)
                if 0 <= i - 3 < NPART:
                    values(i - 3)

        @block.vector
        def _(dve):
            def lowest_of(i):
                kind, h = PARTS[i]
                dve.wait_ge(scored, i + 1)
                if i >= NE:
                    dve.wait_ge(probs_T, i - NE + 1)
                for t, (at, n) in enumerate(spans(kind)):
                    last = dve.tensor_tensor_reduce(E2[i % NE][:, at:at + n], PS[:, i % NS, at:at + n],
                                                    bias_of(kind, h, t), -0.125, 3e38, ALU.add, ALU.min,
                                                    MINS[:, i, t:t + 1])
                last.then_inc(lowest, 1)

            def weights(i):
                kind, h = PARTS[i]
                dve.wait_ge(exped, i + 1)
                dve.reciprocal(RECS[:, i, :], SUMS[:, i, :]).then_inc(recip, 1)
                dve.wait_ge(recip, i + 1)
                if i < 24:
                    gate = GATEC[:, :, 8 * ("cmp", "sel", "win").index(kind) + h]
                    dve.tensor_tensor(RECS[:, i, :], RECS[:, i, :], gate, ALU.mult).then_inc(gated, 1)
                    dve.wait_ge(gated, i + 1 + i // 3)
                    if kind == "cmp":
                        dve.tensor_tensor(RECS[:, i, 0:1], RECS[:, i, 0:1], cst("from31"), ALU.mult).then_inc(gated, 1)
                        dve.wait_ge(gated, i + 2 + i // 3)
                for t, (at, n) in enumerate(spans(kind)):
                    e = E2[i % NE][:, at:at + n]
                    last = dve.tensor_scalar(e, e, RECS[:, i, t:t + 1], None, ALU.mult)
                last.then_inc(probs, 1)

            for i in range(NPART + 1):
                if i < NPART:
                    lowest_of(i)
                if i >= 1:
                    weights(i - 1)

        @block.scalar
        def _(act):
            def exponentials(i):
                kind, h = PARTS[i]
                act.wait_ge(lowest, i + 1)
                for t, (at, n) in enumerate(spans(kind)):
                    e = E2[i % NE][:, at:at + n]
                    last = act.activation(e, e, ACT.Exp, bias=MINS[:, i, t:t + 1], scale=-1.0,
                                          accum_out=SUMS[:, i, t:t + 1])
                last.then_inc(exped, 1)

            def probs_to_sbuf(i):
                kind, h = PARTS[i]
                act.wait_ge(probs_T, i + 1)
                if i >= NPT:
                    act.wait_ge(valued, i - NPT + 1)
                bank = PS[:, 3 + i % NPT, :]
                if kind == "cmp":
                    act.activation(PT2[i % NPT][0:7, 0:P], bank[0:7, 0:P], ACT.Copy)
                    last = act.activation(PT2[i % NPT][0:15, P:T], bank[0:15, P:T], ACT.Copy)
                else:
                    last = act.activation(PT2[i % NPT], bank[:, 0:384], ACT.Copy)
                last.then_inc(probs_out, 1)

            def heads_out(i):
                kind, h = PARTS[i]
                if h % 2 == 1 and LAST.get(kind, True):
                    o = o_index(kind, h)
                    act.wait_ge(valued, i + 1)
                    act.activation(NT[:, o, :], PS[:, 6 + o % 2, 0:T], ACT.Copy).then_inc(head_out, 1)

            for i in range(NPART + 4):
                if i < NPART:
                    exponentials(i)
                if 0 <= i - 2 < NPART:
                    probs_to_sbuf(i - 2)
                if 0 <= i - 4 < NPART:
                    heads_out(i - 4)
    if stop == 7:
        return ctx

    C0, C1 = B4, B4 + N_OUT
    N_UP = F2 // 256
    C2 = C1 + N_UP
    GAIN2 = [fl(BIG[:, 0:8, :]), T_[:, 2048:4096]]
    squared = sem("hidden_squared")
    scaled = sem("post_scaled")
    out_done = sem("out_done")
    gain2_loaded = sem("gain2_loaded")
    def post_square(act, q, used):
        act.wait_ge(item_used, used)
        for t in range(TT):
            if t:
                act.wait_ge(sq_done, 2 * q + 1)
            act.activation(T_[:, 0:D], PS[:, 4 * t:4 * t + 4, :].rearrange("p b n -> p (b n)"), ACT.Square,
                           accum_out=ST[:, t:t + 1]).then_inc(sq_done, 1)
        act.wait_ge(mean_done, q + 1)
        act.activation(ST[:, 4:6], ST[:, 2:4], ACT.Sqrt).then_inc(sd_done, 1)

    def post_scale(dve, n, gain):
        for t in range(TT):
            dve.scalar_tensor_tensor(out=T_[:, 0:D], in0=PS[:, 4 * t:4 * t + 4, :].rearrange("p b n -> p (b n)"),
                                     scalar=ST[:, 6 + t:7 + t], in1=gain, op0=ALU.mult, op1=ALU.mult)\
                .then_inc(scaled, 1)
            dve.wait_ge(scaled, 2 * n + t + 1)
            dve.tensor_tensor(X[:, t, :], X[:, t, :], T_[:, 0:D], ALU.add).then_inc(res_done, 1)
            dve.wait_ge(res_done, 6 + 2 * n + t + 1)

    with nc.Block() as block:
        @block.sync
        def _(sp):
            sp.dma_start(GAIN2[0], row_gain(A["g_mix_post_2"][0])).then_inc(gain_loaded, 16)
            n = load_rows(sp, C0, A["w_out_2"][0])
            load_cols(sp, n, [(A["w_up_2"][0], 0, N_UP)])
            n = load_rows(sp, n + N_UP, A["w_down_2"][0])
            for t in range(TT):
                sp.wait_ge(res_done, 8 + t + 1)
                sp.dma_start(out[0].rearrange("(t p) d -> p t d", p=P)[:, t, :], X[:, t, :]).then_inc(out_done, 16)
            sp.wait_ge(out_done, 32)

        @block.scalar
        def _(act):
            post_square(act, 4, C1)
            norm_act(act, 5, lambda e, t: e.wait_ge(res_done, 8))
            act.wait_ge(norm_out, 32)
            with act.Fori(0, N_UP // SLOTS) as r:
                for j in range(SLOTS):
                    act.wait_ge(item_used, C1 + SLOTS * r + j + 1)
                    act.wait_ge(squared, H0 + SLOTS * r + j - 1)
                    act.activation(ACTED[:, j % 2, :], PS[:, (N_IN + N_IN2 + j) % 4, :], ACT.Relu).then_inc(pair_out, 1)
            act.wait_ge(squared, H0 + N_UP)
            act.dma_start(GAIN2[1], row_gain(A["g_mlp_post_2"][0])).then_inc(gain2_loaded, 16)
            post_square(act, 6, C2 + N_UP)

        @block.vector
        def _(dve):
            for _ in range(H0):
                dve.engine_nop().then_inc(squared, 1)
            norm_dve(dve, 4, None)
            dve.wait_ge(gain_loaded, 32)
            post_scale(dve, 0, GAIN2[0])
            norm_dve(dve, 5, "g_mlp_pre_2")
            with dve.Fori(0, N_UP // SLOTS) as r:
                for j in range(SLOTS):
                    dve.wait_ge(pair_out, N_IN + N_IN2 + SLOTS * r + j + 1)
                    a = ACTED[:, j % 2, :].rearrange("p (c t) -> p c t", c=2)
                    dve.tensor_tensor(BIG[:, bass.ds(2 * SLOTS * r + 2 * j, 2), :], a, a, ALU.mult).then_inc(squared, 1)
            norm_dve(dve, 6, None)
            dve.wait_ge(gain2_loaded, 16)
            post_scale(dve, 1, GAIN2[1])

        @block.tensor
        def _(pe):
            pe_rows(pe, C0, N_OUT, NT)
            norm_pe(pe, 5)
            pe.wait_ge(norm_out, 32)
            pe_cols(pe, C1, N_IN + N_IN2, N_UP)
            pe.wait_ge(squared, H0 + N_UP)
            pe_rows(pe, C2, N_UP, BIG)
    return ctx


NAMES = ("x", "attn_norm", "w_in", "gdn_conv", "gdn_a_log", "gdn_dt_bias", "gdn_norm", "mlstm_conv", "mlstm_b_i",
         "mlstm_b_f", "mlstm_norm", "rglru_conv", "rglru_conv_b", "rglru_w_a", "rglru_b_a", "rglru_w_x", "rglru_b_x",
         "rglru_lambda", "rwkv_mu", "rwkv_w0", "rwkv_w2", "rwkv_a0", "rwkv_a2", "rwkv_g2", "rwkv_k_k", "rwkv_k_a",
         "rwkv_r_k", "rwkv_ln_w", "rwkv_ln_b", "w_out", "ffn_norm", "ffn_w_gate", "ffn_w_up", "ffn_w_down",
         "final_norm", "w_in_2", "w_out_2", "g_mix_pre_2", "g_mix_post_2", "g_mlp_pre_2", "g_mlp_post_2", "w_up_2",
         "w_down_2", "cmp_pe_2", "phik_w1_2", "phik_w2_2", "phiv_w1_2", "phiv_w2_2", "fox_bias_2", "rel_bias_2")


def kernel(**inputs):
    import concourse.bacc as bacc
    from concourse.bass_utils import run_bass_kernel_spmd

    nc = bacc.Bacc("TRN2", target_bir_lowering=False, num_devices=1)
    arrays = {name: np.ascontiguousarray(inputs[name]) for name in NAMES}
    arrays["const"] = CONST
    handles = {}
    for name, a in arrays.items():
        handles[name] = nc.dram_tensor(f"in_{name}", a.shape, mybir.dt.from_np(a.dtype), kind="ExternalInput").ap()
    out = nc.dram_tensor("out", (1, T, D), F32, kind="ExternalOutput").ap()
    build(nc, handles, out)
    r = run_bass_kernel_spmd(nc, [{f"in_{k}": v for k, v in arrays.items()}], core_ids=[0])
    return r.results[0]["out"]
```

```python
from contextlib import ExitStack

import numpy as np

import concourse.bass as bass
from concourse import mybir

F32 = mybir.dt.float32
F32R = mybir.dt.float32r
ALU = mybir.AluOpType
ACT = mybir.ActivationFunctionType
AX = mybir.AxisListType

P = 128
T = 256
TT = T // P
D = 2048
KD = D // P
W = 512
F1 = 5632
F2 = 8192
EPS = 1e-6
RAWS = 4
NEG = -1e30
HUGE8 = -8e30

GROUPS1 = ((0, 8), (2056, 8), (4112, 4), (5136, 7))
GATES1 = (2048, 4104)
GQ, GK, GV, GZ = 0, 4, 8, 12
MQ, MK, MV, MO = 16, 20, 24, 28
RX, RG = 32, 36
WR, WK, WV, WWA, WG = 40, 44, 48, 52, 53
GROUPS2 = ((0, 5), (1304, 6), (2840, 6), (4384, 6))
NSA_GATES, FOX_GATES = 1280, 4376
AQ, AKC, AVC, AKS, AVS, AKW, AVW = 0, 4, 5, 6, 7, 8, 9
BQ, BK, BV = 10, 14, 18
CQ, CK, CV_ = 22, 26, 30
DQ, DK, DV = 34, 38, 42

TABLE0 = (("attn_norm", 16), ("ffn_norm", 16), ("g_mix_pre_2", 16), ("g_mlp_pre_2", 16), ("cmp_pe_2", 16))
TABLE1 = (("gdn_conv", 48), ("mlstm_conv", 32), ("rglru_conv", 16))
TABLE2 = (("rglru_conv_b", 4), ("rglru_b_a", 4), ("rglru_b_x", 4), ("rglru_lambda", 4), ("rwkv_mu", 14),
          ("rwkv_w0", 4), ("rwkv_a0", 4), ("rwkv_k_k", 4), ("rwkv_k_a", 4), ("rwkv_r_k", 4),
          ("rwkv_ln_w", 4), ("rwkv_ln_b", 4), ("gdn_norm", 1), ("mlstm_norm", 4))
TABLES = (TABLE0, TABLE1, TABLE2)


def column_of():
    at, out = 0, {}
    for table in TABLES:
        for name, n in table:
            out[name] = at
            at += n
    return out, at


COL, NCOL = column_of()


def bucket(d):
    edges = (16, 23, 32, 46, 64, 91, 128, 182)
    return d if d < 16 else 15 + sum(d >= e for e in edges)


def constants():
    i = np.arange(P)
    row, col = i[:, None], i[None, :]
    out = {
        "ones": np.ones((P, T)),
        "ones64": (row // 64 == col // 64) * 1.0,
        "causal_T": np.where(row <= col, 0.0, NEG),
        "strict_T": (row < col) * 1.0,
        "strict64_T": (row < col) * (row // 64 == col // 64) * 1.0,
        "incl64_T": (row <= col) * (row // 64 == col // 64) * 1.0,
        "causal8": np.where(col <= row, 0.0, HUGE8),
    }
    for b in (1, 2, 4, 8, 16, 32, 64):
        out[f"level{b}"] = ((col // b) % 2 == 1) * (row // b == col // b - 1) * 1.0
    out["from31"] = (row >= 31) * 1.0
    t = np.arange(T)
    out["reset64"] = np.broadcast_to((t % 64 != 0) * 1.0, (P, T))
    out["reset128"] = np.broadcast_to((t % 128 != 0) * 1.0, (P, T))
    dist = 255 - np.arange(384)
    hot = np.zeros((P, 384))
    extra = np.zeros((P, 384))
    for n, d in enumerate(dist):
        hot[bucket(max(d, 0)), n] = 8.0
        count = int(d <= 128) + int(d % 4 == 0) + int(d % 16 == 0)
        extra[:16, n] = 0.0 if d >= 0 else HUGE8
        extra[16:24, n] = 8 * np.log(count) if d >= 0 and count else HUGE8
    first = np.concatenate([np.eye(P), hot, extra], axis=1).astype(np.float32)
    flat = {k: v.reshape(P, -1).astype(np.float32) for k, v in out.items()}
    where, at = {}, 0
    for k, v in flat.items():
        where[k] = (at, v.shape[1])
        at += v.shape[1]
    return np.ascontiguousarray(np.concatenate(list(flat.values()), axis=1)), where, first


CONST, CONST_AT, CONST_FIRST = constants()
NCONST = CONST.shape[1]


class Marks:

    def __init__(self, sem, order):
        self.sem, self.order, self.n = sem, list(order), 0
        assert len(set(self.order)) == len(self.order)

    def did(self, name, ins):
        assert self.order[self.n] == name, (self.order[self.n], name)
        self.n += 1
        ins.then_inc(self.sem, 1)

    def wait(self, eng, name):
        eng.wait_ge(self.sem, self.order.index(name) + 1)


def build(nc, A, out, stop=99):
    ctx = ExitStack()

    def sem(name):
        return ctx.enter_context(nc.semaphore(name))

    def at(name, shape, kib, dt=F32):
        return nc.alloc_sbuf_tensor_at(name, shape, dt, offset=SBUF0 + int(kib * 1024))

    SBUF0 = (nc.sbuf_base + 63) // 64 * 64
    slab = ctx.enter_context(nc.sbuf_tensor("slab", [P, 206 * 256], F32))
    del slab
    X = at("X", [P, TT, D], 0)
    BIG = at("BIG", [P, 64, T], 16)
    NT = at("NT", [P, KD, T], 80)
    CST = at("CST", [P, NCONST], 96)
    NTH = at("NTH", [P, KD, T], 80, F32R)
    NTL = at("NTL", [P, KD, T], 96, F32R)
    LJH = at("LJH", [P, 2, T], 96, F32R)
    LJL = at("LJL", [P, 2, T], 98, F32R)
    PAR = at("PAR", [P, NCOL], 112)
    IDENT_T = at("IDENT", [P, P], 113)
    ST = at("ST", [P, 16], 113.5)
    HC = at("HC", [8, 8], 113.625)
    GT = at("GT", [32, 4, T], 114)
    TMP = at("TMP", [P, TT, D], 118)
    RAW = at("RAW", [P, RAWS, 2048], 134)
    WH = at("WH", [P, 2, 2048], 166, F32R)
    WL = at("WL", [P, 2, 2048], 182, F32R)
    RING = at("RING", [P, 4, 4096], 134)
    PS = ctx.enter_context(nc.psum_tensor("PS", [P, 8, 512], F32))

    bias_rows = nc.dram_tensor("bias_rows", (24, 384), F32).ap()
    bias_skew = nc.dram_tensor("bias_skew", (24, P, 384), F32).ap()

    def cst(name, parts=P):
        at, n = CONST_AT[name]
        return CST[0:parts, at:at + n]

    IDENT = IDENT_T[:, :]
    UNIT, ONES64 = cst("ones"), cst("ones64")
    ONES = UNIT[:, 0:P]

    def pick(h, heads):
        return IDENT[0:heads, h:h + 1].broadcast_to([heads, P])

    def par(name, i=0, n=1):
        return PAR[:, COL[name] + i:COL[name] + i + n]

    def spread(columns, n):
        return columns.rearrange("p (k o) -> p k o", o=1).broadcast_to([P, columns.shape[1], n])

    def repeated(block, k):
        return block.rearrange("p (o n) -> p o n", o=1).broadcast_to([P, k, block.shape[1]])

    slot_full = [sem(f"slot_full{i}") for i in range(RAWS)]
    hi_made = sem("hi_made")
    lo_made = sem("lo_made")
    item_used = sem("item_used")
    pair_out = sem("pair_out")
    left_hi = sem("left_hi")
    left_lo = sem("left_lo")
    sq_done = sem("sq_done")
    mean_done = sem("mean_done")
    sd_done = sem("sd_done")
    rs_done = sem("rs_done")
    xn_done = sem("xn_done")
    turned = sem("turned")
    norm_gained = sem("norm_gained")
    norm_hi = sem("norm_hi")
    norm_out = sem("norm_out")

    def steps(eng, count, body, peel=0, lead=False):
        for j in range(peel):
            body(j, 0)
        count -= peel
        rounds = count // 4 - (1 if lead and count % 4 < 2 else 0)
        if rounds > 1:
            with eng.Fori(0, rounds) as r:
                for j in range(4):
                    body(peel + j, r)
        else:
            rounds = 0
        for j in range(4 * rounds, count):
            body(peel + j, 0)

    def half_columns(w):
        return w.rearrange("p (k n) -> p k n", k=8)

    def narrow(w):
        return w.rearrange("p (k n) -> p k n", k=KD)

    def load(sp, s, r, dst, src):
        if s >= RAWS:
            sp.wait_ge(lo_made, s + 4 * r - RAWS + 1)
        sp.dma_start(dst, src).then_inc(slot_full[s % RAWS], 16)

    def load_cols(sp, n0, w, c0, pairs):
        wv = w.rearrange("(k p) n -> p k n", p=P)

        def one(j, r):
            load(sp, n0 + j, r, half_columns(RAW[:, (n0 + j) % RAWS, :]),
                 wv[:, 8 * (j % 2):8 * (j % 2) + 8, bass.ds(c0 + (j // 2) * 256 + 512 * r, 256)])
        steps(sp, 2 * pairs, one, peel=4 if n0 < RAWS else 0)
        return n0 + 2 * pairs

    def load_gate_up(sp, n0, wa, wb, units):
        views = [w.rearrange("(k p) n -> p k n", p=P) for w in (wa, wb)]

        def one(j, r):
            load(sp, n0 + j, r, half_columns(RAW[:, (n0 + j) % RAWS, :]),
                 views[j % 4 // 2][:, 8 * (j % 2):8 * (j % 2) + 8, bass.ds((j // 4) * 256 + 256 * r, 256)])
        steps(sp, 4 * units, one)
        return n0 + 4 * units

    def load_rows(sp, n0, w):
        wv = w.rearrange("(g p) n -> g p n", p=P)
        count = w.shape[0] // P
        steps(sp, count, lambda j, r: load(sp, n0 + j, r, RAW[:, (n0 + j) % RAWS, :],
                                           wv[bass.ds(j + 4 * r, 1)].rearrange("o p n -> (o p) n")))
        return n0 + count

    def load_narrow(sp, n0, w, c0):
        load(sp, n0, 0, narrow(RAW[:, n0 % RAWS, :]), w.rearrange("(k p) n -> p k n", p=P)[:, :, c0:c0 + P])
        return n0 + 1

    def split_hi(act, s, r=0):
        act.wait_ge(slot_full[s % RAWS], 16 * (s // RAWS + 1 + r))
        if s >= 2:
            act.wait_ge(item_used, s + 4 * r - 1)
        act.activation(WH[:, s % 2, :], RAW[:, s % RAWS, :], ACT.Copy).then_inc(hi_made, 1)

    def split_lo(dve, s, r=0):
        dve.wait_ge(hi_made, s + 4 * r + 1)
        dve.tensor_tensor(WL[:, s % 2, :], RAW[:, s % RAWS, :], WH[:, s % 2, :].bitcast(F32), ALU.subtract)\
            .then_inc(lo_made, 1)

    def left_split_hi(act, n0, l0, j, r, src):
        if j >= 2:
            act.wait_ge(item_used, n0 + j + 4 * r - 1)
        act.activation(LJH[:, (l0 + j) % 2, :].rearrange("p (o t) -> p o t", o=1), src[:, bass.ds(j + 4 * r, 1), :],
                       ACT.Copy).then_inc(left_hi, 1)

    def left_split_lo(dve, l0, j, r, src):
        dve.wait_ge(left_hi, l0 + j + 4 * r + 1)
        slot = (l0 + j) % 2
        dve.tensor_tensor(LJL[:, slot, :].rearrange("p (o t) -> p o t", o=1), src[:, bass.ds(j + 4 * r, 1), :],
                          LJH[:, slot, :].bitcast(F32).rearrange("p (o t) -> p o t", o=1), ALU.subtract)\
            .then_inc(left_lo, 1)

    def pe_col_item(pe, s, r, half, bank):
        pe.wait_ge(lo_made, s + 4 * r + 1)
        wh, wl = half_columns(WH[:, s % 2, :]), half_columns(WL[:, s % 2, :])
        for c in range(2):
            cols = slice(c * P, (c + 1) * P)
            for kk in range(8):
                for n, (w, x) in enumerate(((wh, NTH), (wl, NTH), (wh, NTL))):
                    mm = nc.tensor.matmul(PS[:, bank + c, 0:T], w[:, kk, cols], x[:, 8 * half + kk, :],
                                          start=(half == 0 and kk == 0 and n == 0),
                                          stop=(half == 1 and kk == 7 and n == 2), skip_group_check=True)
        mm.then_inc(item_used, 1)

    def pe_cols(pe, n0, q0, pairs):
        def one(j, r):
            q = q0 + j // 2
            if j % 2 == 0 and q >= 2:
                pe.wait_ge(pair_out, q - 1 + 2 * r)
            pe_col_item(pe, n0 + j, r, j % 2, 2 * (q % 2))
        steps(pe, 2 * pairs, one, peel=4 if q0 < 2 else 0)

    def pe_narrow(pe, s, bank):
        pe.wait_ge(lo_made, s + 1)
        wh, wl = narrow(WH[:, s % 2, :]), narrow(WL[:, s % 2, :])
        for k in range(KD):
            for n, (w, x) in enumerate(((wh, NTH), (wl, NTH), (wh, NTL))):
                mm = nc.tensor.matmul(PS[:, bank, 0:T], w[:, k, :], x[:, k, :],
                                      start=(k == 0 and n == 0), stop=(k == KD - 1 and n == 2))
        mm.then_inc(item_used, 1)

    def act_cols(act, n0, q0, pairs, tile0, end):
        def one(j, r):
            if n0 + j + 2 < end:
                split_hi(act, n0 + j + 2, r)
            if j % 2 == 1:
                q = q0 + j // 2
                act.wait_ge(item_used, n0 + j + 4 * r + 1)
                act.activation(BIG[:, bass.ds(tile0 + j - 1 + 4 * r, 2), :], PS[:, 2 * (q % 2):2 * (q % 2) + 2, 0:T],
                               ACT.Copy).then_inc(pair_out, 1)
        steps(act, 2 * pairs, one, lead=(n0 + 2 * pairs + 2 > end))

    def dve_ahead(dve, n0, count, end):
        def one(j, r):
            if n0 + j + 2 < end:
                split_lo(dve, n0 + j + 2, r)
        steps(dve, count, one, lead=(n0 + count + 2 > end))

    def pe_rows(pe, n0, l0, count):
        def one(j, r):
            s = n0 + j
            pe.wait_ge(lo_made, s + 4 * r + 1)
            pe.wait_ge(left_lo, l0 + j + 4 * r + 1)
            sl, sw = (l0 + j) % 2, s % 2
            start = isinstance(r, int) and j == 0
            stop = isinstance(r, int) and j == count - 1
            for t in range(TT):
                tok = slice(t * P, (t + 1) * P)
                for n, (x, w) in enumerate(((LJH, WH), (LJH, WL), (LJL, WH))):
                    for c in range(4):
                        mm = nc.tensor.matmul(PS[:, 4 * t + c, :], x[:, sl, tok], w[:, sw, c * 512:(c + 1) * 512],
                                              start=(start and n == 0), stop=(stop and n == 2),
                                              skip_group_check=True)
            mm.then_inc(item_used, 1)
        steps(pe, count, one, peel=4, lead=True)

    def act_rows(act, n0, l0, count, src, end):
        for j in range(2):
            left_split_hi(act, n0, l0, j, 0, src)

        def one(j, r):
            if n0 + j + 2 < end:
                split_hi(act, n0 + j + 2, r)
            if j + 2 < count:
                left_split_hi(act, n0, l0, j + 2, r, src)
        steps(act, count, one, lead=True)

    def dve_rows(dve, n0, l0, count, src, end):
        for j in range(2):
            left_split_lo(dve, l0, j, 0, src)

        def one(j, r):
            if n0 + j + 2 < end:
                split_lo(dve, n0 + j + 2, r)
            if j + 2 < count:
                left_split_lo(dve, l0, j + 2, r, src)
        steps(dve, count, one, lead=True)

    NF = BIG[:, 0:KD, :]

    def chunk_of(x, i):
        return x[:, 4 * (i // 2):4 * (i // 2) + 4, (i % 2) * P:(i % 2 + 1) * P]

    def norm_act(act, q, ready):
        for t in range(TT):
            ready(act, t)
            act.activation(TMP[:, t, :], X[:, t, :], ACT.Square, accum_out=ST[:, t:t + 1]).then_inc(sq_done, 1)
        act.wait_ge(mean_done, q + 1)
        act.activation(ST[:, 4:6], ST[:, 2:4], ACT.Sqrt).then_inc(sd_done, 1)

    def norm_act_hi(act, q):
        n = q_turn[q]
        for i in range(8):
            act.wait_ge(norm_gained, 8 * n + i + 1)
            act.activation(chunk_of(NTH, i), chunk_of(NF, i), ACT.Copy).then_inc(norm_hi, 1)

    def norm_dve(dve, q, gain):
        dve.wait_ge(sq_done, 2 * q + 2)
        dve.tensor_scalar(ST[:, 2:4], ST[:, 0:2], 1.0 / D, EPS, ALU.mult, ALU.add).then_inc(mean_done, 1)
        dve.wait_ge(sd_done, q + 1)
        dve.reciprocal(ST[:, 6:8], ST[:, 4:6]).then_inc(rs_done, 1)
        dve.wait_ge(rs_done, q + 1)
        if gain is None:
            return
        for t in range(TT):
            dve.tensor_scalar(TMP[:, t, :], X[:, t, :], ST[:, 6 + t:7 + t], None, ALU.mult).then_inc(xn_done, 1)
        n = q_turn[q]

        def low(i):
            dve.wait_ge(norm_hi, 8 * n + i + 1)
            dve.tensor_tensor(chunk_of(NTL, i), chunk_of(NF, i), chunk_of(NTH[:, :, :].bitcast(F32), i), ALU.subtract)\
                .then_inc(norm_out, 1)
        for i in range(8):
            dve.wait_ge(turned, 8 * n + i + 1)
            dve.tensor_tensor(chunk_of(NF, i), PS[:, i, :].rearrange("p (k t) -> p k t", k=4),
                              spread(par(gain, 4 * (i // 2), 4), P), ALU.mult).then_inc(norm_gained, 1)
            if i:
                low(i - 1)
        low(7)

    def norm_pe(pe, q):
        n = q_turn[q]
        pe.wait_ge(xn_done, 2 * n + 2)
        for i in range(8):
            t, b = i % 2, i // 2
            for k in range(4):
                mm = nc.tensor.transpose(PS[:, i, k * P:(k + 1) * P],
                                         TMP[:, t, (4 * b + k) * P:(4 * b + k + 1) * P], IDENT)
            mm.then_inc(turned, 1)

    q_turn = {0: 0, 1: 1, 3: 2, 5: 3}

    in_loaded = sem("in_loaded")
    par_loaded = sem("par_loaded")
    ident_made = sem("ident_made")
    par_turned = sem("par_turned")
    par_out = sem("par_out")
    bias_made = sem("bias_made")
    bias_out = sem("bias_out")
    bias_moved = sem("bias_moved")
    gates_out = sem("gates_out")
    gates_moved = sem("gates_moved")

    w_in = A["w_in"][0]
    NI = 2 * sum(n for _, n in GROUPS1)
    IA = NI + 2
    flat2 = lambda v: v.rearrange("p a b -> p (a b)")
    PROWS = [BIG[:, 16 + i, 0:P] for i in range(3)]
    FIRSTC = flat2(BIG[:, 20:24, :])[:, 0:P + 768]
    HOT8, EXTRA8 = FIRSTC[0:32, P:P + 384], FIRSTC[0:24, P + 384:P + 768]
    BIASR = flat2(BIG[:, 24:26, :])[0:24, 0:384]
    RB = BIG[0:32, 26, 0:24]

    with nc.Block() as block:
        @block.sync
        def _(sp):
            sp.dma_start(FIRSTC, A["const_first"]).then_inc(in_loaded, 16)
            sp.dma_start(X[:, :, :], A["x"][0].rearrange("(t p) d -> p t d", p=P)).then_inc(in_loaded, 16)
            n = 0
            for c, pairs in GROUPS1:
                n = load_cols(sp, n, w_in, c, pairs)
            for c in GATES1:
                n = load_narrow(sp, n, w_in, c)
            sp.wait_ge(gates_out, 1)
            for m in range(2):
                sp.dma_start(GT[0:4, 2 + m, :], GT[4:8, m, :]).then_inc(gates_moved, 16)
            sp.wait_ge(gates_moved, 32)

        @block.scalar
        def _(act):
            for b, table in enumerate(TABLES):
                at = 0
                for name, n in table:
                    src = A[name]
                    letters = " ".join("abcd"[:len(src.shape)])
                    flat = src.rearrange(f"{letters} -> ({letters})")
                    act.dma_start(PROWS[b][at:at + n, :], flat.rearrange("(r c) -> r c", c=P))\
                        .then_inc(par_loaded, 16)
                    at += n
            act.dma_start(RB, A["rel_bias_2"]).then_inc(par_loaded, 16)
            for n, name in enumerate(("gdn_a_log", "gdn_dt_bias", "mlstm_b_i", "mlstm_b_f")):
                act.dma_start(HC[0:4, n:n + 1], A[name][0].rearrange("(h o) -> h o", o=1)).then_inc(par_loaded, 16)
            act.dma_start(HC[0:8, 4:5], A["fox_bias_2"][0].rearrange("(h o) -> h o", o=1)).then_inc(par_loaded, 16)
            norm_act(act, 0, lambda e, t: e.wait_ge(in_loaded, 32))
            norm_act_hi(act, 0)
            split_hi(act, 0)
            split_hi(act, 1)
            act.wait_ge(bias_out, 1)
            act.dma_start(bias_rows, BIASR).then_inc(bias_moved, 16)
            act.wait_ge(bias_moved, 16)
            act.dma_start(bias_skew, bias_rows.rearrange("h (o i) -> h o i", o=1).broadcast_to([24, P, 384]))\
                .then_inc(bias_moved, 16)
            act.wait_ge(norm_out, 8)
            at, n = 0, 0
            for _, pairs in GROUPS1:
                act_cols(act, n, n // 2, pairs, at, IA)
                n, at = n + 2 * pairs, at + 2 * pairs
            act.wait_ge(item_used, IA)
            act.activation(GT[0:8, 0:2, :], PS[0:8, 6:8, 0:T], ACT.Copy).then_inc(gates_out, 1)
            act.wait_ge(bias_moved, 32)

        @block.vector
        def _(dve):
            dve.wait_ge(in_loaded, 32)
            dve.tensor_copy(IDENT, FIRSTC[:, 0:P]).then_inc(ident_made, 1)
            at = 0
            for b, table in enumerate(TABLES):
                n = sum(k for _, k in table)
                dve.wait_ge(par_turned, b + 1)
                dve.tensor_copy(PAR[:, at:at + n], PS[:, 4 + b, 0:n]).then_inc(par_out, 1)
                at += n
            dve.wait_ge(bias_made, 1)
            dve.tensor_tensor(BIASR, PS[0:24, 7, 0:384], EXTRA8, ALU.add).then_inc(bias_out, 1)
            dve.wait_ge(par_out, 3)
            norm_dve(dve, 0, "attn_norm")
            split_lo(dve, 0)
            split_lo(dve, 1)
            dve_ahead(dve, 0, NI, IA)

        @block.tensor
        def _(pe):
            pe.wait_ge(ident_made, 1)
            pe.wait_ge(par_loaded, 16 * (sum(len(t) for t in TABLES) + 6))
            for b, table in enumerate(TABLES):
                n = sum(k for _, k in table)
                nc.tensor.transpose(PS[:, 4 + b, 0:n], PROWS[b][0:n, :], IDENT[0:n, 0:n]).then_inc(par_turned, 1)
            nc.tensor.matmul(PS[0:24, 7, 0:384], RB, HOT8, start=True, stop=True).then_inc(bias_made, 1)
            pe.wait_ge(par_out, 3)
            pe.wait_ge(bias_out, 1)
            norm_pe(pe, 0)
            pe.wait_ge(norm_out, 8)
            n = 0
            for _, pairs in GROUPS1:
                pe_cols(pe, n, n // 2, pairs)
                n += 2 * pairs
            for m in range(2):
                pe_narrow(pe, NI + m, 6 + m)
    if stop == 0:
        return ctx

    R_ = RING[:, :, :].rearrange("p s n -> p (s n)")
    T_ = TMP[:, :, :].rearrange("p t n -> p (t n)")

    def area(base, at, k, n=P):
        return base[:, at:at + k * n].rearrange("p (k n) -> p k n", k=k)

    CV = area(R_, 0, 24, T)
    CONVS = ([("gdn_conv", 12, j, GQ + j) for j in range(12)] + [("mlstm_conv", 8, j, MQ + j) for j in range(8)]
             + [("rglru_conv", 4, j, RX + j) for j in range(4)])
    SPARE = BIG[:, 54:64, :]
    ROW = lambda n: SPARE[0:4, n, :]
    O8 = BIG[:, 16:24, :]

    conv_lead = sem("conv_lead")
    conv_tap = sem("conv_tap")
    conv_silu = sem("conv_silu")
    NCV = len(CONVS)
    const_loaded = sem("const_loaded")
    with nc.Block() as block:
        @block.sync
        def _(sp):
            sp.dma_start(CST[:, :], A["const"]).then_inc(const_loaded, 16)
            sp.wait_ge(const_loaded, 16)

        @block.scalar
        def _(act):
            for i, (name, n, j, u) in enumerate(CONVS):
                w = par(name, 3 * n + j)
                if name == "rglru_conv":
                    act.activation(CV[:, i, :], BIG[:, u, :], ACT.Identity, bias=par("rglru_conv_b", j), scale=w)\
                        .then_inc(conv_lead, 1)
                else:
                    act.activation(CV[:, i, :], BIG[:, u, :], ACT.Copy, scale=w).then_inc(conv_lead, 1)
            for g in range(5):
                act.wait_ge(conv_tap, 2 * NCV + 4 * g + 4)
                act.activation(CV[:, 4 * g:4 * g + 4, :], CV[:, 4 * g:4 * g + 4, :], ACT.Silu).then_inc(conv_silu, 1)

        @block.vector
        def _(dve):
            for step, tap in enumerate((2, 1, 0)):
                for i, (name, n, j, u) in enumerate(CONVS):
                    s = 3 - tap
                    if step == 0:
                        dve.wait_ge(conv_lead, i + 1)
                    else:
                        dve.wait_ge(conv_tap, (step - 1) * NCV + i + 1)
                    dve.scalar_tensor_tensor(out=CV[:, i, s:T], in0=BIG[:, u, 0:T - s], scalar=par(name, tap * n + j),
                                             in1=CV[:, i, s:T], op0=ALU.mult, op1=ALU.add).then_inc(conv_tap, 1)

    def marks(name, order):
        return Marks(sem(name), order)

    def m3(at, k=8):
        return area(R_, 6144 + at * 1024, k)
    EGB, DT_, AT_, LT_, QD, KDT, XI, XT, CT, CX = [m3(i) for i in range(10)]
    EGB, QD, KDT = [v.rearrange("p m t -> p (m t)").rearrange("p (h t) -> p h t", h=4) for v in (EGB, QD, KDT)]
    fl = lambda v: v.rearrange("p a b -> p (a b)")
    VB, KN, VNEW = [fl(BIG[:, 4 * i:4 * i + 4, :]).rearrange("p (m t) -> p m t", m=8) for i in range(3)]
    SQ8, T18 = [area(T_, 2048 * i, 8, T) for i in range(2)]
    RR, SS = [area(T_, 512 * i, 4) for i in range(2)]
    COLS = SPARE[:, 9, 0:16]
    SM = SPARE[:, 9, 16:32]
    NB = SPARE[:, 9, 32:40]
    LEVELS = (1, 2, 4, 8, 16, 32, 64)

    def ps_m(bank, nb=2):
        return PS[:, bank:bank + nb, :].rearrange("p b (m t) -> p (b m) t", t=P)

    def ps_t(bank, nb=2):
        return PS[:, bank:bank + nb, :].rearrange("p b (m t) -> p (b m) t", t=T)

    gp = marks("gdn_products", ["ssq", "cols", "rows", "kkqk", "v_nat", "k_nat", "cx0"]
               + [f"{s}{l}" for l in range(1, 7) for s in ("cx", "y")] + ["vn0", "o0", "ks", "vn1", "o1"])
    ga = marks("gdn_scalar", ["beta", "ealog", "ex1", "ln", "sd", "egb", "dt", "kd"] + [f"cxs{l}" for l in range(1, 7)]
               + ["vn0s", "s", "o0s", "vn1s", "o1s"])
    gv = marks("gdn_vector", ["sq", "xg", "ax", "e1", "sp", "g", "scan", "t1", "rn", "qk_norm", "cols_out", "nb", "dt",
                              "gl", "dl", "at", "lt1", "lt2", "lt", "ct0", "vb", "qd", "kdt", "kn"]
               + ["x0", "ct1"] + [s for l in range(1, 6) for s in (f"x{l}", f"ct{l + 1}")] + ["x6", "r1"])
    with nc.Block() as block:
        @block.scalar
        def _(act):
            ga.did("beta", act.activation(ROW(0), GT[0:4, 2, :], ACT.Sigmoid))
            ga.did("ealog", act.activation(HC[0:4, 5:6], HC[0:4, 0:1], ACT.Exp))
            gv.wait(act, "ax")
            ga.did("ex1", act.activation(ROW(2), ROW(2), ACT.Exp, scale=-1.0))
            gv.wait(act, "e1")
            ga.did("ln", act.activation(ROW(2), ROW(2), ACT.Ln))
            gv.wait(act, "t1")
            ga.did("sd", act.activation(T18, T18, ACT.Sqrt))
            gv.wait(act, "gl")
            ga.did("egb", act.activation(EGB, ps_t(4), ACT.Exp))
            gv.wait(act, "dt")
            ga.did("dt", act.activation(DT_, DT_, ACT.Exp))
            gv.wait(act, "dl")
            ga.did("kd", act.activation(SM, SM, ACT.Exp))
            for l in range(1, 7):
                gp.wait(act, f"cx{l}")
                ga.did(f"cxs{l}", act.activation(CX, ps_m(0), ACT.Copy))
            gp.wait(act, "vn0")
            ga.did("vn0s", act.activation(VNEW[:, 0:4, :], ps_m(6, 1), ACT.Copy))
            gp.wait(act, "o0")
            ga.did("s", act.activation(SS, ps_m(0, 1), ACT.Copy))
            ga.did("o0s", act.activation(O8[:, 0:4, 0:P], ps_m(7, 1), ACT.Copy))
            gp.wait(act, "vn1")
            ga.did("vn1s", act.activation(VNEW[:, 4:8, :], ps_m(6, 1), ACT.Copy))
            gp.wait(act, "o1")
            ga.did("o1s", act.activation(O8[:, 0:4, P:T], ps_m(2, 1), ACT.Copy))

        @block.vector
        def _(dve):
            dve.wait_ge(conv_silu, 5)
            gv.did("sq", dve.tensor_tensor(SQ8, CV[:, 0:8, :], CV[:, 0:8, :], ALU.mult))
            gv.did("xg", dve.tensor_scalar(ROW(1), GT[0:4, 0, :], HC[0:4, 1:2], None, ALU.add))
            gv.wait(dve, "xg")
            gv.did("ax", dve.scalar_tensor_tensor(out=ROW(2), in0=ROW(1), scalar=-1.0, in1=ROW(1), op0=ALU.mult, op1=ALU.max))
            ga.wait(dve, "ex1")
            gv.did("e1", dve.tensor_scalar(ROW(2), ROW(2), 1.0, None, ALU.add))
            ga.wait(dve, "ln")
            gv.did("sp", dve.scalar_tensor_tensor(out=ROW(3), in0=ROW(1), scalar=0.0, in1=ROW(2),
                                                  op0=ALU.max, op1=ALU.add))
            gv.wait(dve, "sp")
            gv.did("g", dve.tensor_scalar(ROW(4), ROW(3), HC[0:4, 5:6], -1.0, ALU.mult, ALU.mult))
            gv.wait(dve, "g")
            gv.did("scan", dve.tensor_tensor_scan(ROW(5), cst("reset128", 4), ROW(4), 0.0, ALU.mult, ALU.add))
            gp.wait(dve, "ssq")
            gv.did("t1", dve.tensor_scalar(T18, ps_t(0, 4), EPS, None, ALU.add))
            ga.wait(dve, "sd")
            gv.did("rn", dve.reciprocal(T18, T18))
            gv.wait(dve, "rn")
            dve.scalar_tensor_tensor(out=fl(CV[:, 0:4, :]), in0=fl(CV[:, 0:4, :]), scalar=float(P) ** -0.5,
                                     in1=fl(T18[:, 0:4, :]), op0=ALU.mult, op1=ALU.mult)
            gv.did("qk_norm", dve.tensor_tensor(CV[:, 4:8, :], CV[:, 4:8, :], T18[:, 4:8, :], ALU.mult))
            gp.wait(dve, "cols")
            gv.did("cols_out", dve.tensor_copy(COLS, PS[:, 6, 0:16]))
            gv.wait(dve, "cols_out")
            gv.did("nb", dve.tensor_scalar(NB, COLS[:, 8:16], -1.0, None, ALU.mult))
            gp.wait(dve, "rows")
            for m in range(8):
                c, h = m // 4, m % 4
                last = dve.scalar_tensor_tensor(out=DT_[:, m, :], in0=ps_t(4)[:, h, c * P:(c + 1) * P],
                                                scalar=COLS[:, m:m + 1], in1=cst("causal_T"),
                                                op0=ALU.subtract, op1=ALU.add)
            gv.did("dt", last)
            ends = ps_t(4).rearrange("p h (c t) -> p c h t", c=2)[:, :, :, P - 1]
            gv.did("gl", dve.tensor_copy(SM[:, 8:16].rearrange("p (c h) -> p c h", c=2), ends))
            gv.wait(dve, "gl")
            gv.did("dl", dve.tensor_tensor(SM[:, 0:8], SM[:, 8:16], COLS[:, 0:8], ALU.subtract))
            gp.wait(dve, "kkqk")
            ga.wait(dve, "dt")
            gv.did("at", dve.tensor_tensor(AT_, ps_m(2), DT_, ALU.mult))
            gv.did("lt1", dve.tensor_tensor(LT_, ps_m(0), DT_, ALU.mult))
            gv.wait(dve, "lt1")
            gv.did("lt2", dve.tensor_tensor(LT_, LT_, repeated(cst("strict_T"), 8), ALU.mult))
            gv.wait(dve, "lt2")
            for c in range(2):
                last = dve.tensor_tensor(LT_[:, 4 * c:4 * c + 4, :], LT_[:, 4 * c:4 * c + 4, :],
                                         ps_t(6)[:, :, c * P:(c + 1) * P], ALU.mult)
            gv.did("lt", last)
            gv.wait(dve, "lt")
            gv.did("ct0", dve.tensor_tensor(CT, LT_, repeated(cst("level1"), 8), ALU.mult))
            gp.wait(dve, "v_nat")
            gv.did("vb", dve.tensor_tensor(VB, ps_m(6), spread(COLS[:, 8:16], P), ALU.mult))
            ga.wait(dve, "egb")
            gv.did("qd", dve.tensor_tensor(QD, CV[:, 0:4, :], EGB, ALU.mult))
            gv.did("kdt", dve.tensor_tensor(KDT, CV[:, 4:8, :], EGB, ALU.mult))
            gp.wait(dve, "k_nat")
            ga.wait(dve, "kd")
            gv.did("kn", dve.tensor_tensor(KN, ps_m(4), spread(SM[:, 0:8], P), ALU.mult))
            gp.wait(dve, "cx0")
            dve.tensor_tensor(XI, repeated(IDENT, 8), ps_m(0), ALU.subtract)
            gv.did("x0", dve.tensor_tensor(XT, repeated(IDENT, 8), CT, ALU.subtract))
            gv.wait(dve, "x0")
            gv.did("ct1", dve.tensor_tensor(CT, LT_, repeated(cst("level2"), 8), ALU.mult))
            for l in range(1, 7):
                gp.wait(dve, f"y{l}")
                if l < 6:
                    dve.tensor_tensor(XI, XI, ps_m(2), ALU.subtract)
                gv.did(f"x{l}", dve.tensor_tensor(XT, XT, ps_m(4), ALU.subtract))
                if l < 6:
                    gv.did(f"ct{l + 1}", dve.tensor_tensor(CT, LT_, repeated(cst(f"level{LEVELS[l + 1]}"), 8), ALU.mult))
            gp.wait(dve, "ks")
            for h in range(4):
                last = dve.scalar_tensor_tensor(out=RR[:, h, :], in0=ps_m(1, 1)[:, h, :], scalar=NB[:, 4 + h:5 + h],
                                                in1=VB[:, 4 + h, :], op0=ALU.mult, op1=ALU.add)
            gv.did("r1", last)

        @block.tensor
        def _(pe):
            mmul = nc.tensor.matmul

            def each(dst, lhs, rhs, ms):
                for n, m in enumerate(ms):
                    last = mmul(dst[:, n, :], lhs(m), rhs(m), start=True, stop=True)
                return last

            def turn(dst, src, ms):
                for n, m in enumerate(ms):
                    last = nc.tensor.transpose(dst[:, n, :], src(m), IDENT)
                return last

            chunk = lambda base, m: CV[:, base + m % 4, (m // 4) * P:(m // 4 + 1) * P]
            gv.wait(pe, "sq")
            for b in range(4):
                last = mmul(PS[:, b, :], ONES, fl(SQ8[:, 2 * b:2 * b + 2, :]), start=True, stop=True)
            gp.did("ssq", last)
            gv.wait(pe, "scan")
            ga.wait(pe, "beta")
            for n, row in enumerate((ROW(5), ROW(0))):
                for c in range(2):
                    last = nc.tensor.transpose(PS[:, 6, 8 * n + 4 * c:8 * n + 4 * c + 4], row[:, c * P:(c + 1) * P],
                                               IDENT[0:4, 0:4])
            gp.did("cols", last)
            gv.wait(pe, "cols_out")
            for n, row in enumerate((ROW(5), ROW(0))):
                for h in range(4):
                    last = mmul(ps_t(4 + 2 * n)[:, h, :], pick(h, 4), row, start=True, stop=True)
            gp.did("rows", last)
            gv.wait(pe, "qk_norm")
            each(ps_m(0), lambda m: chunk(4, m), lambda m: chunk(4, m), range(8))
            gp.did("kkqk", each(ps_m(2), lambda m: chunk(4, m), lambda m: chunk(0, m), range(8)))
            gv.wait(pe, "lt")
            gp.did("v_nat", turn(ps_m(6), lambda m: chunk(8, m), range(8)))
            ga.wait(pe, "egb")
            gp.did("k_nat", turn(ps_m(4), lambda m: chunk(4, m), range(8)))
            gv.wait(pe, "ct0")
            gp.did("cx0", turn(ps_m(0), lambda m: CT[:, m, :], range(8)))
            for l in range(1, 7):
                gv.wait(pe, f"ct{l}")
                gp.did(f"cx{l}", each(ps_m(0), lambda m: CT[:, m, :], lambda m: XI[:, m, :], range(8)))
                ga.wait(pe, f"cxs{l}")
                if l < 6:
                    each(ps_m(2), lambda m: XT[:, m, :], lambda m: CX[:, m, :], range(8))
                gv.wait(pe, "kn")
                gp.did(f"y{l}", each(ps_m(4), lambda m: CX[:, m, :], lambda m: XT[:, m, :], range(8)))
            gv.wait(pe, "x6")
            gp.did("vn0", each(ps_m(6, 1), lambda m: XT[:, m, :], lambda m: VB[:, m, :], range(4)))
            ga.wait(pe, "vn0s")
            each(ps_m(7, 1), lambda m: VNEW[:, m, :], lambda m: AT_[:, m, :], range(4))
            gp.did("o0", each(ps_m(0, 1), lambda m: KN[:, m, :], lambda m: VNEW[:, m, :], range(4)))
            ga.wait(pe, "s")
            gp.did("ks", each(ps_m(1, 1), lambda m: KDT[:, m, P:T], lambda m: SS[:, m, :], range(4)))
            gv.wait(pe, "r1")
            gp.did("vn1", each(ps_m(6, 1), lambda m: XT[:, 4 + m, :], lambda m: RR[:, m, :], range(4)))
            ga.wait(pe, "vn1s")
            for h in range(4):
                mmul(ps_m(2, 1)[:, h, :], SS[:, h, :], QD[:, h, P:T], start=True, stop=False)
                last = mmul(ps_m(2, 1)[:, h, :], VNEW[:, 4 + h, :], AT_[:, 4 + h, :], start=False, stop=True)
            gp.did("o1", last)
    if stop == 1:
        return ctx

    lp = marks("mlstm_products", ["cols", "rows", "kq", "v_nat", "den_num"])
    la = marks("mlstm_scalar", ["sig", "ex1", "ln", "em", "exp", "ad"])
    lv = marks("mlstm_vector", ["i", "xf", "ax", "e1", "lf", "scan", "c", "m", "nm", "bm", "cols_out", "e", "p", "vn",
                                "md", "rd", "h", "o"])
    EE = area(R_, 6144, 4, 384)
    PP = area(R_, 6144 + 1536, 4, 384)
    DD = area(R_, 6144 + 3072, 4, T)
    SIG = area(R_, 6144 + 4096, 4, T)
    VNM = area(R_, 6144 + 5120, 8)
    with nc.Block() as block:
        @block.scalar
        def _(act):
            la.did("sig", act.activation(SIG, BIG[:, MO:MO + 4, :], ACT.Sigmoid))
            lv.wait(act, "ax")
            la.did("ex1", act.activation(ROW(2), ROW(2), ACT.Exp, scale=-1.0))
            lv.wait(act, "e1")
            la.did("ln", act.activation(ROW(2), ROW(2), ACT.Ln))
            lv.wait(act, "bm")
            la.did("em", act.activation(ROW(7), ROW(7), ACT.Exp, scale=-1.0))
            lv.wait(act, "e")
            la.did("exp", act.activation(EE, EE, ACT.Exp))
            lp.wait(act, "den_num")
            la.did("ad", act.activation(DD, ps_t(0), ACT.Abs))

        @block.vector
        def _(dve):
            lv.did("i", dve.tensor_scalar(ROW(0), GT[0:4, 1, :], HC[0:4, 2:3], None, ALU.add))
            lv.did("xf", dve.tensor_scalar(ROW(1), GT[0:4, 3, :], HC[0:4, 3:4], None, ALU.add))
            lv.wait(dve, "xf")
            lv.did("ax", dve.scalar_tensor_tensor(out=ROW(2), in0=ROW(1), scalar=-1.0, in1=ROW(1), op0=ALU.mult, op1=ALU.max))
            la.wait(dve, "ex1")
            lv.did("e1", dve.tensor_scalar(ROW(2), ROW(2), 1.0, None, ALU.add))
            la.wait(dve, "ln")
            lv.did("lf", dve.scalar_tensor_tensor(out=ROW(3), in0=ROW(1), scalar=0.0, in1=ROW(2),
                                                  op0=ALU.min, op1=ALU.subtract))
            lv.wait(dve, "lf")
            lv.did("scan", dve.tensor_tensor_scan(ROW(4), UNIT[0:4, :], ROW(3), 0.0, ALU.mult, ALU.add))
            lv.wait(dve, "scan")
            lv.did("c", dve.tensor_tensor(ROW(5), ROW(0), ROW(4), ALU.subtract))
            lv.wait(dve, "c")
            lv.did("m", dve.tensor_tensor_scan(ROW(6), ROW(5), ROW(5), 0.0, ALU.max, ALU.max))
            lv.wait(dve, "m")
            lv.did("nm", dve.tensor_scalar(ROW(8), ROW(6), -1.0, None, ALU.mult))
            lv.did("bm", dve.tensor_tensor(ROW(7), ROW(4), ROW(6), ALU.add))
            lp.wait(dve, "cols")
            lv.did("cols_out", dve.tensor_copy(COLS[:, 0:8], PS[:, 0, 0:8]))
            lv.wait(dve, "cols_out")
            lp.wait(dve, "rows")
            for h in range(4):
                nm = ps_t(4)[:, h, :]
                dve.scalar_tensor_tensor(out=EE[:, h, 0:P], in0=nm[:, 0:P], scalar=COLS[:, h:h + 1],
                                         in1=cst("causal_T"), op0=ALU.add, op1=ALU.add)
                dve.tensor_scalar(EE[:, h, P:T], nm[:, P:T], COLS[:, h:h + 1], None, ALU.add)
                last = dve.scalar_tensor_tensor(out=EE[:, h, T:384], in0=nm[:, P:T], scalar=COLS[:, 4 + h:5 + h],
                                                in1=cst("causal_T"), op0=ALU.add, op1=ALU.add)
            lv.did("e", last)
            lp.wait(dve, "kq")
            la.wait(dve, "exp")
            lv.did("p", dve.scalar_tensor_tensor(out=PP, in0=PS[:, 0:4, 0:384], scalar=float(P) ** -0.5, in1=EE,
                                                 op0=ALU.mult, op1=ALU.mult))
            lp.wait(dve, "v_nat")
            lv.did("vn", dve.tensor_copy(VNM, ps_m(4)))
            lp.wait(dve, "den_num")
            la.wait(dve, "ad")
            lv.did("md", dve.tensor_tensor(DD, DD, ps_t(6), ALU.max))
            lv.wait(dve, "md")
            lv.did("rd", dve.reciprocal(DD, DD))
            lv.wait(dve, "rd")
            lv.did("h", dve.tensor_tensor(DD, DD, ps_t(2), ALU.mult))
            lv.wait(dve, "h")
            la.wait(dve, "sig")
            lv.did("o", dve.tensor_tensor(O8[:, 4:8, :], DD, SIG, ALU.mult))

        @block.tensor
        def _(pe):
            mmul = nc.tensor.matmul
            lv.wait(pe, "c")
            for c in range(2):
                last = nc.tensor.transpose(PS[:, 0, 4 * c:4 * c + 4], ROW(5)[:, c * P:(c + 1) * P], IDENT[0:4, 0:4])
            lp.did("cols", last)
            lv.wait(pe, "nm")
            la.wait(pe, "em")
            for n, row in enumerate((ROW(8), ROW(7))):
                for h in range(4):
                    last = mmul(ps_t(4 + 2 * n)[:, h, :], pick(h, 4), row, start=True, stop=True)
            lp.did("rows", last)
            lv.wait(pe, "cols_out")
            for h in range(4):
                q, k = CV[:, 12 + h, :], CV[:, 16 + h, :]
                mmul(PS[:, h, 0:T], k[:, 0:P], q, start=True, stop=True)
                last = mmul(PS[:, h, T:384], k[:, P:T], q[:, P:T], start=True, stop=True)
            lp.did("kq", last)
            lv.wait(pe, "e")
            for c in range(2):
                for h in range(4):
                    last = nc.tensor.transpose(ps_m(4)[:, 4 * c + h, :], BIG[:, MV + h, c * P:(c + 1) * P], IDENT)
            lp.did("v_nat", last)
            lv.wait(pe, "vn")
            for h in range(4):
                for bank, lhs in ((0, [ONES, ONES]), (2, [VNM[:, h, :], VNM[:, 4 + h, :]])):
                    dst = ps_t(bank)[:, h, :]
                    mmul(dst, lhs[0], PP[:, h, 0:T], start=True, stop=False)
                    last = mmul(dst[:, P:T], lhs[1], PP[:, h, T:384], start=False, stop=True)
            lp.did("den_num", last)
    if stop == 2:
        return ctx

    hp = marks("headnorm_products", ["ssq"])
    ha = marks("headnorm_scalar", ["silu", "sd"])
    hv = marks("headnorm_vector", ["sq", "ms", "rs", "scaled", "gated"])
    GATE = area(R_, 6144, 4, T)
    with nc.Block() as block:
        @block.scalar
        def _(act):
            ha.did("silu", act.activation(GATE, BIG[:, GZ:GZ + 4, :], ACT.Silu))
            hv.wait(act, "ms")
            ha.did("sd", act.activation(T18, T18, ACT.Sqrt))

        @block.vector
        def _(dve):
            hv.did("sq", dve.tensor_tensor(SQ8, O8, O8, ALU.mult))
            hp.wait(dve, "ssq")
            hv.did("ms", dve.tensor_scalar(T18, ps_t(0, 4), 1.0 / P, EPS, ALU.mult, ALU.add))
            ha.wait(dve, "sd")
            hv.did("rs", dve.reciprocal(T18, T18))
            hv.wait(dve, "rs")
            for i in range(8):
                gain = par("gdn_norm") if i < 4 else par("mlstm_norm", i - 4)
                last = dve.scalar_tensor_tensor(out=NT[:, i, :], in0=O8[:, i, :], scalar=gain, in1=T18[:, i, :],
                                                op0=ALU.mult, op1=ALU.mult)
            hv.did("scaled", last)
            hv.wait(dve, "scaled")
            ha.wait(dve, "silu")
            hv.did("gated", dve.tensor_tensor(NT[:, 0:4, :], NT[:, 0:4, :], GATE, ALU.mult))

        @block.tensor
        def _(pe):
            hv.wait(pe, "sq")
            for b in range(4):
                last = nc.tensor.matmul(PS[:, b, :], ONES, fl(SQ8[:, 2 * b:2 * b + 2, :]), start=True, stop=True)
            hp.did("ssq", last)

    rg_loaded = sem("rglru_loaded")
    rp = marks("rglru_products", ["r", "i"])
    ra = marks("rglru_scalar", ["le", "ll", "r", "i", "tanh", "a", "sqrt", "gelu"])
    rv = marks("rglru_vector", ["labs", "l1", "lneg", "lsp", "lsp8", "d1", "rec", "sq", "ix", "inp", "scan", "out"])
    WA_, WX_ = area(R_, 6144, 4), area(R_, 6656, 4)
    RR4, II4, TH, AA, GE, DE, HH = [area(R_, 7168 + 1024 * i, 4, T) for i in range(7)]
    LAM = SPARE[:, 9, 64:68]
    LT1, LT2, LSP, LNEG8 = [SPARE[:, 9, 68 + 4 * i:72 + 4 * i] for i in range(4)]
    XB = CV[:, 20:24, :]
    with nc.Block() as block:
        @block.sync
        def _(sp):
            sp.dma_start(WA_, A["rglru_w_a"][0].rearrange("n i j -> i n j")).then_inc(rg_loaded, 16)
            sp.dma_start(WX_, A["rglru_w_x"][0].rearrange("n i j -> i n j")).then_inc(rg_loaded, 16)

        @block.scalar
        def _(act):
            rv.wait(act, "labs")
            ra.did("le", act.activation(LT1, LT1, ACT.Exp, scale=-1.0))
            rv.wait(act, "l1")
            ra.did("ll", act.activation(LT1, LT1, ACT.Ln))
            rp.wait(act, "r")
            for n in range(4):
                last = act.activation(RR4[:, n, :], ps_t(0)[:, n, :], ACT.Sigmoid, bias=par("rglru_b_a", n))
            ra.did("r", last)
            rp.wait(act, "i")
            for n in range(4):
                last = act.activation(II4[:, n, :], ps_t(2)[:, n, :], ACT.Sigmoid, bias=par("rglru_b_x", n))
            ra.did("i", last)
            rv.wait(act, "lsp8")
            ra.wait(act, "r")
            for n in range(4):
                last = act.activation(TH[:, n, :], RR4[:, n, :], ACT.Tanh, scale=LSP[:, n:n + 1])
            ra.did("tanh", last)
            for n in range(4):
                last = act.activation(AA[:, n, :], RR4[:, n, :], ACT.Exp, scale=LNEG8[:, n:n + 1])
            ra.did("a", last)
            rv.wait(act, "sq")
            ra.did("sqrt", act.activation(TH, TH, ACT.Sqrt))
            ra.did("gelu", act.activation(GE, BIG[:, RG:RG + 4, :], ACT.Gelu_apprx_tanh))

        @block.vector
        def _(dve):
            lam = par("rglru_lambda", 0, 4)
            rv.did("labs", dve.scalar_tensor_tensor(out=LT1, in0=lam, scalar=-1.0, in1=lam, op0=ALU.mult, op1=ALU.max))
            ra.wait(dve, "le")
            rv.did("l1", dve.tensor_scalar(LT1, LT1, 1.0, None, ALU.add))
            rv.did("lneg", dve.tensor_scalar(LT2, lam, -1.0, 0.0, ALU.mult, ALU.max))
            rv.wait(dve, "lneg")
            ra.wait(dve, "ll")
            rv.did("lsp", dve.tensor_tensor(LSP, LT2, LT1, ALU.add))
            rv.wait(dve, "lsp")
            dve.tensor_scalar(LNEG8, LSP, -8.0, None, ALU.mult)
            rv.did("lsp8", dve.tensor_scalar(LSP, LSP, 8.0, None, ALU.mult))
            ra.wait(dve, "tanh")
            rv.did("d1", dve.tensor_scalar(DE, TH, 1.0, None, ALU.add))
            rv.wait(dve, "d1")
            rv.did("rec", dve.reciprocal(DE, DE))
            rv.wait(dve, "rec")
            rv.did("sq", dve.scalar_tensor_tensor(out=fl(TH), in0=fl(TH), scalar=2.0, in1=fl(DE),
                                                  op0=ALU.mult, op1=ALU.mult))
            ra.wait(dve, "i")
            rv.did("ix", dve.tensor_tensor(II4, II4, XB, ALU.mult))
            rv.wait(dve, "ix")
            ra.wait(dve, "sqrt")
            rv.did("inp", dve.tensor_tensor(II4, II4, TH, ALU.mult))
            rv.wait(dve, "inp")
            for n in range(4):
                last = dve.tensor_tensor_scan(HH[:, n, :], AA[:, n, :], II4[:, n, :], 0.0, ALU.mult, ALU.add)
            rv.did("scan", last)
            rv.wait(dve, "scan")
            ra.wait(dve, "gelu")
            rv.did("out", dve.tensor_tensor(NT[:, 8:12, :], HH, GE, ALU.mult))

        @block.tensor
        def _(pe):
            pe.wait_ge(rg_loaded, 32)
            for name, w, bank in (("r", WA_, 0), ("i", WX_, 2)):
                for n in range(4):
                    last = nc.tensor.matmul(ps_t(bank)[:, n, :], w[:, n, :], XB[:, n, :], start=True, stop=True)
                rp.did(name, last)
    if stop == 3:
        return ctx

    wload = sem("rwkv_loaded")
    wp = marks("rwkv_products", ["w2", "a2", "g2", "kkss", "v_nat", "b_nat", "k_nat", "lt", "pt", "qbt", "qkt", "cx0"]
               + [s for l in range(1, 6) for s in ((f"cx{l}", f"y{l}", f"yt{l}") if l < 5 else (f"cx{l}", f"yt{l}"))]
               + [s for c in range(4) for s in ((f"r{c}", f"u{c}", f"y_{c}") + ((f"s{c}",) if c < 3 else ()))]
               + ["mean", "rk", "var"])
    wa = marks("rwkv_scalar", ["tanh", "sg", "sig", "a", "g", "w", "wi", "wp", "kksd", "vn", "bn", "kn"]
               + [f"cxs{l}" for l in range(1, 6)]
               + [s for c in range(4) for s in (f"r{c}", f"u{c}", f"y_{c}")] + ["sd"])
    wv = marks("rwkv_vector", ["diff0", "diff", "dmu", "mix", "ld", "cum", "cmp", "kkr", "kksq", "kkt", "kkrec", "kk",
                               "am1", "kp", "rt", "kt", "b", "bt", "at0", "at", "zero", "lt", "pt", "ct0",
                               "qbt", "qkt", "x0", "ct1"]
               + [s for l in range(1, 5) for s in (f"x{l}", f"xt{l}", f"ct{l + 1}")] + ["xt5"]
               + [s for c in range(3) for s in (f"sa{c}", f"s{c}")]
               + ["rk0", "rk1", "cen", "var", "ms", "rs", "n0", "n1", "n2", "rkv", "n3", "out"])
    W2, A2, G2 = R_[0:64, 0:512], R_[64:128, 0:512], R_[:, 512:1024]
    DIFF = area(R_, 1024, 14, T)
    MIXED = BIG[:, 40:54, :]
    r4, k4, v4 = [BIG[:, 40 + 4 * i:44 + 4 * i, :] for i in range(3)]
    e4 = [BIG[:, 4 * i:4 * i + 4, :] for i in range(10)]
    LD, CUM, WC, WI, WP_, AS, GG, KKN, KP_, RTL = e4
    KTL, BTL, ATL, T4 = [area(T_, 1024 * i, 4, T) for i in range(4)]
    M16 = [area(R_, 2048 * i, 16) for i in range(8)]
    MLT, MPT, MQB, MQK, MXI, MXT, MCT, MCX = M16

    def mat(h, t):
        return 8 * (h % 2) + 2 * (h // 2) + t

    VNW, BNW, KNW = [fl(e).rearrange("p (t c) -> p t c", t=2) for e in (AS, CUM, WI)]
    SW = fl(BIG[:, 54:56, :]).rearrange("p (h i) -> p h i", h=4)
    RS_, US = [fl(BIG[:, 56 + 2 * i:58 + 2 * i, :]) for i in range(2)]
    YW = fl(BIG[:, 60:64, :]).rearrange("p (h t) -> p h t", h=4)
    with nc.Block() as block:
        @block.sync
        def _(sp):
            sp.dma_start(W2, A["rwkv_w2"][0]).then_inc(wload, 16)
            sp.dma_start(A2, A["rwkv_a2"][0]).then_inc(wload, 16)
            sp.dma_start(G2, A["rwkv_g2"][0]).then_inc(wload, 16)

        @block.scalar
        def _(act):
            wv.wait(act, "mix")
            wa.did("tanh", act.activation(BIG[0:64, WWA, :], BIG[0:64, WWA, :], ACT.Tanh))
            wa.did("sg", act.activation(BIG[:, WG, :], BIG[:, WG, :], ACT.Sigmoid))
            wp.wait(act, "w2")
            for i in range(4):
                last = act.activation(LD[:, i, :], ps_t(0)[:, i, :], ACT.Sigmoid, bias=par("rwkv_w0", i))
            wa.did("sig", last)
            wp.wait(act, "a2")
            for i in range(4):
                last = act.activation(AS[:, i, :], ps_t(2)[:, i, :], ACT.Sigmoid, bias=par("rwkv_a0", i))
            wa.did("a", last)
            wp.wait(act, "g2")
            wa.did("g", act.activation(GG, ps_t(4), ACT.Copy))
            wv.wait(act, "cmp")
            wa.did("w", act.activation(WC, CUM, ACT.Exp))
            wa.did("wi", act.activation(WI, CUM, ACT.Exp, scale=-1.0))
            wa.did("wp", act.activation(WP_, LD, ACT.Exp))
            wv.wait(act, "kkt")
            wa.did("kksd", act.activation(T4, T4, ACT.Sqrt))
            wv.wait(act, "at")
            wp.wait(act, "v_nat")
            wa.did("vn", act.activation(VNW, PS[:, 0:2, :], ACT.Copy))
            wp.wait(act, "b_nat")
            wa.did("bn", act.activation(BNW, PS[:, 2:4, :], ACT.Copy))
            wp.wait(act, "k_nat")
            wa.did("kn", act.activation(KNW, PS[:, 4:6, :], ACT.Copy))
            for l in range(1, 6):
                wp.wait(act, f"cx{l}")
                wa.did(f"cxs{l}", act.activation(MCX, ps_m(0, 4), ACT.Copy))
            for c in range(4):
                rows = slice(64 * (c % 2), 64 * (c % 2) + 64)
                wp.wait(act, f"r{c}")
                wa.did(f"r{c}", act.activation(RS_[rows, :], PS[rows, 0, :], ACT.Copy))
                wp.wait(act, f"u{c}")
                wa.did(f"u{c}", act.activation(US[rows, :], PS[rows, 1, :], ACT.Copy))
                wp.wait(act, f"y_{c}")
                wa.did(f"y_{c}", act.activation(YW[:, :, 64 * c:64 * c + 64],
                                                PS[:, 2, 0:256].rearrange("p (h t) -> p h t", h=4), ACT.Copy))
            wv.wait(act, "ms")
            wa.did("sd", act.activation(T4, T4, ACT.Sqrt))

        @block.vector
        def _(dve):
            def stt(out, a, s, b, op0, op1):
                return dve.scalar_tensor_tensor(out=out, in0=a, scalar=s, in1=b, op0=op0, op1=op1)

            wv.did("diff0", dve.tensor_scalar(DIFF[:, :, 0:1], MIXED[:, :, 0:1], -1.0, None, ALU.mult))
            wv.did("diff", dve.tensor_tensor(DIFF[:, :, 1:T], MIXED[:, :, 0:T - 1], MIXED[:, :, 1:T], ALU.subtract))
            wv.wait(dve, "diff")
            wv.did("dmu", dve.tensor_tensor(DIFF, DIFF, spread(par("rwkv_mu", 0, 14), T), ALU.mult))
            wv.wait(dve, "dmu")
            wv.did("mix", dve.tensor_tensor(MIXED, MIXED, DIFF, ALU.add))
            wa.wait(dve, "sig")
            wv.did("ld", dve.tensor_scalar(LD, LD, -float(np.exp(-0.5)), None, ALU.mult))
            wv.wait(dve, "ld")
            for i in range(4):
                last = dve.tensor_tensor_scan(CUM[:, i, :], cst("reset64"), LD[:, i, :], 0.0, ALU.mult, ALU.add)
            wv.did("cum", last)
            wv.wait(dve, "cum")
            wv.did("cmp", dve.tensor_tensor(LD, CUM, LD, ALU.subtract))
            wv.did("kkr", dve.tensor_tensor(KKN, k4, spread(par("rwkv_k_k", 0, 4), T), ALU.mult))
            wv.wait(dve, "kkr")
            wv.did("kksq", dve.tensor_tensor(T4, KKN, KKN, ALU.mult))
            wp.wait(dve, "kkss")
            wv.did("kkt", dve.tensor_scalar(T4, ps_t(6), EPS, None, ALU.add))
            wa.wait(dve, "kksd")
            wv.did("kkrec", dve.reciprocal(T4, T4))
            wv.wait(dve, "kkrec")
            wv.did("kk", dve.tensor_tensor(KKN, KKN, T4, ALU.mult))
            wv.wait(dve, "kk")
            wa.wait(dve, "a")
            for i in range(4):
                last = dve.tensor_scalar(T4[:, i, :], AS[:, i, :], -1.0, par("rwkv_k_a", i), ALU.add, ALU.mult)
            wv.did("am1", last)
            wv.wait(dve, "am1")
            wv.did("kp", stt(fl(KP_), fl(T4), 1.0, fl(k4), ALU.add, ALU.mult))
            wv.wait(dve, "kp")
            wa.wait(dve, "wp")
            wv.did("rt", dve.tensor_tensor(RTL, r4, WC, ALU.mult))
            wv.did("kt", dve.tensor_tensor(KTL, KP_, WI, ALU.mult))
            wv.did("b", dve.tensor_tensor(BTL, KKN, AS, ALU.mult))
            wv.wait(dve, "b")
            wv.did("bt", dve.tensor_tensor(BTL, BTL, WI, ALU.mult))
            wv.did("at0", dve.tensor_tensor(ATL, KKN, WP_, ALU.mult))
            wv.wait(dve, "at0")
            wv.did("at", dve.tensor_scalar(ATL, ATL, -1.0, None, ALU.mult))
            wv.did("zero", dve.memset(SW, 0.0))
            strict, incl = repeated(cst("strict64_T"), 16), repeated(cst("incl64_T"), 16)
            wp.wait(dve, "lt")
            wv.did("lt", stt(MLT, ps_m(0, 4), -1.0, strict, ALU.mult, ALU.mult))
            wp.wait(dve, "pt")
            wv.did("pt", dve.tensor_tensor(MPT, ps_m(4, 4), strict, ALU.mult))
            wv.wait(dve, "lt")
            wv.did("ct0", dve.tensor_tensor(MCT, MLT, repeated(cst("level1"), 16), ALU.mult))
            wp.wait(dve, "qbt")
            wv.did("qbt", dve.tensor_tensor(MQB, ps_m(0, 4), incl, ALU.mult))
            wp.wait(dve, "qkt")
            wv.did("qkt", dve.tensor_tensor(MQK, ps_m(4, 4), incl, ALU.mult))
            wp.wait(dve, "cx0")
            dve.tensor_tensor(MXI, repeated(IDENT, 16), ps_m(0, 4), ALU.subtract)
            wv.did("x0", dve.tensor_tensor(MXT, repeated(IDENT, 16), MCT, ALU.subtract))
            wv.wait(dve, "x0")
            wv.did("ct1", dve.tensor_tensor(MCT, MLT, repeated(cst("level2"), 16), ALU.mult))
            for l in range(1, 5):
                wp.wait(dve, f"y{l}")
                wp.wait(dve, f"yt{l}")
                wv.did(f"x{l}", dve.tensor_tensor(MXI, MXI, ps_m(4, 4), ALU.subtract))
                wv.did(f"xt{l}", dve.tensor_tensor(MXT, MXT, ps_m(0, 4), ALU.subtract))
                wv.did(f"ct{l + 1}", dve.tensor_tensor(MCT, MLT, repeated(cst(f"level{LEVELS[l + 1]}"), 16), ALU.mult))
            wp.wait(dve, "yt5")
            wv.did("xt5", dve.tensor_tensor(MXT, MXT, ps_m(0, 4), ALU.subtract))
            for c in range(3):
                wp.wait(dve, f"s{c}")
                if c == 0:
                    wv.wait(dve, "zero")
                for e in range(2):
                    q = slice(64 * e, 64 * e + 64)
                    last = dve.tensor_tensor(SW[q, :, q], SW[q, :, q], ps_m(3, 1)[q, :, q], ALU.add)
                wv.did(f"sa{c}", last)
                wv.wait(dve, f"sa{c}")
                for e in range(2):
                    q = slice(64 * e, 64 * e + 64)
                    decay = WC[q, :, 64 * c + 63:64 * c + 64].broadcast_to([64, 4, 64])
                    last = dve.tensor_tensor(SW[q, :, q], SW[q, :, q], decay, ALU.mult)
                wv.did(f"s{c}", last)
            wv.did("rk0", dve.tensor_tensor(LD, r4, KP_, ALU.mult))
            wv.wait(dve, "rk0")
            wv.did("rk1", dve.tensor_tensor(LD, LD, spread(par("rwkv_r_k", 0, 4), T), ALU.mult))
            wp.wait(dve, "mean")
            wv.did("cen", stt(YW, ps_t(4), -1.0 / 64, YW, ALU.mult, ALU.add))
            wv.wait(dve, "cen")
            wv.did("var", dve.tensor_tensor(KKN, YW, YW, ALU.mult))
            wp.wait(dve, "var")
            wv.did("ms", dve.tensor_scalar(T4, ps_t(6), 1.0 / 64, 64e-5, ALU.mult, ALU.add))
            wa.wait(dve, "sd")
            wv.did("rs", dve.reciprocal(T4, T4))
            wv.wait(dve, "rs")
            wv.did("n0", dve.tensor_tensor(YW, YW, T4, ALU.mult))
            wv.wait(dve, "n0")
            wv.did("n1", dve.tensor_tensor(YW, YW, spread(par("rwkv_ln_w", 0, 4), T), ALU.mult))
            wv.wait(dve, "n1")
            wv.did("n2", dve.tensor_tensor(YW, YW, spread(par("rwkv_ln_b", 0, 4), T), ALU.add))
            wv.did("rkv", dve.tensor_tensor(KKN, v4, ps_t(0), ALU.mult))
            wv.wait(dve, "rkv")
            wv.did("n3", dve.tensor_tensor(YW, YW, KKN, ALU.add))
            wv.wait(dve, "n3")
            wv.did("out", dve.tensor_tensor(NT[:, 12:16, :], YW, GG, ALU.mult))

        @block.tensor
        def _(pe):
            mmul = nc.tensor.matmul
            pe.wait_ge(wload, 48)
            wa.wait(pe, "sg")
            for name, w, x, bank in (("w2", W2, BIG[0:64, WWA, :], 0), ("a2", A2, BIG[64:128, WWA, :], 2),
                                     ("g2", G2, BIG[:, WG, :], 4)):
                for i in range(4):
                    last = mmul(ps_t(bank)[:, i, :], w[:, i * P:(i + 1) * P], x, start=True, stop=True)
                wp.did(name, last)
            wv.wait(pe, "kksq")
            for b in range(2):
                last = mmul(PS[:, 6 + b, :], ONES64, fl(T4[:, 2 * b:2 * b + 2, :]), start=True, stop=True)
            wp.did("kkss", last)
            wv.wait(pe, "at")
            wa.wait(pe, "g")
            for name, src, bank in (("v_nat", v4, 0), ("b_nat", BTL, 2), ("k_nat", KTL, 4)):
                for t in range(TT):
                    for i in range(4):
                        last = nc.tensor.transpose(PS[:, bank + t, i * P:(i + 1) * P],
                                                   src[:, i, t * P:(t + 1) * P], IDENT)
                wp.did(name, last)
            wa.wait(pe, "kn")
            for name, lhs, rhs, bank in (("lt", BTL, ATL, 0), ("pt", KTL, ATL, 4), ("qbt", BTL, RTL, 0),
                                         ("qkt", KTL, RTL, 4)):
                if name == "qbt":
                    wv.wait(pe, "lt")
                if name == "qkt":
                    wv.wait(pe, "pt")
                for m in range(16):
                    h, t = 2 * (m % 8 // 2) + m // 8, m % 2
                    q = slice(64 * (h % 2), 64 * (h % 2) + 64)
                    last = mmul(ps_m(bank, 4)[:, m, :], lhs[q, h // 2, t * P:(t + 1) * P],
                                rhs[q, h // 2, t * P:(t + 1) * P], start=True, stop=True)
                wp.did(name, last)
            wv.wait(pe, "qbt")
            for m in range(16):
                last = nc.tensor.transpose(ps_m(0, 4)[:, m, :], MCT[:, m, :], IDENT)
            wp.did("cx0", last)
            for l in range(1, 6):
                wv.wait(pe, f"ct{l}")
                for m in range(16):
                    last = mmul(ps_m(0, 4)[:, m, :], MCT[:, m, :], MXI[:, m, :], start=True, stop=True)
                wp.did(f"cx{l}", last)
                wa.wait(pe, f"cxs{l}")
                if l < 5:
                    for m in range(16):
                        last = mmul(ps_m(4, 4)[:, m, :], MXT[:, m, :], MCX[:, m, :], start=True, stop=True)
                    wp.did(f"y{l}", last)
                for m in range(16):
                    last = mmul(ps_m(0, 4)[:, m, :], MCX[:, m, :], MXT[:, m, :], start=True, stop=True)
                wp.did(f"yt{l}", last)
            wv.wait(pe, "xt5")
            for c in range(4):
                t, q = c // 2, slice(64 * (c % 2), 64 * (c % 2) + 64)
                cols = slice(64 * c, 64 * c + 64)
                if c:
                    wv.wait(pe, f"s{c - 1}")
                for hp2 in range(4):
                    if c:
                        mmul(PS[q, 0, hp2 * P:(hp2 + 1) * P], ATL[:, hp2, cols], SW[:, hp2, :], start=True, stop=False)
                    for e in range(2):
                        h = 2 * hp2 + e
                        last = mmul(PS[q, 0, 64 * h:64 * h + 64], MPT[q, mat(h, t), q], VNW[q, t, 64 * h:64 * h + 64],
                                    start=(c == 0), stop=(c == 0 or e == 1))
                wp.did(f"r{c}", last)
                wa.wait(pe, f"r{c}")
                for h in range(8):
                    last = mmul(PS[q, 1, 64 * h:64 * h + 64], MXT[q, mat(h, t), q], RS_[q, 64 * h:64 * h + 64],
                                start=True, stop=True)
                wp.did(f"u{c}", last)
                wa.wait(pe, f"u{c}")
                for hp2 in range(4):
                    dst = PS[:, 2, 64 * hp2:64 * hp2 + 64]
                    if c:
                        mmul(dst, SW[:, hp2, :], RTL[:, hp2, cols], start=True, stop=False)
                    for e in range(2):
                        h = 2 * hp2 + e
                        hc, o = slice(64 * h, 64 * h + 64), slice(64 * e, 64 * e + 64)
                        mmul(dst[o, :], US[q, hc], MQB[q, mat(h, t), q], start=(c == 0), stop=False)
                        last = mmul(dst[o, :], VNW[q, t, hc], MQK[q, mat(h, t), q], start=False, stop=True)
                wp.did(f"y_{c}", last)
                if c < 3:
                    for h in range(8):
                        hc, o = slice(64 * h, 64 * h + 64), slice(64 * (h % 2), 64 * (h % 2) + 64)
                        mmul(PS[o, 3, hc], BNW[q, t, hc], US[q, hc], start=True, stop=False)
                        last = mmul(PS[o, 3, hc], KNW[q, t, hc], VNW[q, t, hc], start=False, stop=True)
                    wp.did(f"s{c}", last)
            wa.wait(pe, "y_3")
            for b in range(2):
                last = mmul(PS[:, 4 + b, :], ONES64, fl(YW[:, 2 * b:2 * b + 2, :]), start=True, stop=True)
            wp.did("mean", last)
            wv.wait(pe, "rk1")
            for b in range(2):
                last = mmul(PS[:, b, :], ONES64, fl(LD[:, 2 * b:2 * b + 2, :]), start=True, stop=True)
            wp.did("rk", last)
            wv.wait(pe, "var")
            for b in range(2):
                last = mmul(PS[:, 6 + b, :], ONES64, fl(KKN[:, 2 * b:2 * b + 2, :]), start=True, stop=True)
            wp.did("var", last)
    if stop == 4:
        return ctx

    N_OUT, N_GU = D // P, F1 // 256
    B0 = IA
    B1 = B0 + N_OUT
    B2 = B1 + 4 * N_GU
    B3 = B2 + F1 // P
    NI2 = 2 * sum(n for _, n in GROUPS2)
    B4 = B3 + NI2 + 2
    L1 = N_OUT
    L2 = L1 + F1 // P
    L3 = L2 + N_OUT
    acted = sem("hidden_acted")
    hidden = sem("hidden_made")
    res_done = sem("residual_done")
    gain_loaded = sem("gain_loaded")
    ACTED = area(T_, 0, 2, 512)
    GAIN = fl(BIG[:, 44:52, :])

    def two(x):
        return x.rearrange("p (c t) -> p c t", c=2)

    def row_gain(a):
        return a.rearrange("(o d) -> o d", o=1).broadcast_to([P, D])

    H0 = 2

    def pe_hidden(pe, n0, units):
        with pe.Fori(0, units // 2) as r:
            for u in range(2):
                pe.wait_ge(hidden, H0 + 2 * r + u - 1)
                for j in range(4):
                    pe_col_item(pe, n0 + 4 * u + j, 2 * r, j % 2, 4 * u + j // 2 * 2)

    def act_hidden(act, n0, units):
        with act.Fori(0, units // 2) as r:
            for u in range(2):
                for j in range(4):
                    split_hi(act, n0 + 4 * u + j + 2, 2 * r)
                    if j == 1:
                        act.wait_ge(item_used, n0 + 4 * u + 2 + 8 * r)
                        act.wait_ge(hidden, H0 + 2 * r + u - 1)
                        act.activation(two(ACTED[:, u, :]), PS[:, 4 * u:4 * u + 2, 0:T], ACT.Silu).then_inc(acted, 1)

    def dve_hidden(dve, n0, units):
        with dve.Fori(0, units // 2) as r:
            for u in range(2):
                for j in range(4):
                    split_lo(dve, n0 + 4 * u + j + 2, 2 * r)
                dve.wait_ge(item_used, n0 + 4 * u + 4 + 8 * r)
                dve.wait_ge(acted, 2 * r + u + 1)
                dve.tensor_tensor(BIG[:, bass.ds(4 * r + 2 * u, 2), :], two(ACTED[:, u, :]),
                                  PS[:, 4 * u + 2:4 * u + 4, 0:T], ALU.mult).then_inc(hidden, 1)

    with nc.Block() as block:
        @block.sync
        def _(sp):
            load_rows(sp, B0, A["w_out"][0])
            load_gate_up(sp, B1, A["ffn_w_gate"][0], A["ffn_w_up"][0], N_GU)
            sp.dma_start(GAIN, row_gain(A["final_norm"])).then_inc(gain_loaded, 16)
            n = load_rows(sp, B2, A["ffn_w_down"][0])
            for c, pairs in GROUPS2:
                n = load_cols(sp, n, A["w_in_2"][0], c, pairs)
            for c in (NSA_GATES, FOX_GATES):
                n = load_narrow(sp, n, A["w_in_2"][0], c)

        @block.scalar
        def _(act):
            split_hi(act, B0)
            split_hi(act, B0 + 1)
            act_rows(act, B0, 0, N_OUT, NT, B4)
            norm_act(act, 1, lambda e, t: e.wait_ge(res_done, t + 1))
            norm_act_hi(act, 1)
            act.wait_ge(norm_out, 16)
            act_hidden(act, B1, N_GU)
            act.wait_ge(hidden, H0 + N_GU)
            act_rows(act, B2, L1, F1 // P, BIG, B4)
            norm_act(act, 2, lambda e, t: e.wait_ge(res_done, 2 + t + 1))
            norm_act(act, 3, lambda e, t: e.wait_ge(res_done, 4 + t + 1))
            norm_act_hi(act, 3)
            act.wait_ge(norm_out, 24)
            n, q, at = B3, NI // 2, 0
            for _, pairs in GROUPS2:
                act_cols(act, n, q, pairs, at, B4)
                n, q, at = n + 2 * pairs, q + pairs, at + 2 * pairs
            act.wait_ge(item_used, B4)
            act.activation(GT[0:24, 0, :], PS[0:24, 6, 0:T], ACT.Copy)
            act.activation(GT[0:8, 1, :], PS[0:8, 7, 0:T], ACT.Copy)

        def add_residual(dve, used):
            dve.wait_ge(item_used, used)
            for t in range(TT):
                dve.tensor_tensor(X[:, t, :], X[:, t, :], PS[:, 4 * t:4 * t + 4, :].rearrange("p b n -> p (b n)"),
                                  ALU.add).then_inc(res_done, 1)

        @block.vector
        def _(dve):
            for _ in range(H0):
                dve.engine_nop().then_inc(hidden, 1)
            split_lo(dve, B0)
            split_lo(dve, B0 + 1)
            dve_rows(dve, B0, 0, N_OUT, NT, B4)
            add_residual(dve, B1)
            dve.wait_ge(res_done, 2)
            norm_dve(dve, 1, "ffn_norm")
            dve_hidden(dve, B1, N_GU)
            dve_rows(dve, B2, L1, F1 // P, BIG, B4)
            add_residual(dve, B3)
            dve.wait_ge(res_done, 4)
            norm_dve(dve, 2, None)
            dve.wait_ge(gain_loaded, 16)
            for t in range(TT):
                dve.scalar_tensor_tensor(out=X[:, t, :], in0=X[:, t, :], scalar=ST[:, 6 + t:7 + t], in1=GAIN,
                                         op0=ALU.mult, op1=ALU.mult).then_inc(res_done, 1)
            dve.wait_ge(res_done, 6)
            norm_dve(dve, 3, "g_mix_pre_2")
            dve_ahead(dve, B3, NI2, B4)

        @block.tensor
        def _(pe):
            pe_rows(pe, B0, 0, N_OUT)
            norm_pe(pe, 1)
            pe.wait_ge(norm_out, 16)
            pe_hidden(pe, B1, N_GU)
            pe.wait_ge(hidden, H0 + N_GU)
            pe_rows(pe, B2, L1, F1 // P)
            norm_pe(pe, 3)
            pe.wait_ge(norm_out, 24)
            n, q = B3, NI // 2
            for _, pairs in GROUPS2:
                pe_cols(pe, n, q, pairs)
                n, q = n + 2 * pairs, q + pairs
            for m in range(2):
                pe_narrow(pe, n + m, 6 + m)
    if stop == 5:
        return ctx

    G8 = area(R_, 0, 24, T)
    VNAT = R_[:, 6144:6144 + 3584].rearrange("p (t c) -> p t c", t=TT)
    KDUP = R_[:, 9728:9728 + 1024].rearrange("p (s g t) -> p s g t", s=2, g=2)
    ZSH = R_[:, 10752:10752 + 1024].rearrange("p (v g t) -> p v g t", v=2, g=2)
    CB = area(R_, 11776, 8, 384)
    VTILES = [AVS, AVW] + [BV + i for i in range(4)] + [CV_ + i for i in range(4)] + [DV + i for i in range(4)]
    W1 = [area(T_, 0, 16, T), BIG[:, 46:62, :]]
    SMALL = R_[:, 14848:16384]
    BT = SMALL[:, 0:960].rearrange("p (v l g n) -> p v l g n", v=2, l=16, g=2)
    W2K = SMALL[:, 960:1216].rearrange("p (h d) -> p h d", h=2)
    W2V = SMALL[:, 1216:1344].rearrange("p (h d) -> p h d", h=2)
    HID = SMALL[:, 1344:1464].rearrange("p (v h n) -> p v h n", v=2, h=2)
    KC = SMALL[:, 1464:1494]
    VC = fl(BIG[:, 62:63, :])[0:15, 0:128]
    GATEC = fl(BIG[:, 62:63, :])[:, 128:176].rearrange("p (t n) -> p t n", t=TT)
    FCOL = fl(BIG[:, 62:63, :])[:, 176:192].rearrange("p (t n) -> p t n", t=TT)
    FR = [GT[0:8, i, :] for i in range(4)] + [fl(BIG[:, 63:64, :])[0:8, :]]
    windows_moved = sem("windows_moved")
    keys_moved = sem("keys_moved")
    cload = sem("cmp_weights_loaded")
    biasin = sem("bias_loaded")
    cp = marks("prep_products", ["hid", "kvc"] + ["vn0", "vn1", "cols", "fox"])
    ca = marks("prep_scalar", ["gates", "fex", "fln", "gelu", "vn0", "vn1"])
    cv = marks("prep_vector", ["bt", "fx", "fax", "fe1", "flf", "fscan", "fn8", "kvc", "cols", "cb"])
    with nc.Block() as block:
        @block.sync
        def _(sp):
            sp.dma_start(CST[:, :], A["const"]).then_inc(const_loaded, 16)
            for v, tile in enumerate((AKC, AVC)):
                for g in range(2):
                    src = BIG[64 * g:64 * g + 64, tile, :]
                    sp.dma_start(ZSH[0:64, v, g, :], src).then_inc(windows_moved, 16)
                    sp.dma_start(ZSH[64:128, v, g, 0:T - 1], src[:, 1:T]).then_inc(windows_moved, 16)
            for w, src in zip(W1, ("phik_w1_2", "phiv_w1_2")):
                sp.dma_start(w, A[src][0].rearrange("(l p) h -> p l h", p=P)).then_inc(cload, 16)
            w2 = A["phik_w2_2"][0].rearrange("(h p) d -> p h d", p=P)
            sp.dma_start(W2K[:, :, 0:64], w2).then_inc(cload, 16)
            sp.dma_start(W2K[:, :, 64:128], w2).then_inc(cload, 16)
            sp.dma_start(W2V, A["phiv_w2_2"][0].rearrange("(h p) d -> p h d", p=P)).then_inc(cload, 16)
            for s, tile in enumerate((AKS, AKW)):
                for g in range(2):
                    for e in range(2):
                        sp.dma_start(KDUP[64 * e:64 * e + 64, s, g, :], BIG[64 * g:64 * g + 64, tile, :])\
                            .then_inc(keys_moved, 16)
            skew = bass.AP(bias_skew.tensor, 127, [[383, P], [P * 384, 24], [1, T]])
            sp.dma_start(G8, skew).then_inc(biasin, 16)
            sp.wait_ge(biasin, 16)
            sp.wait_ge(keys_moved, 128)

        @block.scalar
        def _(act):
            ca.did("gates", act.activation(GT[0:24, 0, :], GT[0:24, 0, :], ACT.Sigmoid))
            cv.wait(act, "fax")
            ca.did("fex", act.activation(FR[2], FR[2], ACT.Exp, scale=-1.0))
            cv.wait(act, "fe1")
            ca.did("fln", act.activation(FR[2], FR[2], ACT.Ln))
            cp.wait(act, "hid")
            ca.did("gelu", act.activation(HID, PS[:, 0, 0:120].rearrange("p (v h n) -> p v h n", v=2, h=2),
                                          ACT.Gelu_apprx_tanh))
            for t in range(TT):
                cp.wait(act, f"vn{t}")
                ca.did(f"vn{t}", act.activation(VNAT[:, t, :], fl(PS[:, 2:6, :])[:, 0:1792], ACT.Copy))

        @block.vector
        def _(dve):
            dve.wait_ge(const_loaded, 32)
            dve.wait_ge(windows_moved, 128)
            for v in range(2):
                for g in range(2):
                    for half in range(2):
                        src = ZSH[:, v, g, 16 * half:16 * half + 240].rearrange("p (n l two) -> p l n two", l=8, two=2)
                        last = dve.tensor_tensor(BT[:, v, 8 * half:8 * half + 8, g, :], src[:, :, :, 0],
                                                 spread(par("cmp_pe_2", 8 * half, 8), 15), ALU.add)
            cv.did("bt", last)
            cv.did("fx", dve.tensor_scalar(FR[1], FR[1], HC[0:8, 4:5], None, ALU.add))
            cv.wait(dve, "fx")
            cv.did("fax", dve.scalar_tensor_tensor(out=FR[2], in0=FR[1], scalar=-1.0, in1=FR[1],
                                                   op0=ALU.mult, op1=ALU.max))
            ca.wait(dve, "fex")
            cv.did("fe1", dve.tensor_scalar(FR[2], FR[2], 1.0, None, ALU.add))
            ca.wait(dve, "fln")
            cv.did("flf", dve.scalar_tensor_tensor(out=FR[3], in0=FR[1], scalar=0.0, in1=FR[2],
                                                   op0=ALU.min, op1=ALU.subtract))
            cv.wait(dve, "flf")
            cv.did("fscan", dve.tensor_tensor_scan(FR[4], UNIT[0:8, :], FR[3], 0.0, ALU.mult, ALU.add))
            cv.wait(dve, "fscan")
            cv.did("fn8", dve.tensor_scalar(FR[4], FR[4], -8.0, None, ALU.mult))
            cp.wait(dve, "kvc")
            dve.tensor_copy(KC, PS[:, 1, 0:30])
            cv.did("kvc", dve.tensor_copy(VC, PS[0:15, 1, 32:160]))
            cp.wait(dve, "cols")
            dve.tensor_copy(GATEC, PS[:, 6, 0:48].rearrange("p (t n) -> p t n", t=TT))
            cv.did("cols", dve.tensor_copy(FCOL, PS[:, 6, 48:64].rearrange("p (t n) -> p t n", t=TT)))
            cv.wait(dve, "cols")
            cp.wait(dve, "fox")
            for h in range(8):
                row = ps_t(2, 4)[:, h, :]
                dve.scalar_tensor_tensor(out=CB[:, h, 0:P], in0=row[:, 0:P], scalar=FCOL[:, 0, h:h + 1],
                                         in1=cst("causal8"), op0=ALU.subtract, op1=ALU.add)
                dve.tensor_scalar(CB[:, h, P:T], row[:, 0:P], FCOL[:, 1, h:h + 1], None, ALU.subtract)
                last = dve.scalar_tensor_tensor(out=CB[:, h, T:384], in0=row[:, P:T], scalar=FCOL[:, 1, h:h + 1],
                                                in1=cst("causal8"), op0=ALU.subtract, op1=ALU.add)
            cv.did("cb", last)

        @block.tensor
        def _(pe):
            mmul = nc.tensor.matmul
            pe.wait_ge(cload, 80)
            cv.wait(pe, "bt")
            for v in range(2):
                for ht in range(2):
                    at = (2 * v + ht) * 30
                    for l in range(16):
                        last = mmul(PS[:, 0, at:at + 30], W1[v][:, l, ht * P:(ht + 1) * P],
                                    BT[:, v, l, :, :].rearrange("p g n -> p (g n)"), start=(l == 0), stop=(l == 15))
            cp.did("hid", last)
            ca.wait(pe, "gelu")
            for ht in range(2):
                mmul(PS[:, 1, 0:30], W2K[:, ht, :], HID[:, 0, ht, :], start=(ht == 0), stop=(ht == 1))
            for g in range(2):
                for ht in range(2):
                    last = mmul(PS[0:15, 1, 32 + 64 * g:96 + 64 * g], HID[:, 1, ht, 15 * g:15 * g + 15], W2V[:, ht, :],
                                start=(ht == 0), stop=(ht == 1))
            cp.did("kvc", last)
            for t in range(TT):
                if t:
                    ca.wait(pe, "vn0")
                for i, tile in enumerate(VTILES):
                    last = nc.tensor.transpose(fl(PS[:, 2:6, :])[:, i * P:(i + 1) * P],
                                               BIG[:, tile, t * P:(t + 1) * P], IDENT)
                cp.did(f"vn{t}", last)
            cv.wait(pe, "fn8")
            ca.wait(pe, "gates")
            for t in range(TT):
                nc.tensor.transpose(PS[:, 6, 24 * t:24 * t + 24], GT[0:24, 0, t * P:(t + 1) * P], IDENT[0:24, 0:24])
                last = nc.tensor.transpose(PS[:, 6, 48 + 8 * t:56 + 8 * t], FR[4][:, t * P:(t + 1) * P], IDENT[0:8, 0:8])
            cp.did("cols", last)
            ca.wait(pe, "vn1")
            for h in range(8):
                last = mmul(ps_t(2, 4)[:, h, :], pick(h, 8), FR[4], start=True, stop=True)
            cp.did("fox", last)
    if stop == 6:
        return ctx

    PARTS = [(kind, h) for h in range(8) for kind in ("sel", "win", "cmp")]
    PARTS += [(kind, h) for kind in ("moba", "fox", "long") for h in range(8)]
    NPART = len(PARTS)
    FIRST = {"sel": True, "win": False, "cmp": False}
    LAST = {"sel": False, "win": False, "cmp": True}
    NE, NS, NPT = 4, 3, 3
    E2 = [T_[:, 384 * i:384 * i + 384] for i in range(NE)]
    PT2 = [T_[:, 1536 + 384 * i:1920 + 384 * i] for i in range(NPT)]
    STAT = T_[:, 2688:2688 + 3 * 2 * NPART].rearrange("p (s n q) -> p s n q", s=3, q=2)
    MINS, SUMS, RECS = [STAT[:, i] for i in range(3)]
    scored = sem("scored")
    lowest = sem("lowest")
    exped = sem("exped")
    recip = sem("reciprocals")
    gated = sem("reciprocals_gated")
    probs = sem("probs")
    probs_T = sem("probs_T")
    probs_out = sem("probs_out")
    valued = sem("valued")
    head_out = sem("head_pair_out")

    def query(kind, h):
        tile = {"moba": BQ, "fox": CQ, "long": DQ}.get(kind, AQ) + h // 2
        return BIG[64 * (h % 2):64 * (h % 2) + 64, tile, :]

    def key(kind, h):
        e = slice(64 * (h % 2), 64 * (h % 2) + 64)
        if kind in ("sel", "win"):
            return KDUP[e, ("sel", "win").index(kind), h // 4, :]
        if kind == "cmp":
            return KC[e, 15 * (h // 4):15 * (h // 4) + 15]
        return BIG[e, {"moba": BK, "fox": CK, "long": DK}[kind] + h // 2, :]

    def value(kind, h, t):
        if kind in ("sel", "win"):
            at = P * ("sel", "win").index(kind) + 64 * (h // 4)
        else:
            at = P * {"moba": 2, "fox": 6, "long": 10}[kind] + 64 * h
        return VNAT[:, t, at:at + 64]

    def spans(kind):
        return ((0, 7), (P, 15)) if kind == "cmp" else ((0, P), (P, T))

    def bias_of(kind, h, t):
        if kind == "fox":
            return CB[:, h, 0:P] if t == 0 else CB[:, h, P:384]
        row = G8[:, {"moba": 8, "long": 16}.get(kind, 0) + h, :]
        if kind == "cmp":
            first = 159 if t == 0 else 31
            n = spans(kind)[t][1]
            return row[:, first:first + 16 * (n - 1) + 1:16]
        return row[:, P:T] if t == 0 else row

    def o_index(kind, h):
        return {"moba": 4, "fox": 8, "long": 12}.get(kind, 0) + h // 2

    with nc.Block() as block:
        @block.tensor
        def _(pe):
            mmul = nc.tensor.matmul

            def scores(i):
                kind, h = PARTS[i]
                if i >= NS:
                    pe.wait_ge(lowest, i - NS + 1)
                q, k = query(kind, h), key(kind, h)
                for t, (at, n) in enumerate(spans(kind)):
                    last = mmul(PS[:, i % NS, at:at + n], q[:, t * P:(t + 1) * P], k[:, 0:n], start=True, stop=True)
                last.then_inc(scored, 1)

            def turn_probs(i):
                kind, h = PARTS[i]
                pe.wait_ge(probs, i + 1)
                if i >= NPT:
                    pe.wait_ge(probs_out, i - NPT + 1)
                bank, e = PS[:, 3 + i % NPT, :], E2[i % NE]
                if kind == "cmp":
                    for t, (at, n) in enumerate(spans(kind)):
                        last = nc.tensor.transpose(bank[0:n, at:at + P], e[:, at:at + n], IDENT)
                else:
                    for b in range(3):
                        last = nc.tensor.transpose(bank[:, b * P:(b + 1) * P], e[:, b * P:(b + 1) * P], IDENT)
                last.then_inc(probs_T, 1)

            def values(i):
                kind, h = PARTS[i]
                pe.wait_ge(probs_out, i + 1)
                o, e = o_index(kind, h), 64 * (h % 2)
                first, final = FIRST.get(kind, True), LAST.get(kind, True)
                if first and h % 2 == 0 and o >= 2:
                    pe.wait_ge(head_out, o - 1)
                dst, pt = PS[e:e + 64, 6 + o % 2, 0:T], PT2[i % NPT]
                if kind == "cmp":
                    v = VC[:, 64 * (h // 4):64 * (h // 4) + 64]
                    mmul(dst[:, 0:P], v[0:7, :], pt[0:7, 0:P], start=False, stop=False)
                    last = mmul(dst[:, P:T], v, pt[0:15, P:T], start=False, stop=True)
                else:
                    mmul(dst, value(kind, h, 0), pt[:, 0:T], start=first, stop=False)
                    last = mmul(dst[:, P:T], value(kind, h, 1), pt[:, T:384], start=False, stop=final)
                last.then_inc(valued, 1)

            for i in range(NPART + 3):
                if i < NPART:
                    scores(i)
                if 0 <= i - 2 < NPART:
                    turn_probs(i - 2)
                if 0 <= i - 3 < NPART:
                    values(i - 3)

        @block.vector
        def _(dve):
            def lowest_of(i):
                kind, h = PARTS[i]
                dve.wait_ge(scored, i + 1)
                if i >= NE:
                    dve.wait_ge(probs_T, i - NE + 1)
                for t, (at, n) in enumerate(spans(kind)):
                    last = dve.tensor_tensor_reduce(E2[i % NE][:, at:at + n], PS[:, i % NS, at:at + n],
                                                    bias_of(kind, h, t), -0.125, 3e38, ALU.add, ALU.min,
                                                    MINS[:, i, t:t + 1])
                last.then_inc(lowest, 1)

            def weights(i):
                kind, h = PARTS[i]
                dve.wait_ge(exped, i + 1)
                dve.reciprocal(RECS[:, i, :], SUMS[:, i, :]).then_inc(recip, 1)
                dve.wait_ge(recip, i + 1)
                if i < 24:
                    gate = GATEC[:, :, 8 * ("cmp", "sel", "win").index(kind) + h]
                    dve.tensor_tensor(RECS[:, i, :], RECS[:, i, :], gate, ALU.mult).then_inc(gated, 1)
                    dve.wait_ge(gated, i + 1 + i // 3)
                    if kind == "cmp":
                        dve.tensor_tensor(RECS[:, i, 0:1], RECS[:, i, 0:1], cst("from31"), ALU.mult).then_inc(gated, 1)
                        dve.wait_ge(gated, i + 2 + i // 3)
                for t, (at, n) in enumerate(spans(kind)):
                    e = E2[i % NE][:, at:at + n]
                    last = dve.tensor_scalar(e, e, RECS[:, i, t:t + 1], None, ALU.mult)
                last.then_inc(probs, 1)

            for i in range(NPART + 1):
                if i < NPART:
                    lowest_of(i)
                if i >= 1:
                    weights(i - 1)

        @block.scalar
        def _(act):
            def exponentials(i):
                kind, h = PARTS[i]
                act.wait_ge(lowest, i + 1)
                for t, (at, n) in enumerate(spans(kind)):
                    e = E2[i % NE][:, at:at + n]
                    last = act.activation(e, e, ACT.Exp, bias=MINS[:, i, t:t + 1], scale=-1.0,
                                          accum_out=SUMS[:, i, t:t + 1])
                last.then_inc(exped, 1)

            def probs_to_sbuf(i):
                kind, h = PARTS[i]
                act.wait_ge(probs_T, i + 1)
                if i >= NPT:
                    act.wait_ge(valued, i - NPT + 1)
                bank = PS[:, 3 + i % NPT, :]
                if kind == "cmp":
                    act.activation(PT2[i % NPT][0:7, 0:P], bank[0:7, 0:P], ACT.Copy)
                    last = act.activation(PT2[i % NPT][0:15, P:T], bank[0:15, P:T], ACT.Copy)
                else:
                    last = act.activation(PT2[i % NPT], bank[:, 0:384], ACT.Copy)
                last.then_inc(probs_out, 1)

            def heads_out(i):
                kind, h = PARTS[i]
                if h % 2 == 1 and LAST.get(kind, True):
                    o = o_index(kind, h)
                    act.wait_ge(valued, i + 1)
                    act.activation(NT[:, o, :], PS[:, 6 + o % 2, 0:T], ACT.Copy).then_inc(head_out, 1)

            for i in range(NPART + 4):
                if i < NPART:
                    exponentials(i)
                if 0 <= i - 2 < NPART:
                    probs_to_sbuf(i - 2)
                if 0 <= i - 4 < NPART:
                    heads_out(i - 4)
    if stop == 7:
        return ctx

    C0 = B4
    C1 = C0 + N_OUT
    N_UP = F2 // 256
    C2 = C1 + 2 * N_UP
    C3 = C2 + F2 // P
    Q2 = (NI + NI2) // 2
    GAIN2 = T_[:, 2048:4096]
    squared = sem("hidden_squared")
    scaled = sem("post_scaled")
    out_done = sem("out_done")
    gain2_loaded = sem("gain2_loaded")
    def post_square(act, q, used):
        act.wait_ge(item_used, used)
        for t in range(TT):
            if t:
                act.wait_ge(sq_done, 2 * q + 1)
            act.activation(T_[:, 0:D], PS[:, 4 * t:4 * t + 4, :].rearrange("p b n -> p (b n)"), ACT.Square,
                           accum_out=ST[:, t:t + 1]).then_inc(sq_done, 1)
        act.wait_ge(mean_done, q + 1)
        act.activation(ST[:, 4:6], ST[:, 2:4], ACT.Sqrt).then_inc(sd_done, 1)

    def post_scale(dve, n, gain):
        for t in range(TT):
            dve.scalar_tensor_tensor(out=T_[:, 0:D], in0=PS[:, 4 * t:4 * t + 4, :].rearrange("p b n -> p (b n)"),
                                     scalar=ST[:, 6 + t:7 + t], in1=gain, op0=ALU.mult, op1=ALU.mult)\
                .then_inc(scaled, 1)
            dve.wait_ge(scaled, 2 * n + t + 1)
            dve.tensor_tensor(X[:, t, :], X[:, t, :], T_[:, 0:D], ALU.add).then_inc(res_done, 1)
            dve.wait_ge(res_done, 6 + 2 * n + t + 1)

    with nc.Block() as block:
        @block.sync
        def _(sp):
            sp.dma_start(GAIN, row_gain(A["g_mix_post_2"][0])).then_inc(gain_loaded, 16)
            load_rows(sp, C0, A["w_out_2"][0])
            load_cols(sp, C1, A["w_up_2"][0], 0, N_UP)
            load_rows(sp, C2, A["w_down_2"][0])
            for t in range(TT):
                sp.wait_ge(res_done, 8 + t + 1)
                sp.dma_start(out[0].rearrange("(t p) d -> p t d", p=P)[:, t, :], X[:, t, :]).then_inc(out_done, 16)
            sp.wait_ge(out_done, 32)

        @block.scalar
        def _(act):
            split_hi(act, C0)
            split_hi(act, C0 + 1)
            act_rows(act, C0, L2, N_OUT, NT, C3)
            post_square(act, 4, C1)
            norm_act(act, 5, lambda e, t: e.wait_ge(res_done, 8))
            norm_act_hi(act, 5)
            act.wait_ge(norm_out, 32)
            act.dma_start(GAIN2, row_gain(A["g_mlp_post_2"][0])).then_inc(gain2_loaded, 16)

            def up(j, r):
                split_hi(act, C1 + j + 2, r)
                if j % 2 == 1:
                    act.wait_ge(item_used, C1 + j + 1 + 4 * r)
                    act.wait_ge(squared, H0 + j // 2 - 1 + 2 * r)
                    act.activation(two(ACTED[:, j // 2 % 2, :]), PS[:, j // 2 % 2 * 2:j // 2 % 2 * 2 + 2, 0:T], ACT.Relu)\
                        .then_inc(pair_out, 1)
            steps(act, 2 * N_UP, up)
            act.wait_ge(squared, H0 + N_UP)
            act_rows(act, C2, L3, F2 // P, BIG, C3)
            post_square(act, 6, C3)

        @block.vector
        def _(dve):
            for _ in range(H0):
                dve.engine_nop().then_inc(squared, 1)
            split_lo(dve, C0)
            split_lo(dve, C0 + 1)
            dve_rows(dve, C0, L2, N_OUT, NT, C3)
            norm_dve(dve, 4, None)
            dve.wait_ge(gain_loaded, 32)
            post_scale(dve, 0, GAIN)
            norm_dve(dve, 5, "g_mlp_pre_2")

            def square(j, r):
                split_lo(dve, C1 + j + 2, r)
                if j % 2 == 1:
                    dve.wait_ge(pair_out, Q2 + j // 2 + 1 + 2 * r)
                    a = two(ACTED[:, j // 2 % 2, :])
                    dve.tensor_tensor(BIG[:, bass.ds(j - 1 + 4 * r, 2), :], a, a, ALU.mult).then_inc(squared, 1)
            steps(dve, 2 * N_UP, square)
            dve_rows(dve, C2, L3, F2 // P, BIG, C3)
            norm_dve(dve, 6, None)
            dve.wait_ge(gain2_loaded, 16)
            post_scale(dve, 1, GAIN2)

        @block.tensor
        def _(pe):
            assert Q2 % 2 == 0
            pe_rows(pe, C0, L2, N_OUT)
            norm_pe(pe, 5)
            pe.wait_ge(norm_out, 32)
            pe_cols(pe, C1, Q2, N_UP)
            pe.wait_ge(squared, H0 + N_UP)
            pe_rows(pe, C2, L3, F2 // P)
    return ctx


NAMES = ("x", "attn_norm", "w_in", "gdn_conv", "gdn_a_log", "gdn_dt_bias", "gdn_norm", "mlstm_conv", "mlstm_b_i",
         "mlstm_b_f", "mlstm_norm", "rglru_conv", "rglru_conv_b", "rglru_w_a", "rglru_b_a", "rglru_w_x", "rglru_b_x",
         "rglru_lambda", "rwkv_mu", "rwkv_w0", "rwkv_w2", "rwkv_a0", "rwkv_a2", "rwkv_g2", "rwkv_k_k", "rwkv_k_a",
         "rwkv_r_k", "rwkv_ln_w", "rwkv_ln_b", "w_out", "ffn_norm", "ffn_w_gate", "ffn_w_up", "ffn_w_down",
         "final_norm", "w_in_2", "w_out_2", "g_mix_pre_2", "g_mix_post_2", "g_mlp_pre_2", "g_mlp_post_2", "w_up_2",
         "w_down_2", "cmp_pe_2", "phik_w1_2", "phik_w2_2", "phiv_w1_2", "phiv_w2_2", "fox_bias_2", "rel_bias_2")


def kernel(**inputs):
    import concourse.bacc as bacc
    from concourse.bass_utils import run_bass_kernel_spmd

    nc = bacc.Bacc("TRN2", target_bir_lowering=False, num_devices=1)
    arrays = {name: np.ascontiguousarray(inputs[name]) for name in NAMES}
    arrays["const"] = CONST
    arrays["const_first"] = CONST_FIRST
    handles = {}
    for name, a in arrays.items():
        handles[name] = nc.dram_tensor(f"in_{name}", a.shape, mybir.dt.from_np(a.dtype), kind="ExternalInput").ap()
    out = nc.dram_tensor("out", (1, T, D), F32, kind="ExternalOutput").ap()
    build(nc, handles, out)
    r = run_bass_kernel_spmd(nc, [{f"in_{k}": v for k, v in arrays.items()}], core_ids=[0])
    return r.results[0]["out"]
```

```python
from contextlib import ExitStack

import numpy as np

import concourse.bass as bass
from concourse import mybir

F32 = mybir.dt.float32
F32R = mybir.dt.float32r
ALU = mybir.AluOpType
ACT = mybir.ActivationFunctionType

P = 128
T = 256
TT = T // P
D = 2048
KD = D // P
F1 = 5632
F2 = 8192
EPS = 1e-6
RAWS = 4
NEG = -1e30
HUGE8 = -8e30

GROUPS1 = ((0, 8), (2056, 8), (4112, 4), (5136, 7))
GATES1 = (2048, 4104)
GQ, GK, GV, GZ = 0, 4, 8, 12
MQ, MK, MV, MO = 16, 20, 24, 28
RX, RG = 32, 36
WR, WK, WV, WWA, WG = 40, 44, 48, 52, 53
GROUPS2 = ((0, 5), (1304, 6), (2840, 6), (4384, 6))
NSA_GATES, FOX_GATES = 1280, 4376
AQ, AKC, AVC, AKS, AVS, AKW, AVW = 0, 4, 5, 6, 7, 8, 9
BQ, BK, BV = 10, 14, 18
CQ, CK, CV_ = 22, 26, 30
DQ, DK, DV = 34, 38, 42

TABLE0 = (("attn_norm", 16), ("ffn_norm", 16), ("g_mix_pre_2", 16), ("g_mlp_pre_2", 16), ("cmp_pe_2", 16))
TABLE1 = (("gdn_conv", 48), ("mlstm_conv", 32), ("rglru_conv", 16))
TABLE2 = (("rglru_conv_b", 4), ("rglru_b_a", 4), ("rglru_b_x", 4), ("rglru_lambda", 4), ("rwkv_mu", 14),
          ("rwkv_w0", 4), ("rwkv_a0", 4), ("rwkv_k_k", 4), ("rwkv_k_a", 4), ("rwkv_r_k", 4),
          ("rwkv_ln_w", 4), ("rwkv_ln_b", 4), ("gdn_norm", 1), ("mlstm_norm", 4))
TABLES = (TABLE0, TABLE1, TABLE2)


def column_of():
    at, out = 0, {}
    for table in TABLES:
        for name, n in table:
            out[name] = at
            at += n
    return out, at


COL, NCOL = column_of()


def bucket(d):
    edges = (16, 23, 32, 46, 64, 91, 128, 182)
    return d if d < 16 else 15 + sum(d >= e for e in edges)


def constants():
    i = np.arange(P)
    row, col = i[:, None], i[None, :]
    out = {
        "ones": np.ones((P, T)),
        "ones64": (row // 64 == col // 64) * 1.0,
        "causal_T": np.where(row <= col, 0.0, NEG),
        "causal8": np.where(col <= row, 0.0, HUGE8),
    }
    for b in (1, 2, 4, 8, 16, 32, 64):
        out[f"level{b}"] = ((col // b) % 2 == 1) * (row // b == col // b - 1) * 1.0
    row, col = row % 64, col[:, 0:64]
    out["ident64"] = (row == col) * 1.0
    out["strict64_T"] = (row < col) * 1.0
    out["incl64_T"] = (row <= col) * 1.0
    for b in (1, 2, 4, 8, 16, 32):
        out[f"half_level{b}"] = ((col // b) % 2 == 1) * (row // b == col // b - 1) * 1.0
    out["from31"] = (i[:, None] >= 31) * 1.0
    t = np.arange(T)
    out["reset64"] = np.broadcast_to((t % 64 != 0) * 1.0, (P, T))
    out["reset128"] = np.broadcast_to((t % 128 != 0) * 1.0, (P, T))
    dist = 255 - np.arange(384)
    hot = np.zeros((P, 384))
    extra = np.zeros((P, 384))
    for n, d in enumerate(dist):
        hot[bucket(max(d, 0)), n] = 8.0
        count = int(d <= 128) + int(d % 4 == 0) + int(d % 16 == 0)
        extra[:16, n] = 0.0 if d >= 0 else HUGE8
        extra[16:24, n] = 8 * np.log(count) if d >= 0 and count else HUGE8
    first = np.concatenate([np.eye(P), hot, extra], axis=1).astype(np.float32)
    flat = {k: v.reshape(P, -1).astype(np.float32) for k, v in out.items()}
    where, at = {}, 0
    for k, v in flat.items():
        where[k] = (at, v.shape[1])
        at += v.shape[1]
    return np.ascontiguousarray(np.concatenate(list(flat.values()), axis=1)), where, first


CONST, CONST_AT, CONST_FIRST = constants()
NCONST = CONST.shape[1]


class Marks:

    def __init__(self, sem, order):
        self.sem, self.order, self.n = sem, list(order), 0
        assert len(set(self.order)) == len(self.order)

    def did(self, name, ins):
        assert self.order[self.n] == name, (self.order[self.n], name)
        self.n += 1
        ins.then_inc(self.sem, 1)

    def wait(self, eng, name):
        eng.wait_ge(self.sem, self.order.index(name) + 1)


def build(nc, A, out, stop=99):
    ctx = ExitStack()

    def sem(name):
        return ctx.enter_context(nc.semaphore(name))

    def at(name, shape, kib, dt=F32):
        return nc.alloc_sbuf_tensor_at(name, shape, dt, offset=SBUF0 + int(kib * 1024))

    SBUF0 = (nc.sbuf_base + 63) // 64 * 64
    slab = ctx.enter_context(nc.sbuf_tensor("slab", [P, 206 * 256], F32))
    del slab
    X = at("X", [P, TT, D], 0)
    BIG = at("BIG", [P, 64, T], 16)
    NT = at("NT", [P, KD, T], 80)
    CST = at("CST", [P, NCONST], 96)
    NTH = at("NTH", [P, KD, T], 80, F32R)
    NTL = at("NTL", [P, KD, T], 96, F32R)
    LJH = at("LJH", [P, 2, T], 96, F32R)
    LJL = at("LJL", [P, 2, T], 98, F32R)
    PAR = at("PAR", [P, NCOL], 112)
    IDENT_T = at("IDENT", [P, P], 113)
    ST = at("ST", [P, 16], 113.5)
    HC = at("HC", [8, 8], 113.625)
    GT = at("GT", [32, 4, T], 114)
    TMP = at("TMP", [P, TT, D], 118)
    RAW = at("RAW", [P, RAWS, 2048], 134)
    WH = at("WH", [P, 2, 2048], 166, F32R)
    WL = at("WL", [P, 2, 2048], 182, F32R)
    SCRATCH = at("SCRATCH", [P, 4, 4096], 134)
    PS = ctx.enter_context(nc.psum_tensor("PS", [P, 8, 512], F32))

    bias_rows = nc.dram_tensor("bias_rows", (24, 384), F32).ap()
    bias_skew = nc.dram_tensor("bias_skew", (24, P, 384), F32).ap()

    def cst(name, parts=P):
        at, n = CONST_AT[name]
        return CST[0:parts, at:at + n]

    IDENT = IDENT_T[:, :]
    UNIT, ONES64 = cst("ones"), cst("ones64")
    ONES = UNIT[:, 0:P]

    def pick(h, heads):
        return IDENT[0:heads, h:h + 1].broadcast_to([heads, P])

    def par(name, i=0, n=1):
        return PAR[:, COL[name] + i:COL[name] + i + n]

    def spread(columns, n):
        return columns.rearrange("p (k o) -> p k o", o=1).broadcast_to([P, columns.shape[1], n])

    def repeated(block, k):
        return block.rearrange("p (o n) -> p o n", o=1).broadcast_to([P, k, block.shape[1]])

    slot_full = [sem(f"slot_full{i}") for i in range(RAWS)]
    hi_made = sem("hi_made")
    lo_made = sem("lo_made")
    item_used = sem("item_used")
    tile_done = sem("tile_done")
    pair_out = sem("pair_out")
    left_hi = sem("left_hi")
    left_lo = sem("left_lo")
    sq_done = sem("sq_done")
    mean_done = sem("mean_done")
    sd_done = sem("sd_done")
    rs_done = sem("rs_done")
    xn_done = sem("xn_done")
    turned = sem("turned")
    norm_gained = sem("norm_gained")
    norm_hi = sem("norm_hi")
    norm_out = sem("norm_out")

    def steps(eng, count, body, peel=0, lead=False):
        for j in range(peel):
            body(j, 0)
        count -= peel
        rounds = count // 4 - (1 if lead and count % 4 < 2 else 0)
        if rounds > 1:
            with eng.Fori(0, rounds) as r:
                for j in range(4):
                    body(peel + j, r)
        else:
            rounds = 0
        for j in range(4 * rounds, count):
            body(peel + j, 0)

    def half_columns(w):
        return w.rearrange("p (k n) -> p k n", k=8)

    def narrow(w):
        return w.rearrange("p (k n) -> p k n", k=KD)

    def load(sp, s, r, dst, src):
        if s >= RAWS:
            sp.wait_ge(lo_made, s + 4 * r - RAWS + 1)
        sp.dma_start(dst, src).then_inc(slot_full[s % RAWS], 16)

    def load_cols(sp, n0, w, c0, pairs):
        wv = w.rearrange("(k p) n -> p k n", p=P)

        def one(j, r):
            load(sp, n0 + j, r, half_columns(RAW[:, (n0 + j) % RAWS, :]),
                 wv[:, 8 * (j % 2):8 * (j % 2) + 8, bass.ds(c0 + (j // 2) * 256 + 512 * r, 256)])
        steps(sp, 2 * pairs, one, peel=4 if n0 < RAWS else 0)
        return n0 + 2 * pairs

    def load_gate_up(sp, n0, wa, wb, units):
        views = [w.rearrange("(k p) n -> p k n", p=P) for w in (wa, wb)]

        def one(j, r):
            load(sp, n0 + j, r, half_columns(RAW[:, (n0 + j) % RAWS, :]),
                 views[j % 4 // 2][:, 8 * (j % 2):8 * (j % 2) + 8, bass.ds((j // 4) * 256 + 256 * r, 256)])
        steps(sp, 4 * units, one)
        return n0 + 4 * units

    def load_rows(sp, n0, w, first=0, last=None):
        wv = w.rearrange("(g p) n -> g p n", p=P)
        count = w.shape[0] // P
        steps(sp, (last or count) - first,
              lambda j, r: load(sp, n0 + first + j, r, RAW[:, (n0 + first + j) % RAWS, :],
                                wv[bass.ds(first + j + 4 * r, 1)].rearrange("o p n -> (o p) n")))
        return n0 + count

    def load_narrow(sp, n0, w, c0):
        load(sp, n0, 0, narrow(RAW[:, n0 % RAWS, :]), w.rearrange("(k p) n -> p k n", p=P)[:, :, c0:c0 + P])
        return n0 + 1

    def split_hi(act, s, r=0):
        act.wait_ge(slot_full[s % RAWS], 16 * (s // RAWS + 1 + r))
        if s >= 2:
            act.wait_ge(item_used, s + 4 * r - 1)
        act.activation(WH[:, s % 2, :], RAW[:, s % RAWS, :], ACT.Copy).then_inc(hi_made, 1)

    def split_lo(dve, s, r=0):
        dve.wait_ge(hi_made, s + 4 * r + 1)
        dve.tensor_tensor(WL[:, s % 2, :], RAW[:, s % RAWS, :], WH[:, s % 2, :].bitcast(F32), ALU.subtract)\
            .then_inc(lo_made, 1)

    def left_split_hi(act, n0, l0, j, r, src):
        if j >= 2:
            act.wait_ge(item_used, n0 + j + 4 * r - 1)
        act.activation(LJH[:, (l0 + j) % 2, :].rearrange("p (o t) -> p o t", o=1), src[:, bass.ds(j + 4 * r, 1), :],
                       ACT.Copy).then_inc(left_hi, 1)

    def left_split_lo(dve, l0, j, r, src):
        dve.wait_ge(left_hi, l0 + j + 4 * r + 1)
        slot = (l0 + j) % 2
        dve.tensor_tensor(LJL[:, slot, :].rearrange("p (o t) -> p o t", o=1), src[:, bass.ds(j + 4 * r, 1), :],
                          LJH[:, slot, :].bitcast(F32).rearrange("p (o t) -> p o t", o=1), ALU.subtract)\
            .then_inc(left_lo, 1)

    def pe_col_item(pe, s, r, half, bank, fresh=None):
        pe.wait_ge(lo_made, s + 4 * r + 1)
        wh, wl = half_columns(WH[:, s % 2, :]), half_columns(WL[:, s % 2, :])
        if fresh is not None:
            n_before = 8 * q_turn[fresh]
            pe.wait_ge(norm_gained, n_before + bank + 2)
        for kk in range(8):
            if fresh is not None and kk % 4 == 0:
                pe.wait_ge(norm_out, n_before + 4 * half + kk // 2 + 2)
            for c in range(2):
                cols = slice(c * P, (c + 1) * P)
                for n, (w, x) in enumerate(((wh, NTH), (wl, NTH), (wh, NTL))):
                    mm = nc.tensor.matmul(PS[:, bank + c, 0:T], w[:, kk, cols], x[:, 8 * half + kk, :],
                                          start=(half == 0 and kk == 0 and n == 0),
                                          stop=(half == 1 and kk == 7 and n == 2), skip_group_check=True)
        mm.then_inc(item_used, 1)

    def pe_cols(pe, n0, q0, pairs, fresh=None):
        def one(j, r):
            q = q0 + j // 2
            if j % 2 == 0 and q >= 2:
                pe.wait_ge(pair_out, q - 1 + 2 * r)
            pe_col_item(pe, n0 + j, r, j % 2, 2 * (q % 2), fresh if j < 2 and isinstance(r, int) else None)
        steps(pe, 2 * pairs, one, peel=4 if fresh is not None else 0)

    def pe_narrow(pe, s, bank):
        pe.wait_ge(lo_made, s + 1)
        wh, wl = narrow(WH[:, s % 2, :]), narrow(WL[:, s % 2, :])
        for k in range(KD):
            for n, (w, x) in enumerate(((wh, NTH), (wl, NTH), (wh, NTL))):
                mm = nc.tensor.matmul(PS[:, bank, 0:T], w[:, k, :], x[:, k, :],
                                      start=(k == 0 and n == 0), stop=(k == KD - 1 and n == 2))
        mm.then_inc(item_used, 1)

    def act_cols(act, n0, q0, pairs, tile0, end):
        def one(j, r):
            if n0 + j + 2 < end:
                split_hi(act, n0 + j + 2, r)
            if j % 2 == 1:
                q = q0 + j // 2
                act.wait_ge(item_used, n0 + j + 4 * r + 1)
                act.activation(BIG[:, bass.ds(tile0 + j - 1 + 4 * r, 2), :], PS[:, 2 * (q % 2):2 * (q % 2) + 2, 0:T],
                               ACT.Copy).then_inc(pair_out, 1)
        steps(act, 2 * pairs, one, lead=(n0 + 2 * pairs + 2 > end))

    def dve_ahead(dve, n0, count, end):
        def one(j, r):
            if n0 + j + 2 < end:
                split_lo(dve, n0 + j + 2, r)
        steps(dve, count, one, lead=(n0 + count + 2 > end))

    def pe_rows(pe, n0, l0, count):
        def one(j, r):
            s = n0 + j
            pe.wait_ge(lo_made, s + 4 * r + 1)
            pe.wait_ge(left_lo, l0 + j + 4 * r + 1)
            sl, sw = (l0 + j) % 2, s % 2
            start = isinstance(r, int) and j == 0
            stop = isinstance(r, int) and j == count - 1
            for t in range(TT):
                tok = slice(t * P, (t + 1) * P)
                for n, (x, w) in enumerate(((LJH, WH), (LJH, WL), (LJL, WH))):
                    for c in range(4):
                        mm = nc.tensor.matmul(PS[:, 4 * t + c, :], x[:, sl, tok], w[:, sw, c * 512:(c + 1) * 512],
                                              start=(start and n == 0), stop=(stop and n == 2),
                                              skip_group_check=True)
                if t == 0 and stop:
                    mm.then_inc(tile_done, 1)
            mm.then_inc(item_used, 1)
        steps(pe, count, one, peel=4, lead=True)

    def act_rows(act, n0, l0, count, src, end, then=None):
        for j in range(2):
            left_split_hi(act, n0, l0, j, 0, src)
        if then:
            then()

        def one(j, r):
            if n0 + j + 2 < end:
                split_hi(act, n0 + j + 2, r)
            if j + 2 < count:
                left_split_hi(act, n0, l0, j + 2, r, src)
        steps(act, count, one, lead=True)

    def dve_rows(dve, n0, l0, count, src, end, then=None):
        for j in range(2):
            left_split_lo(dve, l0, j, 0, src)
        if then:
            then()

        def one(j, r):
            if n0 + j + 2 < end and j != count - 1:
                split_lo(dve, n0 + j + 2, r)
            if j + 2 < count:
                left_split_lo(dve, l0, j + 2, r, src)
        steps(dve, count, one, lead=True)

    NF = BIG[:, 0:KD, :]

    def chunk_of(x, i):
        return x[:, 4 * (i // 2):4 * (i // 2) + 4, (i % 2) * P:(i % 2 + 1) * P]

    def norm_act(act, q, ready):
        for t in range(TT):
            ready(act, t)
            act.activation(TMP[:, t, :], X[:, t, :], ACT.Square, accum_out=ST[:, t:t + 1]).then_inc(sq_done, 1)
        act.wait_ge(mean_done, q + 1)
        act.activation(ST[:, 4:6], ST[:, 2:4], ACT.Sqrt).then_inc(sd_done, 1)

    def norm_act_hi(act, q):
        n = q_turn[q]
        for i in range(8):
            act.wait_ge(norm_gained, 8 * n + i + 1)
            act.activation(chunk_of(NTH, i), chunk_of(NF, i), ACT.Copy).then_inc(norm_hi, 1)

    def norm_dve(dve, q, gain, between=None):
        dve.wait_ge(sq_done, 2 * q + 2)
        dve.tensor_scalar(ST[:, 2:4], ST[:, 0:2], 1.0 / D, EPS, ALU.mult, ALU.add).then_inc(mean_done, 1)
        dve.wait_ge(sd_done, q + 1)
        dve.reciprocal(ST[:, 6:8], ST[:, 4:6]).then_inc(rs_done, 1)
        dve.wait_ge(rs_done, q + 1)
        if gain is None:
            return
        for t in range(TT):
            dve.tensor_scalar(TMP[:, t, :], X[:, t, :], ST[:, 6 + t:7 + t], None, ALU.mult).then_inc(xn_done, 1)
        n = q_turn[q]
        if between:
            between()

        def low(i):
            dve.wait_ge(norm_hi, 8 * n + i + 1)
            dve.tensor_tensor(chunk_of(NTL, i), chunk_of(NF, i), chunk_of(NTH[:, :, :].bitcast(F32), i), ALU.subtract)\
                .then_inc(norm_out, 1)
        for i in range(8):
            dve.wait_ge(turned, 8 * n + i + 1)
            dve.tensor_tensor(chunk_of(NF, i), PS[:, i, :].rearrange("p (k t) -> p k t", k=4),
                              spread(par(gain, 4 * (i // 2), 4), P), ALU.mult).then_inc(norm_gained, 1)
            if i:
                low(i - 1)
        low(7)

    def norm_pe(pe, q):
        n = q_turn[q]
        pe.wait_ge(xn_done, 2 * n + 2)
        for i in range(8):
            t, b = i % 2, i // 2
            for k in range(4):
                mm = nc.tensor.transpose(PS[:, i, k * P:(k + 1) * P],
                                         TMP[:, t, (4 * b + k) * P:(4 * b + k + 1) * P], IDENT)
            mm.then_inc(turned, 1)

    q_turn = {0: 0, 1: 1, 3: 2, 5: 3}

    in_loaded = sem("in_loaded")
    first_loaded = sem("first_constants_loaded")
    par_loaded = sem("par_loaded")
    ident_made = sem("ident_made")
    par_turned = sem("par_turned")
    par_out = sem("par_out")
    bias_made = sem("bias_made")
    bias_out = sem("bias_out")
    bias_moved = sem("bias_moved")
    gates_out = sem("gates_out")
    gates_moved = sem("gates_moved")

    N_OUT = D // P
    NPAR = 16 * (sum(len(t) for t in TABLES) + 6)
    w_in = A["w_in"][0]
    NI = 2 * sum(n for _, n in GROUPS1)
    IA = NI + 2
    B0 = IA
    flat2 = lambda v: v.rearrange("p a b -> p (a b)")
    PROWS = [BIG[:, 16 + i, 0:P] for i in range(3)]
    FIRSTC = flat2(BIG[:, 20:24, :])[:, 0:P + 768]
    HOT8, EXTRA8 = FIRSTC[0:32, P:P + 384], FIRSTC[0:24, P + 384:P + 768]
    BIASR = flat2(BIG[:, 24:26, :])[0:24, 0:384]
    RB = BIG[0:32, 26, 0:24]

    def load_table(eng, b):
        at = 0
        for name, n in TABLES[b]:
            src = A[name]
            letters = " ".join("abcd"[:len(src.shape)])
            flat = src.rearrange(f"{letters} -> ({letters})")
            eng.dma_start(PROWS[b][at:at + n, :], flat.rearrange("(r c) -> r c", c=P)).then_inc(par_loaded, 16)
            at += n

    with nc.Block() as block:
        @block.sync
        def _(sp):
            sp.dma_start(X[:, :, :], A["x"][0].rearrange("(t p) d -> p t d", p=P)).then_inc(in_loaded, 16)
            sp.dma_start(FIRSTC, A["const_first"]).then_inc(first_loaded, 16)
            load_table(sp, 0)
            load_table(sp, 1)
            sp.dma_start(RB, A["rel_bias_2"]).then_inc(par_loaded, 16)
            for n, name in enumerate(("gdn_a_log", "gdn_dt_bias", "mlstm_b_i", "mlstm_b_f")):
                sp.dma_start(HC[0:4, n:n + 1], A[name][0].rearrange("(h o) -> h o", o=1)).then_inc(par_loaded, 16)
            sp.dma_start(HC[0:8, 4:5], A["fox_bias_2"][0].rearrange("(h o) -> h o", o=1)).then_inc(par_loaded, 16)
            n = 0
            for c, pairs in GROUPS1:
                n = load_cols(sp, n, w_in, c, pairs)
            for c in GATES1:
                n = load_narrow(sp, n, w_in, c)
            sp.wait_ge(gates_out, 1)
            for m in range(2):
                sp.dma_start(GT[0:4, 2 + m, :], GT[4:8, m, :]).then_inc(gates_moved, 16)
            sp.wait_ge(gates_moved, 32)

        @block.scalar
        def _(act):
            load_table(act, 2)
            norm_act(act, 0, lambda e, t: e.wait_ge(in_loaded, 16))
            split_hi(act, 0)
            split_hi(act, 1)
            norm_act_hi(act, 0)
            act.wait_ge(bias_out, 1)
            act.dma_start(bias_rows, BIASR).then_inc(bias_moved, 16)
            act.wait_ge(bias_moved, 16)
            act.dma_start(bias_skew, bias_rows.rearrange("h (o i) -> h o i", o=1).broadcast_to([24, P, 384]))\
                .then_inc(bias_moved, 16)
            act.wait_ge(norm_out, 8)
            at, n = 0, 0
            for _, pairs in GROUPS1:
                act_cols(act, n, n // 2, pairs, at, IA)
                n, at = n + 2 * pairs, at + 2 * pairs
            act.wait_ge(item_used, IA)
            act.activation(GT[0:8, 0:2, :], PS[0:8, 6:8, 0:T], ACT.Copy).then_inc(gates_out, 1)
            act.wait_ge(bias_moved, 32)

        @block.vector
        def _(dve):
            dve.wait_ge(first_loaded, 16)
            dve.tensor_copy(IDENT, FIRSTC[:, 0:P]).then_inc(ident_made, 1)
            at = 0
            for b, table in enumerate(TABLES):
                n = sum(k for _, k in table)
                dve.wait_ge(par_turned, b + 1)
                dve.tensor_copy(PAR[:, at:at + n], PS[:, 4 + b, 0:n]).then_inc(par_out, 1)
                at += n
            dve.wait_ge(bias_made, 1)
            dve.tensor_tensor(BIASR, PS[0:24, 7, 0:384], EXTRA8, ALU.add).then_inc(bias_out, 1)
            dve.wait_ge(par_out, 3)

            def first_items():
                split_lo(dve, 0)
                split_lo(dve, 1)
            norm_dve(dve, 0, "attn_norm", first_items)
            dve_ahead(dve, 0, NI, IA)

        @block.tensor
        def _(pe):
            pe.wait_ge(ident_made, 1)
            pe.wait_ge(par_loaded, NPAR)
            for b, table in enumerate(TABLES):
                n = sum(k for _, k in table)
                nc.tensor.transpose(PS[:, 4 + b, 0:n], PROWS[b][0:n, :], IDENT[0:n, 0:n]).then_inc(par_turned, 1)
            nc.tensor.matmul(PS[0:24, 7, 0:384], RB, HOT8, start=True, stop=True).then_inc(bias_made, 1)
            pe.wait_ge(par_out, 3)
            pe.wait_ge(bias_out, 1)
            norm_pe(pe, 0)
            n = 0
            for _, pairs in GROUPS1:
                pe_cols(pe, n, n // 2, pairs, 0 if n == 0 else None)
                n += 2 * pairs
            for m in range(2):
                pe_narrow(pe, NI + m, 6 + m)
    if stop == 0:
        return ctx

    R_ = SCRATCH[:, :, :].rearrange("p s n -> p (s n)")
    T_ = TMP[:, :, :].rearrange("p t n -> p (t n)")

    def area(base, at, k, n=P):
        return base[:, at:at + k * n].rearrange("p (k n) -> p k n", k=k)

    CV = area(R_, 0, 24, T)
    CONVS = ([("gdn_conv", 12, j, GQ + j) for j in range(12)] + [("mlstm_conv", 8, j, MQ + j) for j in range(8)]
             + [("rglru_conv", 4, j, RX + j) for j in range(4)])
    SPARE = BIG[:, 54:64, :]
    ROW = lambda n: SPARE[0:4, n, :]
    O8 = BIG[:, 16:24, :]

    conv_lead = sem("conv_lead")
    conv_tap = sem("conv_tap")
    conv_silu = sem("conv_silu")
    NCV = 12
    pool_done = sem("pool_done")
    QK_CONVOLVED = 7
    const_loaded = sem("const_loaded")
    with nc.Block() as block:
        @block.sync
        def _(sp):
            sp.dma_start(CST[:, :], A["const"]).then_inc(const_loaded, 16)
            sp.wait_ge(const_loaded, 16)

        @block.scalar
        def _(act):
            for i, (name, n, j, u) in enumerate(CONVS[:NCV]):
                act.activation(CV[:, i, :], BIG[:, u, :], ACT.Copy, scale=par(name, 3 * n + j)).then_inc(conv_lead, 1)
            for g in range(3):
                act.wait_ge(conv_tap, 2 * NCV + 4 * g + 4)
                act.activation(CV[:, 4 * g:4 * g + 4, :], CV[:, 4 * g:4 * g + 4, :], ACT.Silu).then_inc(conv_silu, 1)

        @block.vector
        def _(dve):
            for step, tap in enumerate((2, 1, 0)):
                for i, (name, n, j, u) in enumerate(CONVS[:NCV]):
                    s = 3 - tap
                    if step == 0:
                        dve.wait_ge(conv_lead, i + 1)
                    else:
                        dve.wait_ge(conv_tap, (step - 1) * NCV + i + 1)
                    dve.scalar_tensor_tensor(out=CV[:, i, s:T], in0=BIG[:, u, 0:T - s], scalar=par(name, tap * n + j),
                                             in1=CV[:, i, s:T], op0=ALU.mult, op1=ALU.add).then_inc(conv_tap, 1)

    def marks(name, order):
        return Marks(sem(name), order)

    def m3(at, k=8):
        return area(R_, 6144 + at * 1024, k)
    EGB, DT_, AT_, LT_, QD, KDT, XI, XT, CT, CX = [m3(i) for i in range(10)]
    EGB, QD, KDT = [v.rearrange("p m t -> p (m t)").rearrange("p (h t) -> p h t", h=4) for v in (EGB, QD, KDT)]
    fl = lambda v: v.rearrange("p a b -> p (a b)")
    VB, KN, VNEW = [fl(BIG[:, 4 * i:4 * i + 4, :]).rearrange("p (m t) -> p m t", m=8) for i in range(3)]
    SQ8 = area(T_, 0, 8, T)
    RR, SS = [area(T_, 512 * i, 4) for i in range(2)]
    COLS = SPARE[:, 9, 0:16]
    SM = SPARE[:, 9, 16:32]
    NB = SPARE[:, 9, 32:40]
    MIXED, DIFF = BIG[:, 40:54, :], NT[:, 0:14, :]
    LEVELS = (1, 2, 4, 8, 16, 32, 64)

    def ps_m(bank, nb=2):
        return PS[:, bank:bank + nb, :].rearrange("p b (m t) -> p (b m) t", t=P)

    def ps_t(bank, nb=2):
        return PS[:, bank:bank + nb, :].rearrange("p b (m t) -> p (b m) t", t=T)

    RSC = ST[:, 0:16]

    def token_sums(dst, src, heads):
        w = heads.shape[1]
        for n in range(2 * src.shape[1]):
            last = nc.tensor.matmul(dst[:, w * n:w * n + w], src[:, n // 2, (n % 2) * P:(n % 2 + 1) * P], heads,
                                    start=True, stop=True)
        return last

    def to_channels(dst, w):
        for n in range(2 * dst.shape[1]):
            for e in range(w):
                col = RSC[:, w * n + e:w * n + e + 1].broadcast_to([P, P // w])
                last = nc.tensor.matmul(dst[e * P // w:(e + 1) * P // w, n // 2, (n % 2) * P:(n % 2 + 1) * P], col,
                                        IDENT, start=True, stop=True)
        return last

    def ps_c(bank):
        return PS[:, bank:bank + 2, :].rearrange("p b (m t) -> p (b m) t", t=64)

    gp = marks("gdn_products", ["ssq", "cols", "rsb", "rows", "kkqk", "cx0", "v_nat", "k_nat"]
               + [f"{s}{l}" for l in range(1, 7) for s in (("cx", "y", "yt") if l < 6 else ("cx", "yt"))] + ["vn0", "o0", "ks", "vn1", "o1"])
    ga = marks("gdn_scalar", ["beta", "ealog", "ex1", "ln", "sd", "egb", "dt", "kd"] + [f"cxs{l}" for l in range(1, 7)]
               + ["vn0s", "s", "o0s", "vn1s", "o1s"])
    gv = marks("gdn_vector", ["sq", "xg", "ax", "e1", "sp", "g", "scan", "ms", "rs", "qk_norm", "cols_out", "nb", "dt",
                              "gl", "dl", "lt1", "lt", "ct0", "at", "x0", "ct1", "vb", "kn"]
               + [s for l in range(1, 6) for s in (f"ct{l + 1}", f"x{l}") + (("qd", "kdt") if l == 1 else ())
                  + (f"xt{l}",)] + ["xt6", "r1"])
    with nc.Block() as block:
        @block.scalar
        def _(act):
            ga.did("beta", act.activation(ROW(0), GT[0:4, 2, :], ACT.Sigmoid))
            ga.did("ealog", act.activation(HC[0:4, 5:6], HC[0:4, 0:1], ACT.Exp))
            gv.wait(act, "ax")
            ga.did("ex1", act.activation(ROW(2), ROW(2), ACT.Exp, scale=-1.0))
            gv.wait(act, "e1")
            ga.did("ln", act.activation(ROW(2), ROW(2), ACT.Ln))
            gv.wait(act, "ms")
            ga.did("sd", act.activation(RSC, RSC, ACT.Sqrt))
            gv.wait(act, "gl")
            ga.did("egb", act.activation(EGB, ps_t(4), ACT.Exp))
            gv.wait(act, "dt")
            ga.did("dt", act.activation(DT_, DT_, ACT.Exp))
            gv.wait(act, "dl")
            ga.did("kd", act.activation(SM, SM, ACT.Exp))
            for l in range(1, 7):
                gp.wait(act, f"cx{l}")
                ga.did(f"cxs{l}", act.activation(CX, ps_m(0), ACT.Copy))
                if l == 4:
                    act.wait_ge(pool_done, QK_CONVOLVED)
                    act.activation(CV[:, 12:20, :], CV[:, 12:20, :], ACT.Silu).then_inc(conv_silu, 1)
            gp.wait(act, "vn0")
            ga.did("vn0s", act.activation(VNEW[:, 0:4, :], ps_m(6, 1), ACT.Copy))
            gp.wait(act, "o0")
            ga.did("s", act.activation(SS, ps_m(0, 1), ACT.Copy))
            ga.did("o0s", act.activation(O8[:, 0:4, 0:P], ps_m(7, 1), ACT.Copy))
            gp.wait(act, "vn1")
            ga.did("vn1s", act.activation(VNEW[:, 4:8, :], ps_m(6, 1), ACT.Copy))
            gp.wait(act, "o1")
            ga.did("o1s", act.activation(O8[:, 0:4, P:T], ps_m(2, 1), ACT.Copy))

        @block.vector
        def _(dve):
            dve.wait_ge(conv_silu, 3)
            gv.did("sq", dve.tensor_tensor(SQ8, CV[:, 0:8, :], CV[:, 0:8, :], ALU.mult))
            gv.did("xg", dve.tensor_scalar(ROW(1), GT[0:4, 0, :], HC[0:4, 1:2], None, ALU.add))
            gv.wait(dve, "xg")
            gv.did("ax", dve.scalar_tensor_tensor(out=ROW(2), in0=ROW(1), scalar=-1.0, in1=ROW(1), op0=ALU.mult, op1=ALU.max))
            ga.wait(dve, "ex1")
            gv.did("e1", dve.tensor_scalar(ROW(2), ROW(2), 1.0, None, ALU.add))
            ga.wait(dve, "ln")
            gv.did("sp", dve.scalar_tensor_tensor(out=ROW(3), in0=ROW(1), scalar=0.0, in1=ROW(2),
                                                  op0=ALU.max, op1=ALU.add))
            gv.wait(dve, "sp")
            gv.did("g", dve.tensor_scalar(ROW(4), ROW(3), HC[0:4, 5:6], -1.0, ALU.mult, ALU.mult))
            gv.wait(dve, "g")
            gv.did("scan", dve.tensor_tensor_scan(ROW(5), cst("reset128", 4), ROW(4), 0.0, ALU.mult, ALU.add))
            gp.wait(dve, "ssq")
            gv.did("ms", dve.tensor_scalar(RSC, PS[:, 7, T:T + 16], EPS, None, ALU.add))
            ga.wait(dve, "sd")
            gv.did("rs", dve.reciprocal(RSC, RSC))
            gp.wait(dve, "rsb")
            dve.scalar_tensor_tensor(out=fl(CV[:, 0:4, :]), in0=fl(CV[:, 0:4, :]), scalar=float(P) ** -0.5,
                                     in1=fl(ps_t(0)), op0=ALU.mult, op1=ALU.mult)
            gv.did("qk_norm", dve.tensor_tensor(CV[:, 4:8, :], CV[:, 4:8, :], ps_t(2), ALU.mult))
            gp.wait(dve, "cols")
            gv.did("cols_out", dve.tensor_copy(COLS, PS[:, 6, 0:16]))
            gv.wait(dve, "cols_out")
            gv.did("nb", dve.tensor_scalar(NB, COLS[:, 8:16], -1.0, None, ALU.mult))
            gp.wait(dve, "rows")
            for m in range(8):
                c, h = m // 4, m % 4
                last = dve.scalar_tensor_tensor(out=DT_[:, m, :], in0=ps_t(4)[:, h, c * P:(c + 1) * P],
                                                scalar=COLS[:, m:m + 1], in1=cst("causal_T"),
                                                op0=ALU.subtract, op1=ALU.add)
            gv.did("dt", last)
            ends = ps_t(4).rearrange("p h (c t) -> p c h t", c=2)[:, :, :, P - 1]
            gv.did("gl", dve.tensor_copy(SM[:, 8:16].rearrange("p (c h) -> p c h", c=2), ends))
            gv.wait(dve, "gl")
            gv.did("dl", dve.tensor_tensor(SM[:, 0:8], SM[:, 8:16], COLS[:, 0:8], ALU.subtract))
            gp.wait(dve, "kkqk")
            ga.wait(dve, "dt")
            gv.did("lt1", dve.tensor_tensor(LT_, ps_m(0), DT_, ALU.mult))
            gv.wait(dve, "lt1")
            for c in range(2):
                last = dve.tensor_tensor(LT_[:, 4 * c:4 * c + 4, :], LT_[:, 4 * c:4 * c + 4, :],
                                         ps_t(6)[:, :, c * P:(c + 1) * P], ALU.mult)
            gv.did("lt", last)
            gv.wait(dve, "lt")
            gv.did("ct0", dve.tensor_tensor(CT, LT_, repeated(cst("level1"), 8), ALU.mult))
            gv.did("at", dve.tensor_tensor(AT_, ps_m(2), DT_, ALU.mult))
            gp.wait(dve, "cx0")
            dve.tensor_tensor(XI, repeated(IDENT, 8), ps_m(0), ALU.subtract)
            gv.did("x0", dve.tensor_tensor(XT, repeated(IDENT, 8), CT, ALU.subtract))
            gv.wait(dve, "x0")
            gv.did("ct1", dve.tensor_tensor(CT, LT_, repeated(cst("level2"), 8), ALU.mult))
            gp.wait(dve, "v_nat")
            gv.did("vb", dve.tensor_tensor(VB, ps_m(6), spread(COLS[:, 8:16], P), ALU.mult))
            gp.wait(dve, "k_nat")
            ga.wait(dve, "kd")
            gv.did("kn", dve.tensor_tensor(KN, ps_m(4), spread(SM[:, 0:8], P), ALU.mult))
            for l in range(1, 7):
                if l < 6:
                    gp.wait(dve, f"cx{l}")
                    gv.did(f"ct{l + 1}", dve.tensor_tensor(CT, LT_, repeated(cst(f"level{LEVELS[l + 1]}"), 8), ALU.mult))
                    gp.wait(dve, f"y{l}")
                    gv.did(f"x{l}", dve.tensor_tensor(XI, XI, ps_m(2), ALU.subtract))
                if l == 1:
                    ga.wait(dve, "egb")
                    gv.did("qd", dve.tensor_tensor(QD, CV[:, 0:4, :], EGB, ALU.mult))
                    gv.did("kdt", dve.tensor_tensor(KDT, CV[:, 4:8, :], EGB, ALU.mult))
                gp.wait(dve, f"yt{l}")
                gv.did(f"xt{l}", dve.tensor_tensor(XT, XT, ps_m(4), ALU.subtract))
            gp.wait(dve, "ks")
            for h in range(4):
                last = dve.scalar_tensor_tensor(out=RR[:, h, :], in0=ps_m(1, 1)[:, h, :], scalar=NB[:, 4 + h:5 + h],
                                                in1=VB[:, 4 + h, :], op0=ALU.mult, op1=ALU.add)
            gv.did("r1", last)

        @block.gpsimd
        def _(pool):
            def did(ins):
                done[0] += 1
                ins.then_inc(pool_done, 1)
                pool.wait_ge(pool_done, done[0])

            done = [0]
            for name, tiles, u, at in (("mlstm_conv", 8, MQ, 12), ("rglru_conv", 4, RX, 20)):
                dst, src, tap_out = CV[:, at:at + tiles, :], BIG[:, u:u + tiles, :], NT[:, 0:tiles, :]
                did(pool.tensor_tensor(dst, src, spread(par(name, 3 * tiles, tiles), T), ALU.mult))
                for tap in (2, 1, 0):
                    s = 3 - tap
                    did(pool.tensor_tensor(tap_out[:, :, s:T], src[:, :, 0:T - s],
                                           spread(par(name, tap * tiles, tiles), T - s), ALU.mult))
                    did(pool.tensor_tensor(dst[:, :, s:T], dst[:, :, s:T], tap_out[:, :, s:T], ALU.add))
                if name == "rglru_conv":
                    did(pool.tensor_tensor(dst, dst, spread(par("rglru_conv_b", 0, 4), T), ALU.add))
                else:
                    assert done[0] == QK_CONVOLVED
            did(pool.memset(DIFF[:, :, 0:1], 0.0))
            did(pool.tensor_tensor(DIFF[:, :, 0:1], DIFF[:, :, 0:1], MIXED[:, :, 0:1], ALU.subtract))
            did(pool.tensor_tensor(DIFF[:, :, 1:T], MIXED[:, :, 0:T - 1], MIXED[:, :, 1:T], ALU.subtract))
            did(pool.tensor_tensor(DIFF, DIFF, spread(par("rwkv_mu", 0, 14), T), ALU.mult))
            did(pool.tensor_tensor(MIXED, MIXED, DIFF, ALU.add))

        @block.tensor
        def _(pe):
            mmul = nc.tensor.matmul

            def each(dst, lhs, rhs, ms):
                for n, m in enumerate(ms):
                    last = mmul(dst[:, n, :], lhs(m), rhs(m), start=True, stop=True)
                return last

            def turn(dst, src, ms):
                for n, m in enumerate(ms):
                    last = nc.tensor.transpose(dst[:, n, :], src(m), IDENT)
                return last

            chunk = lambda base, m: CV[:, base + m % 4, (m // 4) * P:(m // 4 + 1) * P]
            gv.wait(pe, "sq")
            gp.did("ssq", token_sums(PS[:, 7, T:T + 16], SQ8, UNIT[:, 0:1]))
            gv.wait(pe, "scan")
            ga.wait(pe, "beta")
            for n, row in enumerate((ROW(5), ROW(0))):
                for c in range(2):
                    last = nc.tensor.transpose(PS[:, 6, 8 * n + 4 * c:8 * n + 4 * c + 4], row[:, c * P:(c + 1) * P],
                                               IDENT[0:4, 0:4])
            gp.did("cols", last)
            gv.wait(pe, "rs")
            gp.did("rsb", to_channels(ps_t(0, 4), 1))
            gv.wait(pe, "cols_out")
            for n, row in enumerate((ROW(5), ROW(0))):
                for h in range(4):
                    last = mmul(ps_t(4 + 2 * n)[:, h, :], pick(h, 4), row, start=True, stop=True)
            gp.did("rows", last)
            gv.wait(pe, "qk_norm")
            each(ps_m(0), lambda m: chunk(4, m), lambda m: chunk(4, m), range(8))
            gp.did("kkqk", each(ps_m(2), lambda m: chunk(4, m), lambda m: chunk(0, m), range(8)))
            gv.wait(pe, "ct0")
            gp.did("cx0", turn(ps_m(0), lambda m: CT[:, m, :], range(8)))
            gp.did("v_nat", turn(ps_m(6), lambda m: chunk(8, m), range(8)))
            ga.wait(pe, "egb")
            gp.did("k_nat", turn(ps_m(4), lambda m: chunk(4, m), range(8)))
            for l in range(1, 7):
                gv.wait(pe, f"x{l - 1}" if l > 1 else "ct1")
                gp.did(f"cx{l}", each(ps_m(0), lambda m: CT[:, m, :], lambda m: XI[:, m, :], range(8)))
                ga.wait(pe, f"cxs{l}")
                gv.wait(pe, f"xt{l - 1}" if l > 1 else "kn")
                if l < 6:
                    gp.did(f"y{l}", each(ps_m(2), lambda m: XT[:, m, :], lambda m: CX[:, m, :], range(8)))
                gp.did(f"yt{l}", each(ps_m(4), lambda m: CX[:, m, :], lambda m: XT[:, m, :], range(8)))
            gv.wait(pe, "xt6")
            gp.did("vn0", each(ps_m(6, 1), lambda m: XT[:, m, :], lambda m: VB[:, m, :], range(4)))
            ga.wait(pe, "vn0s")
            each(ps_m(7, 1), lambda m: VNEW[:, m, :], lambda m: AT_[:, m, :], range(4))
            gp.did("o0", each(ps_m(0, 1), lambda m: KN[:, m, :], lambda m: VNEW[:, m, :], range(4)))
            ga.wait(pe, "s")
            gp.did("ks", each(ps_m(1, 1), lambda m: KDT[:, m, P:T], lambda m: SS[:, m, :], range(4)))
            gv.wait(pe, "r1")
            gp.did("vn1", each(ps_m(6, 1), lambda m: XT[:, 4 + m, :], lambda m: RR[:, m, :], range(4)))
            ga.wait(pe, "vn1s")
            for h in range(4):
                mmul(ps_m(2, 1)[:, h, :], SS[:, h, :], QD[:, h, P:T], start=True, stop=False)
                last = mmul(ps_m(2, 1)[:, h, :], VNEW[:, 4 + h, :], AT_[:, 4 + h, :], start=False, stop=True)
            gp.did("o1", last)
    if stop == 1:
        return ctx

    lp = marks("mlstm_products", ["cols", "rows", "kq", "v_nat", "den_num"])
    la = marks("mlstm_scalar", ["ex1", "ln", "em", "sig", "exp", "ad"])
    lv = marks("mlstm_vector", ["i", "xf", "ax", "e1", "lf", "scan", "c", "m", "nm", "bm", "cols_out", "e", "p", "vn",
                                "md", "rd", "h", "o"])
    EE = area(R_, 6144, 4, 384)
    PP = area(R_, 6144 + 1536, 4, 384)
    DD = area(R_, 6144 + 3072, 4, T)
    SIG = area(R_, 6144 + 4096, 4, T)
    VNM = area(R_, 6144 + 5120, 8)
    rg_loaded = sem("rglru_loaded")
    rp = marks("rglru_products", ["r", "i"])
    ra = marks("rglru_scalar", ["le", "ll", "r", "i", "tanh", "a", "gelu", "sqrt"])
    rv = marks("rglru_vector", ["labs", "l1", "lneg", "lsp", "lsp8", "a2", "sq", "ix", "inp", "scan", "out"])
    WA_, WX_ = area(R_, 12288, 4), area(R_, 12800, 4)
    RR4, II4, TH, AA = [area(T_, 1024 * i, 4, T) for i in range(4)]
    GE, DE = [area(R_, 13312 + 1024 * i, 4, T) for i in range(2)]
    HH = NT[:, 8:12, :]
    LT1, LT2, LSP, LNEG8 = [SPARE[:, 9, 68 + 4 * i:72 + 4 * i] for i in range(4)]
    XB = CV[:, 20:24, :]
    with nc.Block() as block:
        @block.sync
        def _(sp):
            sp.dma_start(WA_, A["rglru_w_a"][0].rearrange("n i j -> i n j")).then_inc(rg_loaded, 16)
            sp.dma_start(WX_, A["rglru_w_x"][0].rearrange("n i j -> i n j")).then_inc(rg_loaded, 16)

        @block.scalar
        def _(act):
            lv.wait(act, "ax")
            la.did("ex1", act.activation(ROW(2), ROW(2), ACT.Exp, scale=-1.0))
            rv.wait(act, "labs")
            ra.did("le", act.activation(LT1, LT1, ACT.Exp, scale=-1.0))
            lv.wait(act, "e1")
            la.did("ln", act.activation(ROW(2), ROW(2), ACT.Ln))
            rv.wait(act, "l1")
            ra.did("ll", act.activation(LT1, LT1, ACT.Ln))
            lv.wait(act, "bm")
            la.did("em", act.activation(ROW(7), ROW(7), ACT.Exp, scale=-1.0))
            rp.wait(act, "r")
            for n in range(4):
                last = act.activation(RR4[:, n, :], ps_t(2)[:, n, :], ACT.Sigmoid, bias=par("rglru_b_a", n))
            ra.did("r", last)
            rp.wait(act, "i")
            for n in range(4):
                last = act.activation(II4[:, n, :], ps_t(0)[:, n, :], ACT.Sigmoid, bias=par("rglru_b_x", n))
            ra.did("i", last)
            la.did("sig", act.activation(SIG, BIG[:, MO:MO + 4, :], ACT.Sigmoid))
            rv.wait(act, "lsp8")
            ra.wait(act, "r")
            for n in range(4):
                last = act.activation(TH[:, n, :], RR4[:, n, :], ACT.Tanh, scale=LSP[:, n:n + 1])
            ra.did("tanh", last)
            lv.wait(act, "e")
            la.did("exp", act.activation(EE, EE, ACT.Exp))
            for n in range(4):
                last = act.activation(AA[:, n, :], RR4[:, n, :], ACT.Exp, scale=LNEG8[:, n:n + 1])
            ra.did("a", last)
            ra.did("gelu", act.activation(GE, BIG[:, RG:RG + 4, :], ACT.Gelu_apprx_tanh))
            rv.wait(act, "sq")
            ra.did("sqrt", act.activation(TH, TH, ACT.Sqrt))
            lp.wait(act, "den_num")
            la.did("ad", act.activation(DD, ps_t(0), ACT.Abs))

        @block.vector
        def _(dve):
            lv.did("i", dve.tensor_scalar(ROW(0), GT[0:4, 1, :], HC[0:4, 2:3], None, ALU.add))
            lv.did("xf", dve.tensor_scalar(ROW(1), GT[0:4, 3, :], HC[0:4, 3:4], None, ALU.add))
            lv.wait(dve, "xf")
            lv.did("ax", dve.scalar_tensor_tensor(out=ROW(2), in0=ROW(1), scalar=-1.0, in1=ROW(1), op0=ALU.mult, op1=ALU.max))
            lam = par("rglru_lambda", 0, 4)
            rv.did("labs", dve.scalar_tensor_tensor(out=LT1, in0=lam, scalar=-1.0, in1=lam, op0=ALU.mult, op1=ALU.max))
            la.wait(dve, "ex1")
            lv.did("e1", dve.tensor_scalar(ROW(2), ROW(2), 1.0, None, ALU.add))
            ra.wait(dve, "le")
            rv.did("l1", dve.tensor_scalar(LT1, LT1, 1.0, None, ALU.add))
            rv.did("lneg", dve.tensor_scalar(LT2, lam, -1.0, 0.0, ALU.mult, ALU.max))
            la.wait(dve, "ln")
            lv.did("lf", dve.scalar_tensor_tensor(out=ROW(3), in0=ROW(1), scalar=0.0, in1=ROW(2),
                                                  op0=ALU.min, op1=ALU.subtract))
            lv.wait(dve, "lf")
            lv.did("scan", dve.tensor_tensor_scan(ROW(4), UNIT[0:4, :], ROW(3), 0.0, ALU.mult, ALU.add))
            lv.wait(dve, "scan")
            lv.did("c", dve.tensor_tensor(ROW(5), ROW(0), ROW(4), ALU.subtract))
            lv.wait(dve, "c")
            lv.did("m", dve.tensor_tensor_scan(ROW(6), ROW(5), ROW(5), 0.0, ALU.max, ALU.max))
            lv.wait(dve, "m")
            lv.did("nm", dve.tensor_scalar(ROW(8), ROW(6), -1.0, None, ALU.mult))
            lv.did("bm", dve.tensor_tensor(ROW(7), ROW(4), ROW(6), ALU.add))
            rv.wait(dve, "lneg")
            ra.wait(dve, "ll")
            rv.did("lsp", dve.tensor_tensor(LSP, LT2, LT1, ALU.add))
            rv.wait(dve, "lsp")
            dve.tensor_scalar(LNEG8, LSP, -8.0, None, ALU.mult)
            rv.did("lsp8", dve.tensor_scalar(LSP, LSP, 8.0, None, ALU.mult))
            lp.wait(dve, "cols")
            lv.did("cols_out", dve.tensor_copy(COLS[:, 0:8], PS[:, 4, 0:8]))
            lv.wait(dve, "cols_out")
            lp.wait(dve, "rows")
            for h in range(4):
                nm = ps_t(4)[:, h, :]
                dve.scalar_tensor_tensor(out=EE[:, h, 0:P], in0=nm[:, 0:P], scalar=COLS[:, h:h + 1],
                                         in1=cst("causal_T"), op0=ALU.add, op1=ALU.add)
                dve.tensor_scalar(EE[:, h, P:T], nm[:, P:T], COLS[:, h:h + 1], None, ALU.add)
                last = dve.scalar_tensor_tensor(out=EE[:, h, T:384], in0=nm[:, P:T], scalar=COLS[:, 4 + h:5 + h],
                                                in1=cst("causal_T"), op0=ALU.add, op1=ALU.add)
            lv.did("e", last)
            lp.wait(dve, "kq")
            la.wait(dve, "exp")
            lv.did("p", dve.scalar_tensor_tensor(out=PP, in0=PS[:, 0:4, 0:384], scalar=float(P) ** -0.5, in1=EE,
                                                 op0=ALU.mult, op1=ALU.mult))
            lp.wait(dve, "v_nat")
            lv.did("vn", dve.tensor_copy(VNM, ps_m(4)))
            ra.wait(dve, "a")
            rv.did("a2", dve.tensor_tensor(DE, AA, AA, ALU.mult))
            rv.wait(dve, "a2")
            rv.did("sq", dve.scalar_tensor_tensor(out=fl(TH), in0=fl(DE), scalar=1.0, in1=fl(TH),
                                                  op0=ALU.add, op1=ALU.mult))
            rv.did("ix", dve.tensor_tensor(II4, II4, XB, ALU.mult))
            rv.wait(dve, "ix")
            ra.wait(dve, "sqrt")
            rv.did("inp", dve.tensor_tensor(II4, II4, TH, ALU.mult))
            rv.wait(dve, "inp")
            for n in range(4):
                last = dve.tensor_tensor_scan(HH[:, n, :], AA[:, n, :], II4[:, n, :], 0.0, ALU.mult, ALU.add)
            rv.did("scan", last)
            rv.wait(dve, "scan")
            rv.did("out", dve.tensor_tensor(HH, HH, GE, ALU.mult))
            lp.wait(dve, "den_num")
            la.wait(dve, "ad")
            lv.did("md", dve.tensor_tensor(DD, DD, ps_t(6), ALU.max))
            lv.wait(dve, "md")
            lv.did("rd", dve.reciprocal(DD, DD))
            lv.wait(dve, "rd")
            lv.did("h", dve.tensor_tensor(DD, DD, ps_t(2), ALU.mult))
            lv.wait(dve, "h")
            la.wait(dve, "sig")
            lv.did("o", dve.tensor_tensor(O8[:, 4:8, :], DD, SIG, ALU.mult))

        @block.tensor
        def _(pe):
            mmul = nc.tensor.matmul
            pe.wait_ge(rg_loaded, 32)
            for name, w, bank in (("r", WA_, 2), ("i", WX_, 0)):
                for n in range(4):
                    last = mmul(ps_t(bank)[:, n, :], w[:, n, :], XB[:, n, :], start=True, stop=True)
                rp.did(name, last)
            lv.wait(pe, "c")
            for c in range(2):
                last = nc.tensor.transpose(PS[:, 4, 4 * c:4 * c + 4], ROW(5)[:, c * P:(c + 1) * P], IDENT[0:4, 0:4])
            lp.did("cols", last)
            lv.wait(pe, "nm")
            la.wait(pe, "em")
            lv.wait(pe, "cols_out")
            for n, row in enumerate((ROW(8), ROW(7))):
                for h in range(4):
                    last = mmul(ps_t(4 + 2 * n)[:, h, :], pick(h, 4), row, start=True, stop=True)
            lp.did("rows", last)
            ra.wait(pe, "i")
            for h in range(4):
                q, k = CV[:, 12 + h, :], CV[:, 16 + h, :]
                mmul(PS[:, h, 0:T], k[:, 0:P], q, start=True, stop=True)
                last = mmul(PS[:, h, T:384], k[:, P:T], q[:, P:T], start=True, stop=True)
            lp.did("kq", last)
            lv.wait(pe, "e")
            for c in range(2):
                for h in range(4):
                    last = nc.tensor.transpose(ps_m(4)[:, 4 * c + h, :], BIG[:, MV + h, c * P:(c + 1) * P], IDENT)
            lp.did("v_nat", last)
            lv.wait(pe, "vn")
            for h in range(4):
                for bank, lhs in ((0, [ONES, ONES]), (2, [VNM[:, h, :], VNM[:, 4 + h, :]])):
                    dst = ps_t(bank)[:, h, :]
                    mmul(dst, lhs[0], PP[:, h, 0:T], start=True, stop=False)
                    last = mmul(dst[:, P:T], lhs[1], PP[:, h, T:384], start=False, stop=True)
            lp.did("den_num", last)
    if stop == 2:
        return ctx

    hp = marks("headnorm_products", ["ssq", "rsb"])
    ha = marks("headnorm_scalar", ["silu", "sd"])
    hv = marks("headnorm_vector", ["sq", "ms", "rs", "scaled", "gated"])
    GATE = area(R_, 6144, 4, T)
    with nc.Block() as block:
        @block.scalar
        def _(act):
            ha.did("silu", act.activation(GATE, BIG[:, GZ:GZ + 4, :], ACT.Silu))
            hv.wait(act, "ms")
            ha.did("sd", act.activation(RSC, RSC, ACT.Sqrt))

        @block.vector
        def _(dve):
            hv.did("sq", dve.tensor_tensor(SQ8, O8, O8, ALU.mult))
            hp.wait(dve, "ssq")
            hv.did("ms", dve.tensor_scalar(RSC, PS[:, 4, 0:16], 1.0 / P, EPS, ALU.mult, ALU.add))
            ha.wait(dve, "sd")
            hv.did("rs", dve.reciprocal(RSC, RSC))
            hp.wait(dve, "rsb")
            for i in range(8):
                gain = par("gdn_norm") if i < 4 else par("mlstm_norm", i - 4)
                last = dve.scalar_tensor_tensor(out=NT[:, i, :], in0=O8[:, i, :], scalar=gain, in1=ps_t(0, 4)[:, i, :],
                                                op0=ALU.mult, op1=ALU.mult)
            hv.did("scaled", last)
            hv.wait(dve, "scaled")
            ha.wait(dve, "silu")
            hv.did("gated", dve.tensor_tensor(NT[:, 0:4, :], NT[:, 0:4, :], GATE, ALU.mult))

        @block.tensor
        def _(pe):
            hv.wait(pe, "sq")
            hp.did("ssq", token_sums(PS[:, 4, 0:16], SQ8, UNIT[:, 0:1]))
            hv.wait(pe, "rs")
            hp.did("rsb", to_channels(ps_t(0, 4), 1))

    if stop == 3:
        return ctx

    wload = sem("rwkv_loaded")
    wp = marks("rwkv_products", ["w2", "a2", "g2", "kkss", "kkb", "v_nat", "b_nat", "k_nat", "lt", "pt", "qbt", "qkt", "cx0"]
               + [s for l in range(1, 6) for s in ((f"cx{l}",) + (("rv",) if l == 1 else ()) + (f"y{l}", f"yt{l}") if l < 5 else (f"cx{l}", f"yt{l}"))]
               + [s for c in range(4) for s in (((f"r{c}",) if c else ()) + (f"u{c}",) + ((f"s{c}",) if c < 3 else ())
                                                + (f"y_{c}",))]
               + ["mean", "rk", "var", "rsb"])
    wa = marks("rwkv_scalar", ["tanh", "sg", "sig", "a", "g", "w", "wi", "wp", "kksd", "vn", "bn", "kn"]
               + ["cxs1", "rv"] + [f"cxs{l}" for l in range(2, 6)]
               + [s for c in range(4) for s in (f"u{c}", f"y_{c}")] + ["sd"])
    wv = marks("rwkv_vector", ["ld", "cum", "cmp", "kkr", "kksq", "kkms", "kkrec", "kk",
                               "am1", "kp", "rt", "kt", "b", "bt", "at0", "at", "zero", "lt", "ct0", "pt",
                               "qbt", "qkt", "x0", "ct1"]
               + [s for l in range(1, 5) for s in (f"ct{l + 1}", f"x{l}", f"xt{l}")] + ["xt5"]
               + [s for c in range(4) for s in (((f"r{c}",) if c else ()) + ((f"sa{c}", f"s{c}") if c < 3 else ()))]
               + ["rk0", "rk1", "cen", "var", "rkv", "ms", "rs", "n0", "n1", "n2", "n3", "out"])
    W2, A2, G2 = R_[0:64, 15360:15872], R_[64:128, 15360:15872], R_[:, 15872:16384]
    r4, k4, v4 = [BIG[:, 40 + 4 * i:44 + 4 * i, :] for i in range(3)]
    e4 = [BIG[:, 4 * i:4 * i + 4, :] for i in range(10)]
    LD, CUM, WC, WI, WP_, AS, GG, KKN, KP_, RTL = e4
    KTL, BTL, ATL, T4 = [area(T_, 1024 * i, 4, T) for i in range(4)]
    M16 = [area(R_, 8192 + 1024 * i, 16, 64) for i in range(8)]
    MLT, MPT, MQB, MQK, MXI, MXT, MCT, MCX = M16

    def mat(h, t):
        return 8 * (h % 2) + 2 * (h // 2) + t

    VNW, BNW, KNW = [fl(e).rearrange("p (t c) -> p t c", t=2) for e in (AS, CUM, WI)]
    SWS = [fl(BIG[:, 54 + 2 * i:56 + 2 * i, :]).rearrange("p (h i) -> p h i", h=4) for i in range(2)]
    RVS = fl(KTL).rearrange("p (t c) -> p t c", t=2)
    US = fl(BIG[:, 58:60, :])
    YW = fl(BIG[:, 60:64, :]).rearrange("p (h t) -> p h t", h=4)
    with nc.Block() as block:
        @block.sync
        def _(sp):
            sp.dma_start(W2, A["rwkv_w2"][0]).then_inc(wload, 16)
            sp.dma_start(A2, A["rwkv_a2"][0]).then_inc(wload, 16)
            sp.dma_start(G2, A["rwkv_g2"][0]).then_inc(wload, 16)
            load_rows(sp, B0, A["w_out"][0], 0, RAWS)

        @block.scalar
        def _(act):
            wa.did("tanh", act.activation(BIG[0:64, WWA, :], BIG[0:64, WWA, :], ACT.Tanh))
            wa.did("sg", act.activation(BIG[:, WG, :], BIG[:, WG, :], ACT.Sigmoid))
            wp.wait(act, "w2")
            for i in range(4):
                last = act.activation(LD[:, i, :], ps_t(0)[:, i, :], ACT.Sigmoid, bias=par("rwkv_w0", i))
            wa.did("sig", last)
            wp.wait(act, "a2")
            for i in range(4):
                last = act.activation(AS[:, i, :], ps_t(2)[:, i, :], ACT.Sigmoid, bias=par("rwkv_a0", i))
            wa.did("a", last)
            wp.wait(act, "g2")
            wa.did("g", act.activation(GG, ps_t(4), ACT.Copy))
            wv.wait(act, "cmp")
            wa.did("w", act.activation(WC, CUM, ACT.Exp))
            wa.did("wi", act.activation(WI, CUM, ACT.Exp, scale=-1.0))
            wa.did("wp", act.activation(WP_, LD, ACT.Exp))
            wv.wait(act, "kkms")
            wa.did("kksd", act.activation(RSC, RSC, ACT.Sqrt))
            wv.wait(act, "at")
            wp.wait(act, "v_nat")
            wa.did("vn", act.activation(VNW, PS[:, 0:2, :], ACT.Copy))
            wp.wait(act, "b_nat")
            wa.did("bn", act.activation(BNW, PS[:, 2:4, :], ACT.Copy))
            wp.wait(act, "k_nat")
            wa.did("kn", act.activation(KNW, PS[:, 4:6, :], ACT.Copy))
            for l in range(1, 6):
                wp.wait(act, f"cx{l}")
                wa.did(f"cxs{l}", act.activation(MCX, ps_c(0), ACT.Copy))
                if l == 1:
                    wp.wait(act, "rv")
                    wa.did("rv", act.activation(RVS, PS[:, 6:8, :], ACT.Copy))
            for c in range(4):
                rows = slice(64 * (c % 2), 64 * (c % 2) + 64)
                wp.wait(act, f"u{c}")
                wa.did(f"u{c}", act.activation(US[rows, :], PS[rows, 1, :], ACT.Copy))
                wp.wait(act, f"y_{c}")
                wa.did(f"y_{c}", act.activation(YW[:, :, 64 * c:64 * c + 64],
                                                PS[:, 2, 0:256].rearrange("p (h t) -> p h t", h=4), ACT.Copy))
            wv.wait(act, "ms")
            wa.did("sd", act.activation(RSC, RSC, ACT.Sqrt))

        @block.vector
        def _(dve):
            def stt(out, a, s, b, op0, op1):
                return dve.scalar_tensor_tensor(out=out, in0=a, scalar=s, in1=b, op0=op0, op1=op1)

            wa.wait(dve, "sig")
            wv.did("ld", dve.tensor_scalar(LD, LD, -float(np.exp(-0.5)), None, ALU.mult))
            wv.wait(dve, "ld")
            for i in range(4):
                last = dve.tensor_tensor_scan(CUM[:, i, :], cst("reset64"), LD[:, i, :], 0.0, ALU.mult, ALU.add)
            wv.did("cum", last)
            wv.wait(dve, "cum")
            wv.did("cmp", dve.tensor_tensor(LD, CUM, LD, ALU.subtract))
            wv.did("kkr", dve.tensor_tensor(KKN, k4, spread(par("rwkv_k_k", 0, 4), T), ALU.mult))
            wv.wait(dve, "kkr")
            wv.did("kksq", dve.tensor_tensor(T4, KKN, KKN, ALU.mult))
            wp.wait(dve, "kkss")
            wv.did("kkms", dve.tensor_scalar(RSC, PS[:, 6, 0:16], EPS, None, ALU.add))
            wa.wait(dve, "kksd")
            wv.did("kkrec", dve.reciprocal(RSC, RSC))
            wp.wait(dve, "kkb")
            wv.did("kk", dve.tensor_tensor(KKN, KKN, ps_t(6), ALU.mult))
            wv.wait(dve, "kk")
            wa.wait(dve, "a")
            for i in range(4):
                last = dve.tensor_scalar(T4[:, i, :], AS[:, i, :], -1.0, par("rwkv_k_a", i), ALU.add, ALU.mult)
            wv.did("am1", last)
            wv.wait(dve, "am1")
            wv.did("kp", stt(fl(KP_), fl(T4), 1.0, fl(k4), ALU.add, ALU.mult))
            wv.wait(dve, "kp")
            wa.wait(dve, "wp")
            wv.did("rt", dve.tensor_tensor(RTL, r4, WC, ALU.mult))
            wv.did("kt", dve.tensor_tensor(KTL, KP_, WI, ALU.mult))
            wv.did("b", dve.tensor_tensor(BTL, KKN, AS, ALU.mult))
            wv.wait(dve, "b")
            wv.did("bt", dve.tensor_tensor(BTL, BTL, WI, ALU.mult))
            wv.did("at0", dve.tensor_tensor(ATL, KKN, WP_, ALU.mult))
            wv.wait(dve, "at0")
            wv.did("at", dve.tensor_scalar(ATL, ATL, -1.0, None, ALU.mult))
            dve.memset(SWS[0], 0.0)
            wv.did("zero", dve.memset(SWS[1], 0.0))
            strict, incl = repeated(cst("strict64_T"), 16), repeated(cst("incl64_T"), 16)
            unit = repeated(cst("ident64"), 16)
            wp.wait(dve, "lt")
            wv.did("lt", stt(MLT, ps_c(0), -1.0, strict, ALU.mult, ALU.mult))
            wv.wait(dve, "lt")
            wv.did("ct0", dve.tensor_tensor(MCT, MLT, repeated(cst("half_level1"), 16), ALU.mult))
            wp.wait(dve, "pt")
            wv.did("pt", dve.tensor_tensor(MPT, ps_c(2), strict, ALU.mult))
            wp.wait(dve, "qbt")
            wv.did("qbt", dve.tensor_tensor(MQB, ps_c(4), incl, ALU.mult))
            wp.wait(dve, "qkt")
            wv.did("qkt", dve.tensor_tensor(MQK, ps_c(6), incl, ALU.mult))
            wp.wait(dve, "cx0")
            dve.tensor_tensor(MXI, unit, ps_c(0), ALU.subtract)
            wv.did("x0", dve.tensor_tensor(MXT, unit, MCT, ALU.subtract))
            wv.wait(dve, "x0")
            wv.did("ct1", dve.tensor_tensor(MCT, MLT, repeated(cst("half_level2"), 16), ALU.mult))
            for l in range(1, 6):
                if l < 5:
                    wp.wait(dve, f"cx{l}")
                    wv.did(f"ct{l + 1}", dve.tensor_tensor(MCT, MLT, repeated(cst(f"half_level{LEVELS[l + 1]}"), 16),
                                                           ALU.mult))
                    wp.wait(dve, f"y{l}")
                    wv.did(f"x{l}", dve.tensor_tensor(MXI, MXI, ps_c(2), ALU.subtract))
                wp.wait(dve, f"yt{l}")
                wv.did(f"xt{l}", dve.tensor_tensor(MXT, MXT, ps_c(4), ALU.subtract))
            for c in range(4):
                if c:
                    rows = slice(64 * (c % 2), 64 * (c % 2) + 64)
                    wp.wait(dve, f"r{c}")
                    wv.did(f"r{c}", dve.tensor_tensor(RVS[rows, c // 2, :], RVS[rows, c // 2, :], PS[rows, 0, :], ALU.add))
                if c == 3:
                    break
                wp.wait(dve, f"s{c}")
                if c == 0:
                    wv.wait(dve, "zero")
                else:
                    wp.wait(dve, f"y_{c - 1}")
                old, new = SWS[c % 2], SWS[(c + 1) % 2]
                for e in range(2):
                    q = slice(64 * e, 64 * e + 64)
                    last = dve.tensor_tensor(new[q, :, q], old[q, :, q], ps_m(3, 1)[q, :, q], ALU.add)
                wv.did(f"sa{c}", last)
                wv.wait(dve, f"sa{c}")
                for e in range(2):
                    q = slice(64 * e, 64 * e + 64)
                    decay = WC[q, :, 64 * c + 63:64 * c + 64].broadcast_to([64, 4, 64])
                    last = dve.tensor_tensor(new[q, :, q], new[q, :, q], decay, ALU.mult)
                wv.did(f"s{c}", last)
            wv.did("rk0", dve.tensor_tensor(LD, r4, KP_, ALU.mult))
            wv.wait(dve, "rk0")
            wv.did("rk1", dve.tensor_tensor(LD, LD, spread(par("rwkv_r_k", 0, 4), T), ALU.mult))
            wp.wait(dve, "mean")
            wv.did("cen", stt(YW, ps_t(4), -1.0 / 64, YW, ALU.mult, ALU.add))
            wv.wait(dve, "cen")
            wv.did("var", dve.tensor_tensor(KKN, YW, YW, ALU.mult))
            wp.wait(dve, "rk")
            wv.did("rkv", dve.tensor_tensor(LD, v4, ps_t(0), ALU.mult))
            wp.wait(dve, "var")
            wv.did("ms", dve.tensor_scalar(RSC, PS[:, 6, 0:16], 1.0 / 64, 64e-5, ALU.mult, ALU.add))
            wa.wait(dve, "sd")
            wv.did("rs", dve.reciprocal(RSC, RSC))
            wp.wait(dve, "rsb")
            wv.did("n0", dve.tensor_tensor(YW, YW, ps_t(6), ALU.mult))
            wv.wait(dve, "n0")

        @block.tensor
        def _(pe):
            mmul = nc.tensor.matmul
            pe.wait_ge(wload, 48)
            wa.wait(pe, "sg")
            for name, w, x, bank in (("w2", W2, BIG[0:64, WWA, :], 0), ("a2", A2, BIG[64:128, WWA, :], 2),
                                     ("g2", G2, BIG[:, WG, :], 4)):
                for i in range(4):
                    last = mmul(ps_t(bank)[:, i, :], w[:, i * P:(i + 1) * P], x, start=True, stop=True)
                wp.did(name, last)
            wv.wait(pe, "kksq")
            wp.did("kkss", token_sums(PS[:, 6, 0:16], T4, ONES64[:, 0:P:64]))
            wv.wait(pe, "kkrec")
            wp.did("kkb", to_channels(ps_t(6), 2))
            wv.wait(pe, "at")
            wa.wait(pe, "g")
            for name, src, bank in (("v_nat", v4, 0), ("b_nat", BTL, 2), ("k_nat", KTL, 4)):
                for t in range(TT):
                    for i in range(4):
                        last = nc.tensor.transpose(PS[:, bank + t, i * P:(i + 1) * P],
                                                   src[:, i, t * P:(t + 1) * P], IDENT)
                wp.did(name, last)
            wa.wait(pe, "kn")
            halves = [slice(0, 64), slice(64, 128)]
            for name, lhs, rhs, bank in (("lt", BTL, ATL, 0), ("pt", KTL, ATL, 2), ("qbt", BTL, RTL, 4),
                                         ("qkt", KTL, RTL, 6)):
                for n in range(32):
                    c, h = n // 8, n % 8
                    e, chunk64 = halves[h % 2], slice(64 * c, 64 * c + 64)
                    last = mmul(ps_c(bank)[halves[c % 2], mat(h, c // 2), :], lhs[e, h // 2, chunk64],
                                rhs[e, h // 2, chunk64], start=True, stop=True)
                wp.did(name, last)

            def each64(bank, lhs, rhs):
                for n in range(32):
                    q = halves[n % 2]
                    last = mmul(ps_c(bank)[q, n // 2, :], lhs[q, n // 2, :],
                                rhs[q, q] if rhs is IDENT else rhs[q, n // 2, :], start=True, stop=True)
                return last

            wv.wait(pe, "ct0")
            wp.did("cx0", each64(0, MCT, IDENT))
            for l in range(1, 6):
                wv.wait(pe, f"x{l - 1}" if l > 1 else "ct1")
                wp.did(f"cx{l}", each64(0, MCT, MXI))
                if l == 1:
                    for n in range(32):
                        t, h, q = n // 16, n // 2 % 8, halves[n % 2]
                        last = mmul(PS[q, 6 + t, 64 * h:64 * h + 64], MPT[q, mat(h, t), :],
                                    VNW[q, t, 64 * h:64 * h + 64], start=True, stop=True)
                    wp.did("rv", last)
                wa.wait(pe, f"cxs{l}")
                if l > 1:
                    wv.wait(pe, f"xt{l - 1}")
                if l < 5:
                    wp.did(f"y{l}", each64(2, MXT, MCX))
                wp.did(f"yt{l}", each64(4, MCX, MXT))
            wv.wait(pe, "xt5")
            for c in range(4):
                t, q = c // 2, slice(64 * (c % 2), 64 * (c % 2) + 64)
                cols = slice(64 * c, 64 * c + 64)
                SW = SWS[c % 2]
                if c:
                    wv.wait(pe, f"s{c - 1}")
                    for hp2 in range(4):
                        last = mmul(PS[q, 0, hp2 * P:(hp2 + 1) * P], ATL[:, hp2, cols], SW[:, hp2, :], start=True,
                                    stop=True)
                    wp.did(f"r{c}", last)
                    wv.wait(pe, f"r{c}")
                else:
                    wa.wait(pe, "rv")
                for h in range(8):
                    last = mmul(PS[q, 1, 64 * h:64 * h + 64], MXT[q, mat(h, t), :], RVS[q, t, 64 * h:64 * h + 64],
                                start=True, stop=True)
                wp.did(f"u{c}", last)
                wa.wait(pe, f"u{c}")
                if c < 3:
                    for h in range(8):
                        hc, o = slice(64 * h, 64 * h + 64), slice(64 * (h % 2), 64 * (h % 2) + 64)
                        mmul(PS[o, 3, hc], BNW[q, t, hc], US[q, hc], start=True, stop=False)
                        last = mmul(PS[o, 3, hc], KNW[q, t, hc], VNW[q, t, hc], start=False, stop=True)
                    wp.did(f"s{c}", last)
                for hp2 in range(4):
                    dst = PS[:, 2, 64 * hp2:64 * hp2 + 64]
                    if c:
                        mmul(dst, SW[:, hp2, :], RTL[:, hp2, cols], start=True, stop=False)
                    for e in range(2):
                        h = 2 * hp2 + e
                        hc, o = slice(64 * h, 64 * h + 64), slice(64 * e, 64 * e + 64)
                        mmul(dst[o, :], US[q, hc], MQB[q, mat(h, t), :], start=(c == 0), stop=False)
                        last = mmul(dst[o, :], VNW[q, t, hc], MQK[q, mat(h, t), :], start=False, stop=True)
                wp.did(f"y_{c}", last)
            wa.wait(pe, "y_3")
            for b in range(2):
                last = mmul(PS[:, 4 + b, :], ONES64, fl(YW[:, 2 * b:2 * b + 2, :]), start=True, stop=True)
            wp.did("mean", last)
            wv.wait(pe, "rk1")
            for b in range(2):
                last = mmul(PS[:, b, :], ONES64, fl(LD[:, 2 * b:2 * b + 2, :]), start=True, stop=True)
            wp.did("rk", last)
            wv.wait(pe, "var")
            wp.did("var", token_sums(PS[:, 6, 0:16], KKN, ONES64[:, 0:P:64]))
            wv.wait(pe, "rs")
            wp.did("rsb", to_channels(ps_t(6), 2))

    def finish_rwkv(dve):
        wv.did("n1", dve.tensor_tensor(YW, YW, spread(par("rwkv_ln_w", 0, 4), T), ALU.mult))
        wv.wait(dve, "n1")
        wv.did("n2", dve.tensor_tensor(YW, YW, spread(par("rwkv_ln_b", 0, 4), T), ALU.add))
        wv.wait(dve, "n2")
        wv.did("n3", dve.tensor_tensor(YW, YW, LD, ALU.add))
        wv.wait(dve, "n3")
        wv.did("out", dve.tensor_tensor(NT[:, 12:16, :], YW, GG, ALU.mult))
        wv.wait(dve, "out")
    if stop == 4:
        return ctx

    N_GU = F1 // 256
    B1 = B0 + N_OUT
    B2 = B1 + 4 * N_GU
    B3 = B2 + F1 // P
    NI2 = 2 * sum(n for _, n in GROUPS2)
    B4 = B3 + NI2 + 2
    L1 = N_OUT
    L2 = L1 + F1 // P
    L3 = L2 + N_OUT
    acted = sem("hidden_acted")
    hidden = sem("hidden_made")
    res_done = sem("residual_done")
    gain_loaded = sem("gain_loaded")
    ACTED = area(T_, 0, 2, 512)
    GAIN = fl(BIG[:, 44:52, :])

    def two(x):
        return x.rearrange("p (c t) -> p c t", c=2)

    def row_gain(a):
        return a.rearrange("(o d) -> o d", o=1).broadcast_to([P, D])

    H0 = 2
    W1 = [area(T_, 0, 16, T), BIG[:, 46:62, :]]
    cload = sem("cmp_weights_loaded")

    def pe_hidden(pe, n0, units, fresh):
        for u in range(2):
            for j in range(4):
                pe_col_item(pe, n0 + 4 * u + j, 0, j % 2, 4 * u + j // 2 * 2, fresh if u == 0 and j < 2 else None)
        with pe.Fori(0, units // 2 - 1) as r:
            for u in range(2, 4):
                pe.wait_ge(hidden, H0 + 2 * r + u - 1)
                for j in range(4):
                    pe_col_item(pe, n0 + 4 * u + j, 2 * r, j % 2, 4 * (u % 2) + j // 2 * 2)

    def act_hidden(act, n0, units):
        with act.Fori(0, units // 2) as r:
            for u in range(2):
                for j in range(4):
                    split_hi(act, n0 + 4 * u + j + 2, 2 * r)
                    if j == 1:
                        act.wait_ge(item_used, n0 + 4 * u + 2 + 8 * r)
                        act.wait_ge(hidden, H0 + 2 * r + u - 1)
                        act.activation(two(ACTED[:, u, :]), PS[:, 4 * u:4 * u + 2, 0:T], ACT.Silu).then_inc(acted, 1)

    def dve_hidden(dve, n0, units):
        with dve.Fori(0, units // 2) as r:
            for u in range(2):
                for j in range(4):
                    split_lo(dve, n0 + 4 * u + j + 2, 2 * r)
                dve.wait_ge(item_used, n0 + 4 * u + 4 + 8 * r)
                dve.wait_ge(acted, 2 * r + u + 1)
                dve.tensor_tensor(BIG[:, bass.ds(4 * r + 2 * u, 2), :], two(ACTED[:, u, :]),
                                  PS[:, 4 * u + 2:4 * u + 4, 0:T], ALU.mult).then_inc(hidden, 1)

    with nc.Block() as block:
        @block.sync
        def _(sp):
            load_rows(sp, B0, A["w_out"][0], RAWS)
            load_gate_up(sp, B1, A["ffn_w_gate"][0], A["ffn_w_up"][0], N_GU)
            sp.dma_start(GAIN, row_gain(A["final_norm"])).then_inc(gain_loaded, 16)
            n = load_rows(sp, B2, A["ffn_w_down"][0])
            for c, pairs in GROUPS2:
                n = load_cols(sp, n, A["w_in_2"][0], c, pairs)
            for c in (NSA_GATES, FOX_GATES):
                n = load_narrow(sp, n, A["w_in_2"][0], c)

        @block.scalar
        def _(act):
            split_hi(act, B0)
            split_hi(act, B0 + 1)
            act_rows(act, B0, 0, N_OUT, NT, B4, lambda: wv.wait(act, "out"))
            norm_act(act, 1, lambda e, t: e.wait_ge(res_done, t + 1))
            norm_act_hi(act, 1)
            act.wait_ge(norm_out, 16)
            act_hidden(act, B1, N_GU)
            act.wait_ge(hidden, H0 + N_GU)
            act_rows(act, B2, L1, F1 // P, BIG, B4)
            norm_act(act, 2, lambda e, t: e.wait_ge(res_done, 2 + t + 1))
            norm_act(act, 3, lambda e, t: e.wait_ge(res_done, 4 + t + 1))
            norm_act_hi(act, 3)
            act.wait_ge(norm_out, 24)
            for w, src in zip(W1, ("phik_w1_2", "phiv_w1_2")):
                act.dma_start(w, A[src][0].rearrange("(l p) h -> p l h", p=P)).then_inc(cload, 16)
            n, q, at = B3, NI // 2, 0
            for _, pairs in GROUPS2:
                act_cols(act, n, q, pairs, at, B4)
                n, q, at = n + 2 * pairs, q + pairs, at + 2 * pairs
            act.wait_ge(item_used, B4)
            act.activation(GT[0:24, 0, :], PS[0:24, 6, 0:T], ACT.Copy)
            act.activation(GT[0:8, 1, :], PS[0:8, 7, 0:T], ACT.Copy)

        def add_residual(dve, n, used):
            for t in range(TT):
                if t == 0:
                    dve.wait_ge(tile_done, n + 1)
                else:
                    dve.wait_ge(item_used, used)
                dve.tensor_tensor(X[:, t, :], X[:, t, :], PS[:, 4 * t:4 * t + 4, :].rearrange("p b n -> p (b n)"),
                                  ALU.add).then_inc(res_done, 1)

        @block.vector
        def _(dve):
            for _ in range(H0):
                dve.engine_nop().then_inc(hidden, 1)
            split_lo(dve, B0)
            split_lo(dve, B0 + 1)
            dve_rows(dve, B0, 0, N_OUT, NT, B4, lambda: finish_rwkv(dve))
            add_residual(dve, 0, B1)
            split_lo(dve, B1 + 1)
            dve.wait_ge(res_done, 2)
            norm_dve(dve, 1, "ffn_norm")
            dve_hidden(dve, B1, N_GU)
            dve_rows(dve, B2, L1, F1 // P, BIG, B4)
            add_residual(dve, 1, B3)
            split_lo(dve, B3 + 1)
            dve.wait_ge(res_done, 4)
            norm_dve(dve, 2, None)
            dve.wait_ge(gain_loaded, 16)
            for t in range(TT):
                dve.scalar_tensor_tensor(out=X[:, t, :], in0=X[:, t, :], scalar=ST[:, 6 + t:7 + t], in1=GAIN,
                                         op0=ALU.mult, op1=ALU.mult).then_inc(res_done, 1)
            dve.wait_ge(res_done, 6)
            norm_dve(dve, 3, "g_mix_pre_2")
            dve_ahead(dve, B3, NI2, B4)

        @block.tensor
        def _(pe):
            pe_rows(pe, B0, 0, N_OUT)
            norm_pe(pe, 1)
            pe_hidden(pe, B1, N_GU, 1)
            pe.wait_ge(hidden, H0 + N_GU)
            pe_rows(pe, B2, L1, F1 // P)
            norm_pe(pe, 3)
            n, q = B3, NI // 2
            for _, pairs in GROUPS2:
                pe_cols(pe, n, q, pairs, 3 if n == B3 else None)
                n, q = n + 2 * pairs, q + pairs
            for m in range(2):
                pe_narrow(pe, n + m, 6 + m)
    if stop == 5:
        return ctx

    ZSH = R_[:, 2048:3072].rearrange("p (v g t) -> p v g t", v=2, g=2)
    G8 = area(R_, 4096, 24, T)
    KDUP = R_[:, 10240:11264].rearrange("p (s g t) -> p s g t", s=2, g=2)
    CB = area(R_, 11264, 8, 384)
    VNAT = fl(BIG[:, 46:60, :]).rearrange("p (t c) -> p t c", t=TT)
    C0 = B4
    VTILES = [AVS, AVW] + [BV + i for i in range(4)] + [CV_ + i for i in range(4)] + [DV + i for i in range(4)]
    SMALL = R_[:, 14848:16384]
    BT = SMALL[:, 0:960].rearrange("p (v l g n) -> p v l g n", v=2, l=16, g=2)
    W2K = SMALL[:, 960:1216].rearrange("p (h d) -> p h d", h=2)
    W2V = SMALL[:, 1216:1344].rearrange("p (h d) -> p h d", h=2)
    HID = SMALL[:, 1344:1464].rearrange("p (v h n) -> p v h n", v=2, h=2)
    KC = SMALL[:, 1464:1494]
    HIDN = R_[0:30, 14336:14848]
    VC = fl(BIG[:, 62:63, :])[0:15, 0:128]
    GATEC = fl(BIG[:, 62:63, :])[:, 128:176].rearrange("p (t n) -> p t n", t=TT)
    FCOL = fl(BIG[:, 62:63, :])[:, 176:192].rearrange("p (t n) -> p t n", t=TT)
    FR = [GT[0:8, i, :] for i in range(4)] + [fl(BIG[:, 63:64, :])[0:8, :]]
    windows_moved = sem("windows_moved")
    keys_moved = sem("keys_moved")
    biasin = sem("bias_loaded")
    cp = marks("prep_products", ["hid", "vn0", "hid_T", "kvc", "vn1", "cols", "fox"])
    ca = marks("prep_scalar", ["gates", "fex", "fln", "gelu", "vn0", "hid_T", "vn1"])
    cv = marks("prep_vector", ["bt", "fx", "fax", "fe1", "flf", "fscan", "fn8", "kvc", "cols", "cb"])
    with nc.Block() as block:
        @block.sync
        def _(sp):
            for v, tile in enumerate((AKC, AVC)):
                for g in range(2):
                    src = BIG[64 * g:64 * g + 64, tile, :]
                    sp.dma_start(ZSH[0:64, v, g, :], src).then_inc(windows_moved, 16)
                    sp.dma_start(ZSH[64:128, v, g, 0:T - 1], src[:, 1:T]).then_inc(windows_moved, 16)
            w2 = A["phik_w2_2"][0].rearrange("(h p) d -> p h d", p=P)
            sp.dma_start(W2K[:, :, 0:64], w2).then_inc(cload, 16)
            sp.dma_start(W2K[:, :, 64:128], w2).then_inc(cload, 16)
            sp.dma_start(W2V, A["phiv_w2_2"][0].rearrange("(h p) d -> p h d", p=P)).then_inc(cload, 16)
            for s, tile in enumerate((AKS, AKW)):
                for g in range(2):
                    for e in range(2):
                        sp.dma_start(KDUP[64 * e:64 * e + 64, s, g, :], BIG[64 * g:64 * g + 64, tile, :])\
                            .then_inc(keys_moved, 16)
            sp.dma_start(CST[:, :], A["const"]).then_inc(const_loaded, 16)
            skew = bass.AP(bias_skew.tensor, 127, [[383, P], [P * 384, 24], [1, T]])
            sp.dma_start(G8, skew).then_inc(biasin, 16)
            sp.wait_ge(biasin, 16)
            sp.wait_ge(keys_moved, 128)

        @block.scalar
        def _(act):
            ca.did("gates", act.activation(GT[0:24, 0, :], GT[0:24, 0, :], ACT.Sigmoid))
            cv.wait(act, "fax")
            ca.did("fex", act.activation(FR[2], FR[2], ACT.Exp, scale=-1.0))
            cv.wait(act, "fe1")
            ca.did("fln", act.activation(FR[2], FR[2], ACT.Ln))
            cp.wait(act, "hid")
            ca.did("gelu", act.activation(HIDN, PS[0:30, 0, :], ACT.Gelu_apprx_tanh))
            for t in range(TT):
                cp.wait(act, f"vn{t}")
                ca.did(f"vn{t}", act.activation(VNAT[:, t, :], fl(PS[:, 2:6, :])[:, 0:1792], ACT.Copy))
                if t == 0:
                    cp.wait(act, "hid_T")
                    ca.did("hid_T", act.activation(HID, PS[:, 1, 0:120].rearrange("p (v h n) -> p v h n", v=2, h=2),
                                                   ACT.Copy))

        @block.vector
        def _(dve):
            dve.wait_ge(windows_moved, 128)
            for v in range(2):
                for g in range(2):
                    for half in range(2):
                        src = ZSH[:, v, g, 16 * half:16 * half + 240].rearrange("p (n l two) -> p l n two", l=8, two=2)
                        last = dve.tensor_tensor(BT[:, v, 8 * half:8 * half + 8, g, :], src[:, :, :, 0],
                                                 spread(par("cmp_pe_2", 8 * half, 8), 15), ALU.add)
            cv.did("bt", last)
            cv.did("fx", dve.tensor_scalar(FR[1], FR[1], HC[0:8, 4:5], None, ALU.add))
            cv.wait(dve, "fx")
            cv.did("fax", dve.scalar_tensor_tensor(out=FR[2], in0=FR[1], scalar=-1.0, in1=FR[1],
                                                   op0=ALU.mult, op1=ALU.max))
            ca.wait(dve, "fex")
            cv.did("fe1", dve.tensor_scalar(FR[2], FR[2], 1.0, None, ALU.add))
            ca.wait(dve, "fln")
            cv.did("flf", dve.scalar_tensor_tensor(out=FR[3], in0=FR[1], scalar=0.0, in1=FR[2],
                                                   op0=ALU.min, op1=ALU.subtract))
            cv.wait(dve, "flf")
            dve.wait_ge(const_loaded, 32)
            cv.did("fscan", dve.tensor_tensor_scan(FR[4], UNIT[0:8, :], FR[3], 0.0, ALU.mult, ALU.add))
            cv.wait(dve, "fscan")
            cv.did("fn8", dve.tensor_scalar(FR[4], FR[4], -8.0, None, ALU.mult))
            cp.wait(dve, "kvc")
            dve.tensor_copy(KC, PS[:, 1, 0:30])
            cv.did("kvc", dve.tensor_copy(VC, PS[0:15, 1, 32:160]))
            cp.wait(dve, "cols")
            dve.tensor_copy(GATEC, PS[:, 6, 0:48].rearrange("p (t n) -> p t n", t=TT))
            cv.did("cols", dve.tensor_copy(FCOL, PS[:, 6, 48:64].rearrange("p (t n) -> p t n", t=TT)))
            cv.wait(dve, "cols")
            cp.wait(dve, "fox")
            for h in range(8):
                row = ps_t(2, 4)[:, h, :]
                dve.scalar_tensor_tensor(out=CB[:, h, 0:P], in0=row[:, 0:P], scalar=FCOL[:, 0, h:h + 1],
                                         in1=cst("causal8"), op0=ALU.subtract, op1=ALU.add)
                dve.tensor_scalar(CB[:, h, P:T], row[:, 0:P], FCOL[:, 1, h:h + 1], None, ALU.subtract)
                last = dve.scalar_tensor_tensor(out=CB[:, h, T:384], in0=row[:, P:T], scalar=FCOL[:, 1, h:h + 1],
                                                in1=cst("causal8"), op0=ALU.subtract, op1=ALU.add)
            cv.did("cb", last)

        @block.tensor
        def _(pe):
            mmul = nc.tensor.matmul
            pe.wait_ge(cload, 80)
            cv.wait(pe, "bt")
            for v in range(2):
                for l in range(16):
                    last = mmul(PS[0:30, 0, v * T:(v + 1) * T], BT[:, v, l, :, :].rearrange("p g n -> p (g n)"),
                                W1[v][:, l, :], start=(l == 0), stop=(l == 15))
            cp.did("hid", last)

            def turn_values(t):
                for i, tile in enumerate(VTILES):
                    last = nc.tensor.transpose(fl(PS[:, 2:6, :])[:, i * P:(i + 1) * P],
                                               BIG[:, tile, t * P:(t + 1) * P], IDENT)
                cp.did(f"vn{t}", last)
            turn_values(0)
            ca.wait(pe, "gelu")
            for n in range(4):
                last = nc.tensor.transpose(PS[:, 1, 30 * n:30 * n + 30], HIDN[:, n * P:(n + 1) * P], IDENT[0:30, 0:30])
            cp.did("hid_T", last)
            ca.wait(pe, "hid_T")
            for ht in range(2):
                mmul(PS[:, 1, 0:30], W2K[:, ht, :], HID[:, 0, ht, :], start=(ht == 0), stop=(ht == 1))
            for g in range(2):
                for ht in range(2):
                    last = mmul(PS[0:15, 1, 32 + 64 * g:96 + 64 * g], HID[:, 1, ht, 15 * g:15 * g + 15], W2V[:, ht, :],
                                start=(ht == 0), stop=(ht == 1))
            cp.did("kvc", last)
            ca.wait(pe, "vn0")
            turn_values(1)
            cv.wait(pe, "fn8")
            ca.wait(pe, "gates")
            for t in range(TT):
                nc.tensor.transpose(PS[:, 6, 24 * t:24 * t + 24], GT[0:24, 0, t * P:(t + 1) * P], IDENT[0:24, 0:24])
                last = nc.tensor.transpose(PS[:, 6, 48 + 8 * t:56 + 8 * t], FR[4][:, t * P:(t + 1) * P], IDENT[0:8, 0:8])
            cp.did("cols", last)
            ca.wait(pe, "vn1")
            for h in range(8):
                last = mmul(ps_t(2, 4)[:, h, :], pick(h, 8), FR[4], start=True, stop=True)
            cp.did("fox", last)
    if stop == 6:
        return ctx

    PARTS = [(kind, h) for h in range(8) for kind in ("sel", "win", "cmp")]
    PARTS += [(kind, h) for kind in ("moba", "fox", "long") for h in range(8)]
    NPART = len(PARTS)
    FIRST = {"sel": True, "win": False, "cmp": False}
    LAST = {"sel": False, "win": False, "cmp": True}
    NE, NS, NPT = 4, 3, 3
    E2 = [T_[:, 384 * i:384 * i + 384] for i in range(NE)]
    PT2 = [T_[:, 1536 + 384 * i:1920 + 384 * i] for i in range(NPT)]
    STAT = T_[:, 2688:2688 + 3 * 2 * NPART].rearrange("p (s n q) -> p s n q", s=3, q=2)
    MINS, SUMS, RECS = [STAT[:, i] for i in range(3)]
    scored = sem("scored")
    lowest = sem("lowest")
    exped = sem("exped")
    recip = sem("reciprocals")
    gated = sem("reciprocals_gated")
    probs = sem("probs")
    probs_T = sem("probs_T")
    probs_out = sem("probs_out")
    valued = sem("valued")
    head_out = sem("head_pair_out")

    def query(kind, h):
        tile = {"moba": BQ, "fox": CQ, "long": DQ}.get(kind, AQ) + h // 2
        return BIG[64 * (h % 2):64 * (h % 2) + 64, tile, :]

    def key(kind, h):
        e = slice(64 * (h % 2), 64 * (h % 2) + 64)
        if kind in ("sel", "win"):
            return KDUP[e, ("sel", "win").index(kind), h // 4, :]
        if kind == "cmp":
            return KC[e, 15 * (h // 4):15 * (h // 4) + 15]
        return BIG[e, {"moba": BK, "fox": CK, "long": DK}[kind] + h // 2, :]

    def value(kind, h, t):
        if kind in ("sel", "win"):
            at = P * ("sel", "win").index(kind) + 64 * (h // 4)
        else:
            at = P * {"moba": 2, "fox": 6, "long": 10}[kind] + 64 * h
        return VNAT[:, t, at:at + 64]

    def spans(kind):
        return ((0, 7), (P, 15)) if kind == "cmp" else ((0, P), (P, T))

    def bias_of(kind, h, t):
        if kind == "fox":
            return CB[:, h, 0:P] if t == 0 else CB[:, h, P:384]
        row = G8[:, {"moba": 8, "long": 16}.get(kind, 0) + h, :]
        if kind == "cmp":
            first = 159 if t == 0 else 31
            n = spans(kind)[t][1]
            return row[:, first:first + 16 * (n - 1) + 1:16]
        return row[:, P:T] if t == 0 else row

    def o_index(kind, h):
        return {"moba": 4, "fox": 8, "long": 12}.get(kind, 0) + h // 2

    with nc.Block() as block:
        @block.sync
        def _(sp):
            load_rows(sp, C0, A["w_out_2"][0], 0, 2)

        @block.tensor
        def _(pe):
            mmul = nc.tensor.matmul

            def scores(i):
                kind, h = PARTS[i]
                if i >= NS:
                    pe.wait_ge(lowest, i - NS + 1)
                q, k = query(kind, h), key(kind, h)
                for t, (at, n) in enumerate(spans(kind)):
                    last = mmul(PS[:, i % NS, at:at + n], q[:, t * P:(t + 1) * P], k[:, 0:n], start=True, stop=True)
                last.then_inc(scored, 1)

            def turn_probs(i):
                kind, h = PARTS[i]
                pe.wait_ge(probs, i + 1)
                if i >= NPT:
                    pe.wait_ge(probs_out, i - NPT + 1)
                bank, e = PS[:, 3 + i % NPT, :], E2[i % NE]
                if kind == "cmp":
                    for t, (at, n) in enumerate(spans(kind)):
                        last = nc.tensor.transpose(bank[0:n, at:at + P], e[:, at:at + n], IDENT)
                else:
                    for b in range(3):
                        last = nc.tensor.transpose(bank[:, b * P:(b + 1) * P], e[:, b * P:(b + 1) * P], IDENT)
                last.then_inc(probs_T, 1)

            def values(i):
                kind, h = PARTS[i]
                pe.wait_ge(probs_out, i + 1)
                o, e = o_index(kind, h), 64 * (h % 2)
                first, final = FIRST.get(kind, True), LAST.get(kind, True)
                if first and h % 2 == 0 and o >= 2:
                    pe.wait_ge(head_out, o - 1)
                dst, pt = PS[e:e + 64, 6 + o % 2, 0:T], PT2[i % NPT]
                if kind == "cmp":
                    v = VC[:, 64 * (h // 4):64 * (h // 4) + 64]
                    mmul(dst[:, 0:P], v[0:7, :], pt[0:7, 0:P], start=False, stop=False)
                    last = mmul(dst[:, P:T], v, pt[0:15, P:T], start=False, stop=True)
                else:
                    mmul(dst, value(kind, h, 0), pt[:, 0:T], start=first, stop=False)
                    last = mmul(dst[:, P:T], value(kind, h, 1), pt[:, T:384], start=False, stop=final)
                last.then_inc(valued, 1)

            for i in range(NPART + 3):
                if i < NPART:
                    scores(i)
                if 0 <= i - 2 < NPART:
                    turn_probs(i - 2)
                if 0 <= i - 3 < NPART:
                    values(i - 3)

        @block.vector
        def _(dve):
            def lowest_of(i):
                kind, h = PARTS[i]
                dve.wait_ge(scored, i + 1)
                if i >= NE:
                    dve.wait_ge(probs_T, i - NE + 1)
                for t, (at, n) in enumerate(spans(kind)):
                    last = dve.tensor_tensor_reduce(E2[i % NE][:, at:at + n], PS[:, i % NS, at:at + n],
                                                    bias_of(kind, h, t), -0.125, 3e38, ALU.add, ALU.min,
                                                    MINS[:, i, t:t + 1])
                last.then_inc(lowest, 1)

            def weights(i):
                kind, h = PARTS[i]
                dve.wait_ge(exped, i + 1)
                dve.reciprocal(RECS[:, i, :], SUMS[:, i, :]).then_inc(recip, 1)
                dve.wait_ge(recip, i + 1)
                if i < 24:
                    gate = GATEC[:, :, 8 * ("cmp", "sel", "win").index(kind) + h]
                    dve.tensor_tensor(RECS[:, i, :], RECS[:, i, :], gate, ALU.mult).then_inc(gated, 1)
                    dve.wait_ge(gated, i + 1 + i // 3)
                    if kind == "cmp":
                        dve.tensor_tensor(RECS[:, i, 0:1], RECS[:, i, 0:1], cst("from31"), ALU.mult).then_inc(gated, 1)
                        dve.wait_ge(gated, i + 2 + i // 3)
                for t, (at, n) in enumerate(spans(kind)):
                    e = E2[i % NE][:, at:at + n]
                    last = dve.tensor_scalar(e, e, RECS[:, i, t:t + 1], None, ALU.mult)
                last.then_inc(probs, 1)

            for i in range(NPART + 1):
                if i < NPART:
                    lowest_of(i)
                if i >= 1:
                    weights(i - 1)

        @block.scalar
        def _(act):
            def exponentials(i):
                kind, h = PARTS[i]
                act.wait_ge(lowest, i + 1)
                for t, (at, n) in enumerate(spans(kind)):
                    e = E2[i % NE][:, at:at + n]
                    last = act.activation(e, e, ACT.Exp, bias=MINS[:, i, t:t + 1], scale=-1.0,
                                          accum_out=SUMS[:, i, t:t + 1])
                last.then_inc(exped, 1)

            def probs_to_sbuf(i):
                kind, h = PARTS[i]
                act.wait_ge(probs_T, i + 1)
                if i >= NPT:
                    act.wait_ge(valued, i - NPT + 1)
                bank = PS[:, 3 + i % NPT, :]
                if kind == "cmp":
                    act.activation(PT2[i % NPT][0:7, 0:P], bank[0:7, 0:P], ACT.Copy)
                    last = act.activation(PT2[i % NPT][0:15, P:T], bank[0:15, P:T], ACT.Copy)
                else:
                    last = act.activation(PT2[i % NPT], bank[:, 0:384], ACT.Copy)
                last.then_inc(probs_out, 1)

            def heads_out(i):
                kind, h = PARTS[i]
                if h % 2 == 1 and LAST.get(kind, True):
                    o = o_index(kind, h)
                    act.wait_ge(valued, i + 1)
                    act.activation(NT[:, o, :], PS[:, 6 + o % 2, 0:T], ACT.Copy).then_inc(head_out, 1)

            for i in range(NPART + 4):
                if i < NPART:
                    exponentials(i)
                if 0 <= i - 2 < NPART:
                    probs_to_sbuf(i - 2)
                if 0 <= i - 4 < NPART:
                    heads_out(i - 4)
    if stop == 7:
        return ctx

    C1 = C0 + N_OUT
    N_UP = F2 // 256
    C2 = C1 + 2 * N_UP
    C3 = C2 + F2 // P
    Q2 = (NI + NI2) // 2
    GAIN2 = fl(NT[:, 0:8, :])
    squared = sem("hidden_squared")
    scaled = sem("post_scaled")
    out_done = sem("out_done")
    gain2_loaded = sem("gain2_loaded")
    SQUARES = fl(BIG[:, 52:60, :])

    def product(t):
        return PS[:, 4 * t:4 * t + 4, :].rearrange("p b n -> p (b n)")

    def post_square(act, q, n, used):
        for t in range(TT):
            if t == 0:
                act.wait_ge(tile_done, n + 1)
            else:
                act.wait_ge(item_used, used)
                act.wait_ge(sq_done, 2 * q + 1)
            act.activation(SQUARES, product(t), ACT.Square, accum_out=ST[:, t:t + 1]).then_inc(sq_done, 1)
        act.wait_ge(mean_done, q + 1)
        act.activation(ST[:, 4:6], ST[:, 2:4], ACT.Sqrt).then_inc(sd_done, 1)

    def post_norm(dve, q, n, gain):
        for t in range(TT):
            dve.wait_ge(sq_done, 2 * q + t + 1)
            dve.tensor_tensor(TMP[:, t, :], product(t), gain, ALU.mult).then_inc(scaled, 1)
            if t == 0:
                continue
            norm_dve(dve, q, None)
        for t in range(TT):
            dve.wait_ge(scaled, 2 * n + t + 1)
            dve.scalar_tensor_tensor(out=X[:, t, :], in0=TMP[:, t, :], scalar=ST[:, 6 + t:7 + t], in1=X[:, t, :],
                                     op0=ALU.mult, op1=ALU.add).then_inc(res_done, 1)

    with nc.Block() as block:
        @block.sync
        def _(sp):
            sp.dma_start(GAIN, row_gain(A["g_mix_post_2"][0])).then_inc(gain_loaded, 16)
            load_rows(sp, C0, A["w_out_2"][0], 2)
            load_cols(sp, C1, A["w_up_2"][0], 0, N_UP)
            load_rows(sp, C2, A["w_down_2"][0])
            for t in range(TT):
                sp.wait_ge(res_done, 8 + t + 1)
                sp.dma_start(out[0].rearrange("(t p) d -> p t d", p=P)[:, t, :], X[:, t, :]).then_inc(out_done, 16)
            sp.wait_ge(out_done, 32)

        @block.scalar
        def _(act):
            split_hi(act, C0)
            split_hi(act, C0 + 1)
            act_rows(act, C0, L2, N_OUT, NT, C3)
            post_square(act, 4, 2, C1)
            norm_act(act, 5, lambda e, t: e.wait_ge(res_done, 6 + t + 1))
            norm_act_hi(act, 5)
            act.wait_ge(norm_out, 32)

            def up(j, r):
                split_hi(act, C1 + j + 2, r)
                if j % 2 == 1:
                    act.wait_ge(item_used, C1 + j + 1 + 4 * r)
                    act.wait_ge(squared, H0 + j // 2 - 1 + 2 * r)
                    act.activation(two(ACTED[:, j // 2 % 2, :]), PS[:, j // 2 % 2 * 2:j // 2 % 2 * 2 + 2, 0:T], ACT.Relu)\
                        .then_inc(pair_out, 1)
            steps(act, 2 * N_UP, up)
            act.wait_ge(squared, H0 + N_UP)
            act.dma_start(GAIN2, row_gain(A["g_mlp_post_2"][0])).then_inc(gain2_loaded, 16)
            act_rows(act, C2, L3, F2 // P, BIG, C3)
            post_square(act, 6, 3, C3)

        @block.vector
        def _(dve):
            for _ in range(H0):
                dve.engine_nop().then_inc(squared, 1)
            split_lo(dve, C0)
            split_lo(dve, C0 + 1)
            dve_rows(dve, C0, L2, N_OUT, NT, C3)
            dve.wait_ge(gain_loaded, 32)
            post_norm(dve, 4, 0, GAIN)
            split_lo(dve, C1 + 1)
            dve.wait_ge(res_done, 8)
            norm_dve(dve, 5, "g_mlp_pre_2")

            def square(j, r):
                split_lo(dve, C1 + j + 2, r)
                if j % 2 == 1:
                    dve.wait_ge(pair_out, Q2 + j // 2 + 1 + 2 * r)
                    a = two(ACTED[:, j // 2 % 2, :])
                    dve.tensor_tensor(BIG[:, bass.ds(j - 1 + 4 * r, 2), :], a, a, ALU.mult).then_inc(squared, 1)
            steps(dve, 2 * N_UP, square)
            dve_rows(dve, C2, L3, F2 // P, BIG, C3)
            dve.wait_ge(gain2_loaded, 16)
            post_norm(dve, 6, 1, GAIN2)

        @block.tensor
        def _(pe):
            assert Q2 % 2 == 0
            pe_rows(pe, C0, L2, N_OUT)
            norm_pe(pe, 5)
            pe_cols(pe, C1, Q2, N_UP, 5)
            pe.wait_ge(squared, H0 + N_UP)
            pe_rows(pe, C2, L3, F2 // P)
    return ctx


NAMES = ("x", "attn_norm", "w_in", "gdn_conv", "gdn_a_log", "gdn_dt_bias", "gdn_norm", "mlstm_conv", "mlstm_b_i",
         "mlstm_b_f", "mlstm_norm", "rglru_conv", "rglru_conv_b", "rglru_w_a", "rglru_b_a", "rglru_w_x", "rglru_b_x",
         "rglru_lambda", "rwkv_mu", "rwkv_w0", "rwkv_w2", "rwkv_a0", "rwkv_a2", "rwkv_g2", "rwkv_k_k", "rwkv_k_a",
         "rwkv_r_k", "rwkv_ln_w", "rwkv_ln_b", "w_out", "ffn_norm", "ffn_w_gate", "ffn_w_up", "ffn_w_down",
         "final_norm", "w_in_2", "w_out_2", "g_mix_pre_2", "g_mix_post_2", "g_mlp_pre_2", "g_mlp_post_2", "w_up_2",
         "w_down_2", "cmp_pe_2", "phik_w1_2", "phik_w2_2", "phiv_w1_2", "phiv_w2_2", "fox_bias_2", "rel_bias_2")


def kernel(**inputs):
    import concourse.bacc as bacc
    from concourse.bass_utils import run_bass_kernel_spmd

    nc = bacc.Bacc("TRN2", target_bir_lowering=False, num_devices=1)
    arrays = {name: np.ascontiguousarray(inputs[name]) for name in NAMES}
    arrays["const"] = CONST
    arrays["const_first"] = CONST_FIRST
    handles = {}
    for name, a in arrays.items():
        handles[name] = nc.dram_tensor(f"in_{name}", a.shape, mybir.dt.from_np(a.dtype), kind="ExternalInput").ap()
    out = nc.dram_tensor("out", (1, T, D), F32, kind="ExternalOutput").ap()
    build(nc, handles, out)
    r = run_bass_kernel_spmd(nc, [{f"in_{k}": v for k, v in arrays.items()}], core_ids=[0])
    return r.results[0]["out"]
```
